# Optimizing a Trainium2 kernel written in Bass

```python
import functools
import jax, jax.numpy as jnp
from jax import lax
import numpy as np

D_MODEL = 1024
BATCH = 1
SEQ = 512
DEPTH = 2
DEC_BATCH = 8
DEC_SEQ = 1
PAST_LEN = 256
PAGE_SIZE = 128

N_MIXERS = 2
N_RET_LAYERS = (DEPTH + N_MIXERS - 1) // N_MIXERS
N_DSA_LAYERS = DEPTH // N_MIXERS
ALPHA = (2.0 * DEPTH) ** 0.25
BETA = (8.0 * DEPTH) ** -0.25
LN_EPS = 1e-5

RET_HEADS = 4
RET_DK = 256
RET_DV = 512
RET_QK = RET_HEADS * RET_DK
RET_V = RET_HEADS * RET_DV
RET_IN = 2 * RET_QK + 2 * RET_V
RET_CHUNK = 128
RET_ANGLE_BASE = 10000.0
GN_EPS = 1e-6

DSA_HEADS = 8
DSA_KV_HEADS = 2
DSA_HEAD_DIM = 128
DSA_GROUP = DSA_HEADS // DSA_KV_HEADS
DSA_Q = DSA_HEADS * DSA_HEAD_DIM
DSA_KV = DSA_KV_HEADS * DSA_HEAD_DIM
IDX_HEADS = 16
IDX_DIM = 64
DSA_TOPK = 256
Q_BLOCK = 128
ROPE_THETA = 500000.0
ROT_DIM = DSA_HEAD_DIM // 4
IDX_ROT_DIM = IDX_DIM // 4
DSA_SPLITS = [DSA_Q, DSA_Q + DSA_KV, DSA_Q + 2 * DSA_KV,
              DSA_Q + 2 * DSA_KV + IDX_HEADS * IDX_DIM,
              DSA_Q + 2 * DSA_KV + IDX_HEADS * IDX_DIM + IDX_DIM]
DSA_IN = DSA_Q + 2 * DSA_KV + IDX_HEADS * IDX_DIM + IDX_DIM + IDX_HEADS

N_EXPERTS = 16
N_GROUPS = 4
EXPERTS_PER_GROUP = N_EXPERTS // N_GROUPS
TOPK_EXPERTS = 2
D_EXPERT = 512

kernel_name = "retention_dsa_hybrid_step"

F32 = jnp.float32

def layer_norm(x, g, b):
    xf = x.astype(F32)
    mu = jnp.mean(xf, -1, keepdims=True)
    var = jnp.mean(jnp.square(xf - mu), -1, keepdims=True)
    return ((xf - mu) * lax.rsqrt(var + LN_EPS) * g.astype(F32) + b.astype(F32)).astype(x.dtype)

def rot_tables(pos, inv_freq):
    ang = pos.astype(F32)[:, None] * inv_freq[None, :]
    return jnp.cos(ang), jnp.sin(ang)

def rope_inv_freq(rot_dim):
    return 1.0 / (ROPE_THETA ** (jnp.arange(0, rot_dim, 2, dtype=F32) / rot_dim))

def retnet_inv_freq():
    return jnp.power(RET_ANGLE_BASE, -jnp.linspace(0.0, 1.0, RET_DK // 2, dtype=F32))

def rotate(x, cos, sin):
    half = cos.shape[-1]
    x1 = x[..., :half].astype(F32)
    x2 = x[..., half:2 * half].astype(F32)
    return jnp.concatenate([x1 * cos - x2 * sin, x1 * sin + x2 * cos,
                            x[..., 2 * half:].astype(F32)], -1).astype(x.dtype)

def retention_scan(q, k, v, s0):
    B, T, H, _ = q.shape
    C = min(RET_CHUNK, T)
    n = T // C
    lg = jnp.log(1.0 - jnp.power(2.0, -5.0 - jnp.arange(H, dtype=F32)))
    idx = jnp.arange(C, dtype=F32)
    diff = idx[:, None] - idx[None, :]
    decay = jnp.where(diff >= 0, jnp.exp(lg[:, None, None] * jnp.maximum(diff, 0.0)), 0.0)
    q_dec = jnp.exp(lg[None, :] * (idx[:, None] + 1.0))
    k_dec = jnp.exp(lg[None, :] * (C - 1.0 - idx)[:, None])
    chunk_dec = jnp.exp(lg * C)

    def step(s, qkv):
        qc, kc, vc = (a.astype(F32) for a in qkv)
        att = jnp.einsum('bnhd,bmhd->bhnm', qc, kc) * decay
        o = (jnp.einsum('bhnm,bmhv->bnhv', att, vc)
             + jnp.einsum('bnhd,bhdv->bnhv', qc, s) * q_dec[None, :, :, None])
        s = (chunk_dec[None, :, None, None] * s
             + jnp.einsum('bmhd,bmhv->bhdv', kc * k_dec[None, :, :, None], vc))
        return s, o

    to_chunks = lambda a: a.reshape(B, n, C, *a.shape[2:]).swapaxes(0, 1)
    s, o = lax.scan(step, s0.astype(F32), (to_chunks(q), to_chunks(k), to_chunks(v)))
    return o.swapaxes(0, 1).reshape(B, T, H, RET_DV), s

def retention_mixer(h, s0, w_in, gn_g, w_out, cos, sin):
    B, T, _ = h.shape
    q, k, v, g = jnp.split(h @ w_in, [RET_QK, 2 * RET_QK, 2 * RET_QK + RET_V], axis=-1)
    q = rotate(q.reshape(B, T, RET_HEADS, RET_DK), cos[:, None], sin[:, None])
    k = rotate(k.reshape(B, T, RET_HEADS, RET_DK), cos[:, None], sin[:, None]) * (RET_DK ** -0.5)
    v = v.reshape(B, T, RET_HEADS, RET_DV)
    o, s = retention_scan(q, k, v, s0)
    mu = jnp.mean(o, -1, keepdims=True)
    var = jnp.mean(jnp.square(o - mu), -1, keepdims=True)
    on = (o - mu) * lax.rsqrt(var + GN_EPS) * gn_g.astype(F32).reshape(RET_HEADS, RET_DV)
    y = (on.reshape(B, T, RET_V).astype(h.dtype) * jax.nn.silu(g)) @ w_out
    return y, s

def dsa_project(h, w_in, pos):
    B, T, _ = h.shape
    q, k, v, qi, ki, wi = jnp.split(h @ w_in, DSA_SPLITS, axis=-1)
    cos, sin = rot_tables(pos, rope_inv_freq(ROT_DIM))
    cos_i, sin_i = rot_tables(pos, rope_inv_freq(IDX_ROT_DIM))
    q = rotate(q.reshape(B, T, DSA_HEADS, DSA_HEAD_DIM), cos[:, None], sin[:, None])
    k = rotate(k.reshape(B, T, DSA_KV_HEADS, DSA_HEAD_DIM), cos[:, None], sin[:, None])
    v = v.reshape(B, T, DSA_KV_HEADS, DSA_HEAD_DIM)
    qi = rotate(qi.reshape(B, T, IDX_HEADS, IDX_DIM), cos_i[:, None], sin_i[:, None])
    ki = rotate(ki, cos_i, sin_i)
    return q, k, v, qi, ki, wi

def sparse_attend(q, qi, wi, q_pos, k_all, v_all, ki_all, topk):
    B, Q = q.shape[0], q.shape[1]
    L = k_all.shape[1]
    dots = jnp.einsum('bqhd,bld->bqhl', qi.astype(F32), ki_all.astype(F32)) * (IDX_DIM ** -0.5)
    score = jnp.einsum('bqh,bqhl->bql', wi.astype(F32) * (IDX_HEADS ** -0.5), jax.nn.relu(dots))
    allowed = jnp.arange(L, dtype=jnp.int32)[None, :] <= q_pos[:, None]
    score = jnp.where(allowed[None], score, -jnp.inf)
    _, idx = lax.top_k(score, topk)
    valid = idx <= q_pos[None, :, None]
    gather = jax.vmap(lambda a, i: a[i])
    k_sel = gather(k_all, idx)
    v_sel = gather(v_all, idx)
    qg = q.reshape(B, Q, DSA_KV_HEADS, DSA_GROUP, DSA_HEAD_DIM)
    logits = jnp.einsum('bqngd,bqknd->bqngk', qg, k_sel).astype(F32) * (DSA_HEAD_DIM ** -0.5)
    logits = jnp.where(valid[:, :, None, None, :], logits, -jnp.inf)
    p = jax.nn.softmax(logits, axis=-1).astype(v_sel.dtype)
    o = jnp.einsum('bqngk,bqknd->bqngd', p, v_sel)
    return o.reshape(B, Q, DSA_Q)

def dsa_prompt(h, w_in, w_out, pos):
    B, T, _ = h.shape
    q, k, v, qi, ki, wi = dsa_project(h, w_in, pos)
    topk = min(DSA_TOPK, T // 4)
    qb = min(Q_BLOCK, T)
    nb = T // qb
    blk = lambda a: a.reshape(B, nb, qb, *a.shape[2:]).swapaxes(0, 1)
    o = lax.map(lambda xs: sparse_attend(xs[0], xs[1], xs[2], xs[3], k, v, ki, topk),
                (blk(q), blk(qi), blk(wi), pos.reshape(nb, qb)))
    o = o.swapaxes(0, 1).reshape(B, T, DSA_Q)
    return o @ w_out, (k, v, ki)

def dsa_sample(h, cache_k, cache_v, cache_kidx, page_table, w_in, w_out, pos):
    DB, T, _ = h.shape
    q, k, v, qi, ki, wi = dsa_project(h, w_in, pos)
    past = lambda c: c[page_table].reshape(DB, -1, *c.shape[2:])
    k_all = jnp.concatenate([past(cache_k), k.astype(cache_k.dtype)], axis=1)
    v_all = jnp.concatenate([past(cache_v), v.astype(cache_v.dtype)], axis=1)
    ki_all = jnp.concatenate([past(cache_kidx), ki.astype(cache_kidx.dtype)], axis=1)
    topk = min(DSA_TOPK, k_all.shape[1] // 4)
    o = sparse_attend(q, qi, wi, pos, k_all, v_all, ki_all, topk)
    return o @ w_out, (k, v, ki)

def grouped_moe(h, w_router, b_router, w_gate, w_up, w_down):
    logits = h.astype(F32) @ w_router.astype(F32) + b_router.astype(F32)
    probs = jax.nn.softmax(logits, axis=-1)
    grp = probs.reshape(*probs.shape[:-1], N_GROUPS, EXPERTS_PER_GROUP)
    grp_score = lax.top_k(grp, TOPK_EXPERTS)[0].sum(-1)
    g_sel = jnp.argmax(grp_score, axis=-1)
    in_grp = (jnp.arange(N_EXPERTS) // EXPERTS_PER_GROUP) == g_sel[..., None]
    vals, idx = lax.top_k(jnp.where(in_grp, probs, -jnp.inf), TOPK_EXPERTS)
    wts = vals / jnp.sum(vals, -1, keepdims=True)
    gates = jnp.sum(jax.nn.one_hot(idx, N_EXPERTS, dtype=F32) * wts[..., None], axis=-2).astype(h.dtype)
    y = jnp.zeros_like(h)
    for e in range(N_EXPERTS):
        a = jax.nn.silu(h @ w_gate[e]) * (h @ w_up[e])
        y = y + gates[..., e:e + 1] * (a @ w_down[e])
    return y

def block(x, c, l, mixer, w_mod, b_mod, ln1_g, ln1_b, ln2_g, ln2_b,
          w_router, b_router, w_gate, w_up, w_down):
    mod = (jax.nn.silu(c) @ w_mod[l] + b_mod[l])[:, None, :]
    sh1, sc1, g1, sh2, sc2, g2 = jnp.split(mod, 6, axis=-1)
    y, st = mixer(x * (1 + sc1) + sh1)
    x = layer_norm(ALPHA * x + g1 * y, ln1_g[l], ln1_b[l])
    f = grouped_moe(x * (1 + sc2) + sh2, w_router, b_router, w_gate[l], w_up[l], w_down[l])
    x = layer_norm(ALPHA * x + g2 * f, ln2_g[l], ln2_b[l])
    return x, st

def run_trunk(x, c, mix_ret, mix_dsa, block_params):
    states_ret, states_dsa = [], []
    for l in range(DEPTH):
        j = l // N_MIXERS
        if l % N_MIXERS == 0:
            x, st = block(x, c, l, functools.partial(mix_ret, j=j), *block_params)
            states_ret.append(st)
        else:
            x, st = block(x, c, l, functools.partial(mix_dsa, j=j), *block_params)
            states_dsa.append(st)
    return x, states_ret, states_dsa

def setup_inputs(seed: int = 0) -> dict:
    key = jax.random.key(seed)
    ks = jax.random.split(key, 32)
    nrm = lambda k, shape, s: jax.random.normal(k, shape, F32) * s
    n_pages = PAST_LEN // PAGE_SIZE
    n_used = DEC_BATCH * n_pages
    n_pool = n_used + max(1, n_used // 4)
    page_table = jax.random.permutation(ks[0], n_pool)[:n_used].reshape(DEC_BATCH, n_pages).astype(jnp.int32)
    ret_cols = jnp.concatenate([jnp.ones((2 * RET_QK,), F32), jnp.full((RET_V,), BETA, F32),
                                jnp.ones((RET_V,), F32)])
    dsa_cols = jnp.concatenate([jnp.ones((DSA_Q + DSA_KV,), F32), jnp.full((DSA_KV,), BETA, F32),
                                jnp.ones((DSA_IN - DSA_Q - 2 * DSA_KV,), F32)])
    return {
        "x_prompt": nrm(ks[1], (BATCH, SEQ, D_MODEL), 1.0),
        "x_sample": nrm(ks[2], (DEC_BATCH, DEC_SEQ, D_MODEL), 1.0),
        "state_ret": nrm(ks[3], (N_RET_LAYERS, DEC_BATCH, RET_HEADS, RET_DK, RET_DV), 0.5),
        "cache_k": nrm(ks[4], (N_DSA_LAYERS, n_pool, PAGE_SIZE, DSA_KV_HEADS, DSA_HEAD_DIM), 1.0),
        "cache_v": nrm(ks[5], (N_DSA_LAYERS, n_pool, PAGE_SIZE, DSA_KV_HEADS, DSA_HEAD_DIM), BETA),
        "cache_kidx": nrm(ks[6], (N_DSA_LAYERS, n_pool, PAGE_SIZE, IDX_DIM), 1.0),
        "page_table": page_table,
        "c_prompt": nrm(ks[7], (BATCH, D_MODEL), 1.0),
        "c_sample": nrm(ks[8], (DEC_BATCH, D_MODEL), 1.0),
        "w_mod": nrm(ks[9], (DEPTH, D_MODEL, 6 * D_MODEL), D_MODEL ** -0.5),
        "b_mod": nrm(ks[10], (DEPTH, 6 * D_MODEL), 0.02),
        "ln1_g": 1.0 + nrm(ks[11], (DEPTH, D_MODEL), 0.02),
        "ln1_b": nrm(ks[12], (DEPTH, D_MODEL), 0.02),
        "ln2_g": 1.0 + nrm(ks[13], (DEPTH, D_MODEL), 0.02),
        "ln2_b": nrm(ks[14], (DEPTH, D_MODEL), 0.02),
        "w_in_ret": nrm(ks[15], (N_RET_LAYERS, D_MODEL, RET_IN), D_MODEL ** -0.5) * ret_cols,
        "gn_ret_g": 1.0 + nrm(ks[16], (N_RET_LAYERS, RET_V), 0.02),
        "w_out_ret": nrm(ks[17], (N_RET_LAYERS, RET_V, D_MODEL), BETA * RET_V ** -0.5),
        "w_in_dsa": nrm(ks[18], (N_DSA_LAYERS, D_MODEL, DSA_IN), D_MODEL ** -0.5) * dsa_cols,
        "w_out_dsa": nrm(ks[19], (N_DSA_LAYERS, DSA_Q, D_MODEL), BETA * DSA_Q ** -0.5),
        "w_router": nrm(ks[20], (D_MODEL, N_EXPERTS), D_MODEL ** -0.5),
        "b_router": nrm(ks[21], (N_EXPERTS,), 0.01),
        "w_gate": nrm(ks[22], (DEPTH, N_EXPERTS, D_MODEL, D_EXPERT), D_MODEL ** -0.5),
        "w_up": nrm(ks[23], (DEPTH, N_EXPERTS, D_MODEL, D_EXPERT), BETA * D_MODEL ** -0.5),
        "w_down": nrm(ks[24], (DEPTH, N_EXPERTS, D_EXPERT, D_MODEL), BETA * D_EXPERT ** -0.5),
    }

def reference(x_prompt, x_sample, state_ret, cache_k, cache_v, cache_kidx, page_table,
              c_prompt, c_sample, w_mod, b_mod, ln1_g, ln1_b, ln2_g, ln2_b,
              w_in_ret, gn_ret_g, w_out_ret, w_in_dsa, w_out_dsa,
              w_router, b_router, w_gate, w_up, w_down):
    block_params = (w_mod, b_mod, ln1_g, ln1_b, ln2_g, ln2_b, w_router, b_router, w_gate, w_up, w_down)
    pos_p = jnp.arange(SEQ, dtype=jnp.int32)
    pos_s = PAST_LEN + jnp.arange(x_sample.shape[1], dtype=jnp.int32)
    cos_rp, sin_rp = rot_tables(pos_p, retnet_inv_freq())
    cos_rs, sin_rs = rot_tables(pos_s, retnet_inv_freq())

    ret_p = lambda h, j: retention_mixer(
        h, jnp.zeros((h.shape[0], RET_HEADS, RET_DK, RET_DV), F32),
        w_in_ret[j], gn_ret_g[j], w_out_ret[j], cos_rp, sin_rp)
    dsa_p = lambda h, j: dsa_prompt(h, w_in_dsa[j], w_out_dsa[j], pos_p)
    y_prompt, sr_p, sd_p = run_trunk(x_prompt, c_prompt, ret_p, dsa_p, block_params)

    ret_s = lambda h, j: retention_mixer(
        h, state_ret[j], w_in_ret[j], gn_ret_g[j], w_out_ret[j], cos_rs, sin_rs)
    dsa_s = lambda h, j: dsa_sample(h, cache_k[j], cache_v[j], cache_kidx[j], page_table,
                                    w_in_dsa[j], w_out_dsa[j], pos_s)
    y_sample, sr_s, sd_s = run_trunk(x_sample, c_sample, ret_s, dsa_s, block_params)

    ret_prompt = jnp.stack(sr_p)
    ret_sample = jnp.stack(sr_s)
    k_prompt = jnp.stack([s[0] for s in sd_p])
    v_prompt = jnp.stack([s[1] for s in sd_p])
    kidx_prompt = jnp.stack([s[2] for s in sd_p])
    k_sample = jnp.stack([s[0] for s in sd_s])
    v_sample = jnp.stack([s[1] for s in sd_s])
    kidx_sample = jnp.stack([s[2] for s in sd_s])
    return (y_prompt, y_sample, ret_prompt, ret_sample, k_prompt, v_prompt, kidx_prompt,
            k_sample, v_sample, kidx_sample)


_drawn_inputs = setup_inputs


def setup_inputs(seed=0):
    import zlib

    import numpy as np

    out = dict(_drawn_inputs(seed))
    spreads = {}
    factors = {'gn_ret_g': 8.0}
    for name, (base, spread) in spreads.items():
        noise = np.random.default_rng([zlib.crc32(name.encode()), seed]).standard_normal(out[name].shape)
        drawn = base * np.exp(spread * noise) if base else spread * noise
        out[name] = __import__('jax').numpy.asarray(drawn.astype(out[name].dtype))
    for name, factor in factors.items():
        out[name] = (out[name] * factor).astype(out[name].dtype)
    return out
```

```python
import math
from contextlib import ExitStack

import numpy as np

import concourse.bass as bass
from concourse import mybir

F32 = mybir.dt.float32
BF16 = mybir.dt.bfloat16
I32 = mybir.dt.int32
ALU = mybir.AluOpType
ACT = mybir.ActivationFunctionType
AX = mybir.AxisListType

P = 128
D = 1024
KD = D // P
SEQ, DEC = 512, 8
NT = SEQ // P
TOK = SEQ + DEC
TILES = NT + 1
DEPTH = 2
ALPHA = (2.0 * DEPTH) ** 0.25
LN_EPS, GN_EPS = 1e-5, 1e-6
NB = 512

RH, RDK, RDV = 4, 256, 512
CH = 128
GAMMA = [1.0 - 2.0 ** (-5.0 - h) for h in range(RH)]

QH, KVH, HD = 8, 2, 128
GRP = QH // KVH
IH, ID = 16, 64
DSA_IN = QH * HD + 2 * KVH * HD + IH * ID + ID + IH
TOPK_P = min(256, SEQ // 4)
PAST, PAGE = 256, 128
NPG = PAST // PAGE
TOPK_S = min(256, (PAST + 1) // 4)
LS = PAST + 1
ROT, IROT = HD // 4, ID // 4
NEG = -1.0e30
GONE = -3.0e38

NE, NG, EPG = 16, 4, 4
FE = 512
MAXB = -(-TOK // P)
ITEMS = 24
assert ITEMS >= NE + (2 * TOK) // P and ITEMS % 2 == 0

N_CONST = 5

_cols = {}
_at = 0
for _n, _w in (("ident", P), ("tri", P), ("cum", P), ("ones", P), ("cbias", P), ("qs", TILES * RH),
               ("ks", TILES * RH), ("item", ITEMS), ("blk", MAXB), ("pair", ITEMS // 2), ("w4", NG),
               ("w16", NE), ("valid", TILES), ("dcos", TILES * ROT // 2), ("dsin", TILES * ROT // 2),
               ("icos", TILES * IROT // 2), ("isin", TILES * IROT // 2), ("bexp", DEC * GRP),
               ("bsel", DEC), ("lneps", 1), ("gneps", 1)):
    _cols[_n] = (_at, _w)
    _at += _w
CST_W = _at


def constants():
    f = np.float32
    cst = np.zeros((P, CST_W), f)

    def put(name, a):
        o, w = _cols[name]
        cst[:a.shape[0], o:o + w] = a.reshape(a.shape[0], w)

    i = np.arange(P)
    put("ident", np.eye(P, dtype=f))
    put("tri", (i[None, :] >= i[:, None]).astype(f))
    put("cum", (i[:, None] < i[None, :]).astype(f))
    put("ones", np.ones((P, P), f))
    put("cbias", np.where(i[None, :] <= i[:, None], 0.0, NEG).astype(f))
    lg = np.log(f(1.0) - np.power(f(2.0), f(-5.0) - np.arange(RH, dtype=f))).astype(f)
    qs = np.ones((P, TILES, RH), f)
    ks = np.full((P, TILES, RH), RDK ** -0.5, f)
    qs[:, :NT] = np.exp(lg[None, :] * (i[:, None] + 1.0).astype(f))[:, None]
    ks[:, :NT] = (np.exp(lg[None, :] * (CH - 1.0 - i)[:, None].astype(f)) * f(RDK ** -0.5))[:, None]
    put("qs", qs)
    put("ks", ks)
    row = lambda v: np.tile(np.asarray(v, f)[None, :], (P, 1))
    put("item", row(np.arange(ITEMS)))
    put("blk", row(np.arange(MAXB) * P))
    put("pair", row(2 * np.arange(ITEMS // 2)))
    put("w4", row(NG - np.arange(NG)))
    put("w16", row(NE - np.arange(NE)))
    valid = np.ones((P, TILES), f)
    valid[DEC:, NT] = 0
    put("valid", valid)
    pos = np.zeros((P, TILES), f)
    pos[:, :NT] = (np.arange(NT) * P)[None, :] + i[:, None]
    pos[:, NT] = PAST

    def table(inv):
        ang = (pos[:, :, None] * inv.astype(f)[None, None, :]).astype(f)
        return np.cos(ang).astype(f), np.sin(ang).astype(f)

    theta = f(500000.0)
    for c, s, rot in (("dcos", "dsin", ROT), ("icos", "isin", IROT)):
        co, si = table(f(1.0) / (theta ** (np.arange(0, rot, 2, dtype=f) / f(rot))))
        put(c, co)
        put(s, si)
    bexp = np.zeros((DEC, DEC * GRP), f)
    for b in range(DEC):
        bexp[b, b * GRP:(b + 1) * GRP] = 1
    put("bexp", bexp)
    bsel = np.zeros((DEC * GRP, DEC), f)
    bsel[np.arange(DEC * GRP), np.arange(DEC * GRP) // GRP] = 1
    put("bsel", bsel)
    put("lneps", np.full((P, 1), LN_EPS, f))
    put("gneps", np.full((P, 1), GN_EPS, f))
    inv = np.power(f(10000.0), -np.linspace(0.0, 1.0, RDK // 2, dtype=f)).astype(f)
    rc, rs = table(inv)
    rot = np.stack([rc, rs], 1)
    tok = np.zeros((P, TILES), np.int32)
    tok[:, :] = (np.arange(TILES) * P)[None, :] + i[:, None]
    return cst, np.ascontiguousarray(rot), tok


def rows(t):
    return P if t < NT else DEC


def cols(t):
    return slice(t * P, t * P + rows(t))


def trunk(nc, A, O):
    ctx = ExitStack()
    with ctx:
        sems = {}

        def S(name):
            if name not in sems:
                sems[name] = ctx.enter_context(nc.semaphore(name))
            return sems[name]

        def sb(name, shape, dt=F32):
            return ctx.enter_context(nc.sbuf_tensor(name, shape, dt))

        def dram(name, shape, dt=F32):
            return nc.dram_tensor(name, shape, dt, kind="Internal").ap()

        bank = [ctx.enter_context(nc.psum_tensor(f"bank{i}", [P, NB], F32)) for i in range(8)]

        mod_d = dram("mod_d", (DEPTH, DEC + 1, 6 * D))
        h_d = dram("h_d", (TOK, D))
        slot_d = dram("slot_d", (ITEMS * P, 1), I32)
        y_d = dram("y_d", (ITEMS * P, D))

        X = sb("X", [P, TILES, D])
        HT = sb("HT", [P, KD, TOK])
        RING = sb("RING", [P, 3, KD * NB])
        MWORDS = 21504
        M = sb("M", [P, MWORDS])
        BC = sb("BC", [P, 3, D])
        SC = sb("SC", [DEC, 2, D])
        cst = sb("cst", [P, CST_W])
        rotc = sb("rotc", [P, 2, TILES, P])
        tok = sb("tok", [P, TILES], I32)
        zero_i = sb("zero_i", [P, ITEMS], I32)
        bf_cum = sb("bf_cum", [P, 2, P], BF16)
        wr = sb("wr", [P, KD, NE])
        br = sb("br", [P, NE])
        lnst = sb("lnst", [P, TILES, 2, 6])
        lnmv = sb("lnmv", [P, TILES, 2])
        lnsd = sb("lnsd", [P, TILES])
        lnrs = sb("lnrs", [P, TILES])
        gates = sb("gates", [P, 2, TILES])
        dest_i = sb("dest_i", [P, 2, TILES], I32)
        eid_i = sb("eid_i", [P, ITEMS], I32)
        np_i = sb("np_i", [P, DEPTH], I32)
        slot_i = sb("slot_i", [P, 2], I32)
        slot_c = sb("slot_c", [P, 2], I32)
        dest_c = sb("dest_c", [P, 2, TILES], I32)
        primer = sb("primer", [P, 4], I32)
        ptab = sb("ptab", [1, DEC * NPG], I32)

        def C(name, r=P):
            o, w = _cols[name]
            return cst[0:r, o:o + w]

        def view(off, *shape, r=P, region=None):
            n = int(np.prod(shape))
            assert off + n <= MWORDS
            v = M[0:r, off:off + n]
            if len(shape) == 1:
                return v
            names = "abcd"[:len(shape)]
            return v.rearrange(f"p ({' '.join(names)}) -> p {' '.join(names)}",
                               **{k: s for k, s in zip(names[1:], shape[1:])})

        ident = C("ident")


        stream, state_uses = [], [0] * 3
        for l in range(DEPTH):
            for n in range(12):
                stream.append((("mod", l, n), [("mod_mm", 12 * l + n + 1)]))
        for hp in range(2):
            ret = lambda i: [("ret_mm", (6 * hp + i + 1) * TILES)]
            stream += [(("q", hp), ret(0)), (("k", hp), ret(1)), (("v", hp, 0), ret(2)), (("v", hp, 1), ret(3))]
            for b2 in range(4):
                n = 4 * hp + b2 + 1
                s = len(stream) % 3
                state_uses[s] += 1
                stream.append((("state", hp, b2), [("os_mm", 4 * n), (f"state_st{s}", 32 * state_uses[s])]))
            stream += [(("g", hp, 0), ret(4)), (("g", hp, 1), ret(5))]
        for n in range(2):
            stream.append((("out0", n, 0), [("out_half0", TILES * (n + 1))]))
            stream.append((("out0", n, 1), [("out_mm0", TILES * (n + 1))]))
        N_FIRST = len(stream)
        for n in range(6):
            stream.append((("din", n), [("d_mm", TILES * (n + 1))]))
        stream += [(("ipg",), [("ki_t", DEC)]), (("kpg",), [("kk_t", 2 * DEC)]), (("vpg",), [("s_pv", KVH)])]
        for n in range(2):
            stream.append((("out2", n, 0), [("out_mm2", TILES * (n + 1))]))
        N_LOADS = {"state": 2, "kpg": DEC * NPG, "vpg": DEC * NPG, "ipg": 2 * DEC * NPG}
        place, brought = {}, [0] * 3
        for i, (key, _) in enumerate(stream):
            brought[i % 3] += 16 * N_LOADS.get(key[0], 1)
            place[key] = (i, i % 3, brought[i % 3])

        def slot(key, k=KD, n=NB):
            return RING[:, place[key][1], 0:k * n].rearrange("p (k n) -> p k n", n=n)

        def wait_slot(eng, key):
            eng.wait_ge(S(f"ring_full{place[key][1]}"), place[key][2])

        tiles_of = [(TILES + 1) // 2, TILES // 2]

        def moe_w(j, c):
            w = RING[:, c, :] if j == 0 else M[:, c * KD * NB:(c + 1) * KD * NB]
            return w.rearrange("p (k n) -> p k n", n=NB if c < 2 else D)

        CROW = view(0, D, r=DEC + 1)
        CSIL = view(D, D, r=DEC + 1)
        BMOD = view(2 * D, DEPTH, 6 * D, r=DEC + 1)
        MODV = view(14 * D, 6 * D, r=DEC + 1)
        CT = view(20 * D, KD, DEC + 1)
        HN = [view(0, D), view(D, D)]
        o = 0
        YT = view(o, 16, TOK)
        o += 16 * TOK
        QT = view(o, 4, TOK)
        KT = view(o + 4 * TOK, 4, TOK)
        o += 8 * TOK
        KN = view(o, NT, NB)
        o += NT * NB
        V = view(o, TILES, 2 * NB)
        o += TILES * 2 * NB
        RT, T1, RO = view(o, NB), view(o + NB, NB), view(o + 2 * NB, NB)
        SG = [RT, T1]
        GNB = BC[:, 0, :]
        STATE = BC[:, 1:3, :].rearrange("p h (j v) -> p h j v", j=2)
        att = sb("att", [P, 2, P])
        qmask = sb("qmask", [P, DEC, 4, DEC])
        gnst = sb("gnst", [P, TILES, 6])
        gnmv = sb("gnmv", [P, 2, TILES, 2])
        gnsd = sb("gnsd", [P, 2, TILES])
        gnrs = sb("gnrs", [P, 2, TILES])
        EPT = {0: RT, 2: view(0, NB)}

        o = NB
        DRT = [view(o, NB), view(o + NB, NB)]
        o += 2 * NB
        RX = view(o, 4, 64)
        o += 256
        DQT = view(o, QH, TOK)
        o += QH * TOK
        QIT = view(o, IH // 2, TOK)
        o += QH * TOK
        DKT = view(o, KVH, TOK)
        o += KVH * TOK
        KIT = view(o, TOK)
        o += TOK
        KV = view(o, TILES, 2 * KVH * HD)
        o += TILES * 2 * KVH * HD
        KIW = view(o, TILES, ID + IH)
        o += TILES * (ID + IH)
        KID = view(o, TILES, 2 * ID)
        o += TILES * 2 * ID
        WI = view(o, TILES, IH)
        o += TILES * IH
        o_late = o
        SCORE, BIAS = view(o, NB), view(o + NB, NB)
        o += 2 * NB
        RL = [view(o, NB), view(o + NB, NB)]
        o += 2 * NB
        E = [view(o, NB), view(o + NB, NB)]
        o += 2 * NB
        PT = [view(o, NT, P), view(o + NB, NT, P)]
        o += 2 * NB
        m8 = sb("m8", [P, 8])
        mx = sb("mx", [P, 2])
        nbias = sb("nbias", [P, 2])
        esum = sb("esum", [P, 2])
        ersum = sb("ersum", [P, 2])
        OT = HT
        o = o_late
        KBT = view(o, DEC, KVH, LS)
        o += DEC * KVH * LS
        KIBT = [view(o, LS), view(o + LS, LS)]
        o += 2 * LS
        assert o <= MWORDS, o
        o = 0
        RLS = [view(0, 2, LS, r=DEC), view(2 * LS, 2, LS, r=DEC)]
        SCS, BIS = view(4 * LS, LS, r=DEC), view(5 * LS, LS, r=DEC)
        assert 6 * LS <= 3 * NB + 256
        QM = sb("QM", [P, DEC, KVH, DEC * GRP])
        WM = sb("WM", [DEC, 2, DEC, DEC])
        PS = [sb(f"PS{n}", [DEC * GRP, LS]) for n in range(KVH)]
        PTS = sb("PTS", [P, KVH, NPG, DEC * GRP])
        PNW = sb("PNW", [DEC, KVH, DEC * GRP])
        DG = sb("DG", [DEC * GRP, KVH, DEC * GRP])

        o = 3 * KD * NB
        HG = [view(o, D), view(o + D, D)]
        o += 2 * D
        HGT = [view(o, KD, P), view(o + D, KD, P)]
        o += 2 * D
        SGE = [view(o, FE), view(o + FE, FE)]
        o += 2 * FE
        AE = [view(o, FE), view(o + FE, FE)]
        o += 2 * FE
        AT = [view(o, FE // P, P), view(o + FE, FE // P, P)]
        o += 2 * FE
        Y = [view(o, D), view(o + D, D)]
        o += 2 * D
        assert o <= MWORDS, o
        ro = [3 * KD * NB + 2 * D]

        def rview(*shape):
            ro[0] += int(np.prod(shape))
            assert ro[0] <= MWORDS
            return view(ro[0] - int(np.prod(shape)), *shape)

        LG, PR, KEY, EQ, S1, S2, PM, DST = [rview(TILES, NE) for _ in range(8)]
        PAIRS = rview(TILES * NG, 6)
        GS, GK, GQ = [rview(TILES, NG) for _ in range(3)]
        r1, r2, r3, r4 = [rview(TILES) for _ in range(4)]
        cntv, nbk, cum, sta, thr = [rview(NE) for _ in range(5)]
        big = rview(ITEMS, NE)
        itf = rview(ITEMS)
        mb = sb("mb", [P, TILES, NE], BF16)
        YG = [[view((2 * b + k) * D, D) for k in range(2)] for b in range(2)]
        EPM = view(4 * D, D)

        out_waits = [("rp_st", 16 * RH), *[(f"state_st{s}", 32 * state_uses[s]) for s in range(3)], ("kv_st", 16 * 3 * TILES), ("y_out", 16 * TILES)]

        def pairs(eng, l):
            first = 0
            for k in range(l):
                first = first + eng.value_load(np_i[0:1, k:k + 1], min_val=1, max_val=ITEMS // 2)
            return first, eng.value_load(np_i[0:1, l:l + 1], min_val=1, max_val=ITEMS // 2)

        block = ctx.enter_context(nc.Block())

        @block.sync
        def _(sp):
            def kpn(w, at, n):
                return w.rearrange("(k p) n -> p k n", p=P)[:, :, at:at + n]

            def wait_free(i):
                if i >= 3:
                    for name, v in stream[i - 3][1]:
                        sp.wait_ge(S(name), v)

            def load(key):
                i, s, _ = place[key]
                wait_free(i)
                kind = key[0]
                dst = slot(key)
                if kind == "state":
                    _, hp, b2 = key
                    for bb in range(2):
                        sp.dma_start(dst[:, 4 * bb:4 * bb + 4, :],
                                     A["state_ret"][0, 2 * b2 + bb, 2 * hp:2 * hp + 2]
                                     .rearrange("h (j p) v -> p (h j) v", p=P)).then_inc(S(f"ring_full{s}"), 16)
                    return
                if kind == "mod":
                    src = kpn(A["w_mod"][key[1]], key[2] * NB, NB)
                elif kind in ("q", "k"):
                    src = kpn(A["w_in_ret"][0], {"q": 0, "k": RH * RDK}[kind] + key[1] * NB, NB)
                elif kind in ("v", "g"):
                    at = {"v": 2 * RH * RDK, "g": 2 * RH * RDK + RH * RDV}[kind]
                    src = kpn(A["w_in_ret"][0], at + (2 * key[1] + key[2]) * NB, NB)
                elif kind == "out0":
                    src = kpn(A["w_out_ret"][0, key[2] * D:(key[2] + 1) * D, :], key[1] * NB, NB)
                elif kind == "out2":
                    src = kpn(A["w_out_dsa"][0], key[1] * NB, NB)
                else:
                    w = min(NB, DSA_IN - key[1] * NB)
                    src = kpn(A["w_in_dsa"][0], key[1] * NB, w)
                    dst = slot(key, KD, w)
                sp.dma_start(dst, src).then_inc(S(f"ring_full{s}"), 16)

            def load_pages(key):
                i, s, _ = place[(key,)]
                wait_free(i)
                src = A[{"kpg": "cache_k", "vpg": "cache_v", "ipg": "cache_kidx"}[key]]
                dst = RING[:, s, :]
                for i in range(DEC * NPG):
                    pg = sp.value_load(ptab[0:1, i:i + 1], min_val=0, max_val=src.shape[1] - 1)
                    if key == "ipg":
                        for c in range(2):
                            sp.dma_start(dst[:, i * P + c * ID:i * P + (c + 1) * ID],
                                         src[0, bass.ds(pg, 1)].rearrange("o t d -> (o t) d"))\
                                .then_inc(S(f"ring_full{s}"), 16)
                    else:
                        sp.dma_start(dst[:, i * KVH * HD:(i + 1) * KVH * HD],
                                     src[0, bass.ds(pg, 1)].rearrange("o t h d -> (o t) (h d)"))\
                            .then_inc(S(f"ring_full{s}"), 16)

            def moe_loads(l):
                last = N_FIRST if l == 0 else len(stream)
                for i in range(last, last + 3):
                    wait_free(i)
                sp.wait_ge(S(f"tables{l}"), 1)
                sp.wait_ge(S(f"scattered{l}"), 16 * 2 * TILES)
                first, count = pairs(sp, l)
                with sp.Fori(0, count) as k:
                    i = first + k
                    for j in range(2):
                        e = sp.value_load(eid_i[0:1, bass.ds(k * 2 + j, 1)], min_val=0, max_val=NE - 1)
                        sp.wait_ge(S(f"slots_used{j}"), i + 1)
                        sp.dma_start(slot_i[:, j:j + 1], slot_d[bass.ds((k * 2 + j) * P, P), :])\
                            .then_inc(S(f"slots_in{j}"), 16)
                        for c, w in enumerate(("w_gate", "w_up", "w_down")):
                            sp.wait_ge(S(f"pe_{w}{j}"), i + 1)
                            sp.dma_start(moe_w(j, c), A[w][l, bass.ds(e, 1)]
                                         .rearrange("o (k p) n -> p (o k) n", p=P)).then_inc(S(f"{w}_in{j}"), 16)
                if l == 0:
                    for j in range(2):
                        sp.wait_ge(S(f"pe_w_down{j}"), first + count + 1)

            def loads(part):
                for key, _ in part:
                    if key[0].endswith("pg"):
                        load_pages(key[0])
                    else:
                        load(key)

            sp.dma_start(ptab[0:1, :], A["page_table"].rearrange("(o b) j -> o (b j)", o=1)).then_inc(S("ptab_in"), 16)
            sp.wait_ge(S("ptab_in"), 16)
            loads(stream[:N_FIRST])
            moe_loads(0)
            loads(stream[N_FIRST:])
            moe_loads(1)
            for name, v in out_waits:
                sp.wait_ge(S(name), v)

        @block.tensor
        def _(pe):
            def transposes(dst, srcs, sem):
                for d_, s_ in zip(dst, srcs):
                    r = s_.shape[0]
                    last = pe.transpose(d_, s_, ident[0:r, 0:r])
                last.then_inc(S(sem), 1)

            def rhs_mm(out, lhs, w, sem, start=True, stop=True):
                K = lhs.shape[1]
                for k in range(K):
                    last = pe.matmul(out, lhs[:, k, :], w[:, k, :], start=start and k == 0, stop=stop and k == K - 1)
                last.then_inc(S(sem), 1)

            def modulated(m):
                for t in range(TILES):
                    R = rows(t)
                    pe.wait_ge(S("hn"), TILES * m + t + 1)
                    for g in range(2):
                        if t:
                            pe.wait_ge(S("ht_ev"), 2 * TILES * m + 2 * (t - 1) + g + 1)
                        transposes([bank[6 + g][:, q * R:(q + 1) * R] for q in range(4)],
                                   [HN[t % 2][0:R, (4 * g + q) * P:(4 * g + q + 1) * P] for q in range(4)], "ht_ps")
                pe.wait_ge(S("ht_ev"), 2 * TILES * m + 2 * TILES)

            def out_product(m, src, halves):
                for n in range(2):
                    for kh in range(halves):
                        wait_slot(pe, (f"out{m}", n, kh))
                        for t in range(TILES):
                            if kh == 0 and n == 1 and t >= 3:
                                pe.wait_ge(S(f"out_ev{m}"), t - 2)
                            rhs_mm(bank[(TILES * n + t) % 8][0:rows(t), :], src[:, kh * KD:(kh + 1) * KD, cols(t)],
                                   slot((f"out{m}", n, kh)), f"out_mm{m}" if kh == halves - 1 else f"out_half{m}",
                                   start=kh == 0, stop=kh == halves - 1)

            for j in range(2):
                for name in ("pe_w_gate", "pe_w_up", "pe_w_down", "at_ps"):
                    pe.nop().then_inc(S(f"{name}{j}"), 1)
                pe.nop().then_inc(S(f"hg_ps{j}"), 2)
            pe.wait_ge(S("const_in"), 16 * N_CONST)
            pe.wait_ge(S("c_silu"), 1)
            R = DEC + 1
            transposes([bank[2][:, k * R:(k + 1) * R] for k in range(KD)],
                       [CSIL[:, k * P:(k + 1) * P] for k in range(KD)], "c_ps")
            pe.wait_ge(S("c_t"), 1)
            for l in range(DEPTH):
                for n in range(12):
                    u = 12 * l + n
                    wait_slot(pe, ("mod", l, n))
                    if u >= 2:
                        pe.wait_ge(S("mod_ev"), u - 1)
                    rhs_mm(bank[u % 2][0:R, :], CT, slot(("mod", l, n)), "mod_mm")

            modulated(0)
            item = 0

            def ret_product(w_key, t):
                nonlocal item
                if t == 0:
                    wait_slot(pe, w_key)
                if item >= 2:
                    pe.wait_ge(S("ret_ev"), item - 1)
                rhs_mm(bank[item % 2][0:rows(t), :], HT[:, :, cols(t)], slot(w_key), "ret_mm")
                item += 1

            qk = 0
            yt = 0
            for hp in range(2):
                def turn_qk():
                    nonlocal qk
                    t = qk % TILES
                    R = rows(t)
                    pe.wait_ge(S("ro_rdy"), qk + 1)
                    if qk >= 2:
                        pe.wait_ge(S("qk_ev"), qk - 1)
                    isk = (qk // TILES) % 2
                    src = KN[:, t, :] if isk and t < NT else RO
                    transposes([bank[2 + qk % 2][:, q * R:(q + 1) * R] for q in range(4)],
                               [src[0:R, q * P:(q + 1) * P] for q in range(4)], "qk_ps")
                    qk += 1

                for i in range(2 * TILES):
                    ret_product((("q", "k")[i // TILES], hp), i % TILES)
                    if i:
                        turn_qk()
                ret_product(("v", hp, 0), 0)
                turn_qk()
                for i in range(1, 2 * TILES):
                    ret_product(("v", hp, i // TILES), i % TILES)
                pe.wait_ge(S("qk_ev"), qk)
                pe.wait_ge(S("ret_ev"), item)

                def attend(i):
                    hh, c = divmod(i, NT)
                    rc = hp * 2 * NT + i
                    if rc >= 2:
                        pe.wait_ge(S("att_rdy"), rc - 1)
                    for j in range(2):
                        last = pe.matmul(bank[3 + rc % 2][:, 0:P], KT[:, 2 * hh + j, cols(c)], QT[:, 2 * hh + j, cols(c)],
                                         start=j == 0, stop=j == 1)
                    last.then_inc(S("att_ps"), 1)

                attend(0)
                for i in range(2 * NT):
                    hh, c = divmod(i, NT)
                    rc = hp * 2 * NT + i
                    if i + 1 < 2 * NT:
                        attend(i + 1)
                    pe.wait_ge(S("att_rdy"), rc + 1)
                    if rc:
                        pe.wait_ge(S("s_rdy"), rc)
                        pe.wait_ge(S("o_ev"), rc)
                    vv = V[:, c, hh * NB:(hh + 1) * NB]
                    last = pe.matmul(bank[5][:, :], att[:, rc % 2, :], vv, start=True, stop=c == 0)
                    if c:
                        for j in range(2):
                            last = pe.matmul(bank[5][:, :], QT[:, 2 * hh + j, cols(c)], STATE[:, hh, j, :],
                                             start=False, stop=j == 1)
                    last.then_inc(S("o_ps"), 1)
                    for j in range(2):
                        last = pe.matmul(bank[6 + j][:, :], KN[:, c, (2 * hh + j) * P:(2 * hh + j + 1) * P], vv,
                                         start=True, stop=True)
                    last.then_inc(S("u_ps"), 1)

                def spread(i):
                    si = 2 * DEC * hp + i
                    if si >= 2:
                        pe.wait_ge(S("st_upd"), si - 1)
                    b, hh = divmod(i, 2)
                    pe.matmul(bank[2 + si % 2][:, :], ident[0:DEC, b:b + 1].to_broadcast([DEC, P]),
                              V[0:DEC, NT, hh * NB:(hh + 1) * NB], start=True, stop=True).then_inc(S("vb_ps"), 1)

                spread(0)
                pe.wait_ge(S("qm_rdy"), hp + 1)
                for i in range(2 * DEC):
                    si = 2 * DEC * hp + i
                    b, hh = divmod(i, 2)
                    if i + 1 < 2 * DEC:
                        spread(i + 1)
                    pe.wait_ge(S("st_upd"), si + 1)
                    st = slot(("state", hp, b // 2))
                    for j in range(2):
                        last = pe.matmul(bank[hh][0:DEC, :], qmask[:, b, 2 * hh + j, :],
                                         st[:, 4 * (b % 2) + 2 * hh + j, :], start=b == 0 and j == 0,
                                         stop=b == DEC - 1 and j == 1)
                    last.then_inc(S("os_mm"), 1)
                pe.wait_ge(S("os_ev"), 2 * (hp + 1))

                def turn_y():
                    nonlocal yt
                    t = yt % TILES
                    R = rows(t)
                    hh = (yt // TILES) % 2
                    pe.wait_ge(S("y_rdy"), yt + 1)
                    if yt >= 2:
                        pe.wait_ge(S("yt_ev"), yt - 1)
                    transposes([bank[2 + yt % 2][:, q * R:(q + 1) * R] for q in range(4)],
                               [V[0:R, t, hh * NB + q * P:hh * NB + (q + 1) * P] for q in range(4)], "yt_ps")
                    yt += 1

                for i in range(2 * TILES):
                    ret_product(("g", hp, i // TILES), i % TILES)
                    if i:
                        turn_y()
                turn_y()
            pe.wait_ge(S("yt_ev"), yt)
            pe.wait_ge(S("ret_ev"), item)
            out_product(0, YT, 2)

            def experts(l):
                m = 2 * l + 1
                modulated(m)
                for t in range(TILES):
                    rhs_mm(bank[0][0:rows(t), t * NE:(t + 1) * NE], HT[:, :, cols(t)], wr[:, :, :], f"lg_mm{l}")
                pe.wait_ge(S(f"marks{l}"), 1)
                for t in range(TILES + 1):
                    for t2 in range(min(t, TILES - 1) + 1):
                        last = pe.matmul(bank[1][:, t * NE:(t + 1) * NE], bf_cum[:, 0 if t2 == t else 1, :], mb[:, t2, :],
                                         start=t2 == 0, stop=t2 == min(t, TILES - 1))
                last.then_inc(S(f"rank_mm{l}"), 1)
                pe.wait_ge(S(f"tables{l}"), 1)
                first, count = pairs(pe, l)
                with pe.Fori(0, count) as k:
                    i = first + k
                    def turn_rows(j):
                        pe.wait_ge(S(f"rows_in{j}"), (i + 1) * 16)
                        if j == 0:
                            pe.wait_ge(S(f"at_ev0"), i + 1)
                            pe.wait_ge(S(f"y_ev_d0"), i + 1)
                        else:
                            pe.wait_ge(S(f"y_ev_a0"), i + 1)
                            pe.wait_ge(S(f"at_ev1"), i + 1)
                        for g in range(2):
                            transposes([bank[2 * j + g][:, q * P:(q + 1) * P] for q in range(4)],
                                       [HG[j][:, (4 * g + q) * P:(4 * g + q + 1) * P] for q in range(4)], f"hg_ps{j}")

                    def up(j, c, w):
                        pe.wait_ge(S(f"{w}_in{j}"), (i + 1) * 16)
                        rhs_mm(bank[4 + 2 * j + c][:, :], HGT[j], moe_w(j, c), f"pe_{w}{j}")

                    def turn_a(j):
                        pe.wait_ge(S(f"a_rdy{j}"), i + 2)
                        transposes([bank[3 * j][:, q * P:(q + 1) * P] for q in range(4)],
                                   [AE[j][:, q * P:(q + 1) * P] for q in range(4)], f"at_ps{j}")

                    def down(j):
                        pe.wait_ge(S(f"w_down_in{j}"), (i + 1) * 16)
                        pe.wait_ge(S(f"at_ev{j}"), i + 2)
                        w = moe_w(j, 2)
                        for n in range(2):
                            for k in range(FE // P):
                                last = pe.matmul(bank[(1, 4)[j] + n][:, :], AT[j][:, k, :], w[:, k, n * NB:(n + 1) * NB],
                                                 start=k == 0, stop=k == FE // P - 1)
                            if n == 0:
                                last.then_inc(S(f"y_mm{j}"), 1)
                        last.then_inc(S(f"pe_w_down{j}"), 1)

                    turn_rows(0)
                    turn_rows(1)
                    pe.wait_ge(S(f"hgt0"), 2 * (i + 1))
                    pe.wait_ge(S(f"y_ev_d1"), i + 1)
                    up(0, 0, "w_gate")
                    pe.wait_ge(S(f"y_ev_a1"), i + 1)
                    up(0, 1, "w_up")
                    pe.wait_ge(S(f"hgt1"), 2 * (i + 1))
                    pe.wait_ge(S(f"a_rdy1"), i + 1)
                    up(1, 0, "w_gate")
                    turn_a(0)
                    up(1, 1, "w_up")
                    down(0)
                    turn_a(1)
                    down(1)

            experts(0)

            modulated(2)
            dt = 0

            def turn_d():
                nonlocal dt
                n, t = divmod(dt, TILES)
                R = rows(t)
                pe.wait_ge(S("d_rot"), dt + 1)
                if dt >= 2:
                    pe.wait_ge(S("d_tev"), dt - 1)
                src, nq = ((DRT[dt % 2], 4), (DRT[dt % 2], 4), (KV[:, t, :], 2), (DRT[dt % 2], 4), (DRT[dt % 2], 4),
                           (KID[:, t, :], 1))[n]
                transposes([bank[2 + dt % 2][:, q * R:(q + 1) * R] for q in range(nq)],
                           [src[0:R, q * P:(q + 1) * P] for q in range(nq)], "d_tp")
                dt += 1

            for i in range(6 * TILES):
                n, t = divmod(i, TILES)
                if t == 0:
                    wait_slot(pe, ("din", n))
                if i >= 2:
                    pe.wait_ge(S("d_ev"), i - 1)
                w = min(NB, DSA_IN - n * NB)
                rhs_mm(bank[i % 2][0:rows(t), 0:w], HT[:, :, cols(t)], slot(("din", n), KD, w), "d_mm")
                if i:
                    turn_d()
            turn_d()
            pe.wait_ge(S("d_tev"), 6 * TILES)
            pe.wait_ge(S("d_ev"), 6 * TILES)
            ix = 0
            for t in range(NT):
                L = (t + 1) * P
                if t:
                    for h in range(IH):
                        if ix >= 2:
                            pe.wait_ge(S("ix_rl"), ix - 1)
                        o64 = ID * (h % 2)
                        pe.matmul(bank[ix % 2][:, 0:L], QIT[o64:o64 + ID, h // 2, cols(t)], KIT[o64:o64 + ID, 0:L],
                                  start=True, stop=True).then_inc(S("ix_ps"), 1)
                        ix += 1

                def logits(h):
                    a = t * QH + h
                    if a >= 2:
                        pe.wait_ge(S("lg_ev"), a - 1)
                    pe.matmul(bank[2 + a % 2][:, 0:L], DQT[:, h, cols(t)], DKT[:, h // GRP, 0:L],
                              start=True, stop=True).then_inc(S("lg_ps"), 1)

                def turn_p(h):
                    a = t * QH + h
                    pe.wait_ge(S("p_rdy"), a + 1)
                    if a >= 2:
                        pe.wait_ge(S("pt_ev"), a - 1)
                    transposes([bank[4 + a % 2][:, q * P:(q + 1) * P] for q in range(t + 1)],
                               [E[a % 2][:, q * P:(q + 1) * P] for q in range(t + 1)], "pt_ps")

                def pv(h):
                    a = t * QH + h
                    pe.wait_ge(S("pt_ev"), a + 1)
                    if a >= 2:
                        pe.wait_ge(S("ot_ev"), a - 1)
                    n = h // GRP
                    for c in range(t + 1):
                        last = pe.matmul(bank[6 + a % 2][:, 0:P], KV[:, c, KVH * HD + n * HD:KVH * HD + (n + 1) * HD],
                                         PT[a % 2][:, c, :], start=c == 0, stop=c == t)
                    last.then_inc(S("pv_mm"), 1)

                for s in range(QH + 3):
                    if s < QH:
                        logits(s)
                    if 2 <= s < QH + 2:
                        turn_p(s - 2)
                    if s >= 3:
                        pv(s - 3)

            transposes([bank[0][0:DEC, par * DEC:(par + 1) * DEC] for par in range(2)],
                       [WI[0:DEC, NT, :].rearrange("p (h two) -> p two h", two=2)[:, par, :] for par in range(2)], "w_t")
            wait_slot(pe, ("ipg",))
            wait_slot(pe, ("kpg",))
            pe.wait_ge(S("ot_ev"), NT * QH)
            pe.wait_ge(S("wm_rdy"), 1)
            ipg = RING[:, place[("ipg",)][1], 0:DEC * NPG * P].rearrange("p (i d) -> p i d", d=P)
            kpg = RING[:, place[("kpg",)][1], :].rearrange("p (i n d) -> p i n d", n=KVH, d=HD)
            vpg = RING[:, place[("vpg",)][1], :].rearrange("p (i n d) -> p i n d", n=KVH, d=HD)

            def s_score(b):
                pe.wait_ge(S("s_rl"), b + 1)
                for par in range(2):
                    last = pe.matmul(bank[6][0:DEC, 0:LS], WM[:, par, b, :], RLS[b % 2][:, par, :],
                                     start=b == 0 and par == 0, stop=b == DEC - 1 and par == 1)
                last.then_inc(S("s_sc"), 1)

            for b in range(DEC):
                if b:
                    pe.wait_ge(S("ki_ev"), b)
                transposes([bank[0][:, q * P:(q + 1) * P] for q in range(NPG)],
                           [ipg[:, b * NPG + q, :] for q in range(NPG)], "ki_t")
                for n in range(KVH):
                    if b:
                        pe.wait_ge(S("kk_ev"), 2 * (b - 1) + n + 1)
                    transposes([bank[1 + n][:, q * P:(q + 1) * P] for q in range(NPG)],
                               [kpg[:, b * NPG + q, n, :] for q in range(NPG)], "kk_t")
                pe.wait_ge(S("ki_rdy"), b + 1)
                pe.wait_ge(S("ki_ev"), b + 1)
                if b:
                    pe.wait_ge(S("s_rl"), b)
                for par in range(2):
                    last = pe.matmul(bank[3 + par][0:DEC, 0:LS],
                                     QIT[par * ID:(par + 1) * ID, :, SEQ + b], KIBT[b % 2][par * ID:(par + 1) * ID, :],
                                     start=True, stop=True)
                last.then_inc(S("s_dot"), 1)
                if b:
                    s_score(b - 1)
            s_score(DEC - 1)
            pe.wait_ge(S("s_bias"), 1)
            pe.wait_ge(S("kk_ev"), 2 * DEC)
            pe.wait_ge(S("kn_rdy"), 1)
            for n in range(KVH):
                pe.matmul(bank[n][0:DEC * GRP, 0:LS], C("bexp", DEC), BIS[0:DEC, :], start=True, stop=False)
                for b in range(DEC):
                    last = pe.matmul(bank[n][0:DEC * GRP, 0:LS], QM[:, b, n, :], KBT[:, b, n, :], start=False,
                                     stop=b == DEC - 1)
                last.then_inc(S("s_lg"), 1)
            wait_slot(pe, ("vpg",))
            for n in range(KVH):
                pe.wait_ge(S("s_p"), n + 1)
                r = DEC * GRP
                for q in range(NPG):
                    pe.transpose(bank[2 + n][:, q * r:(q + 1) * r], PS[n][:, q * P:(q + 1) * P], ident[0:r, 0:r])
                pe.matmul(bank[4 + n][0:DEC, 0:r], C("bsel", r), DG[:, n, :], start=True, stop=True).then_inc(S("s_pt"), 1)
            for n in range(KVH):
                pe.wait_ge(S("s_ptev"), n + 1)
                out = bank[6 + n]
                pe.matmul(out[:, 0:DEC * GRP], KV[0:DEC, NT, (KVH + n) * HD:(KVH + n + 1) * HD], PNW[:, n, :],
                          start=True, stop=False)
                for b in range(DEC):
                    for q in range(NPG):
                        last = pe.matmul(out[:, b * GRP:(b + 1) * GRP], vpg[:, b * NPG + q, n, :],
                                         PTS[:, n, q, b * GRP:(b + 1) * GRP], start=False,
                                         stop=b == DEC - 1 and q == NPG - 1)
                last.then_inc(S("s_pv"), 1)
            pe.wait_ge(S("s_ot"), KVH)
            pe.wait_ge(S("ot_ev"), NT * QH)
            out_product(2, OT, 1)
            experts(1)

        @block.scalar
        def _(act):
            def vectors(m, n, parts, sample):
                l, half = divmod(m, 2)
                for i, p_ in parts:
                    at = (3 * half + p_) * D
                    act.dma_start(BC[:, i, :], mod_d[l, DEC:DEC + 1, at:at + D].to_broadcast([P, D])).then_inc(S(n), 16)
                    act.dma_start(SC[:, i, :], mod_d[l, 0:DEC, at:at + D]).then_inc(S(n), 16)

            def modulated(m):
                if m:
                    act.wait_ge(S("x_rdy"), TILES * m)
                act.wait_ge(S("mod_st"), 16 * DEPTH)
                vectors(m, "bc_in", ((0, 1), (1, 0)), True)
                if m == 0:
                    act.wait_ge(S("y_zero"), 16)
                for t in range(TILES):
                    R = rows(t)
                    for g in range(2):
                        act.wait_ge(S("ht_ps"), 2 * TILES * m + 2 * t + g + 1)
                        act.activation(HT[:, 4 * g:4 * g + 4, cols(t)],
                                       bank[6 + g][:, 0:4 * R].rearrange("p (q r) -> p q r", r=R),
                                       ACT.Copy).then_inc(S("ht_ev"), 1)

            def closing(m):
                l, half = divmod(m, 2)
                vectors(m, "ep_in", ((0, 2),), True)
                for i, w in ((1, ("ln1_g", "ln2_g")[half]), (2, ("ln1_b", "ln2_b")[half])):
                    act.dma_start(BC[:, i, :], A[w][l:l + 1, :].to_broadcast([P, D])).then_inc(S("ep_in"), 16)

            def roots(m):
                act.wait_ge(S("ln_var"), 1 * m + 1)
                act.activation(lnsd[:, :], lnmv[:, :, 1], ACT.Sqrt, bias=C("lneps"), scale=1.0).then_inc(S("ln_sd"), 1)

            for j in range(2):
                act.dma_start(primer[:, 2 * j:2 * j + 2], A["tok"][:, 0:2]).then_inc(S(f"y_st{j}"), 16)
                for name in ("at_ev", "y_ev_a"):
                    act.nop().then_inc(S(f"{name}{j}"), 1)
            act.dma_start(CROW[0:DEC, :], A["c_sample"]).then_inc(S("c_in"), 16)
            act.dma_start(CROW[DEC:DEC + 1, :], A["c_prompt"]).then_inc(S("c_in"), 16)
            act.dma_start(cst[:, :], A["cst"]).then_inc(S("const_in"), 16)
            act.dma_start(BMOD[:, :, :], A["b_mod"].rearrange("(o l) n -> o l n", o=1).to_broadcast([DEC + 1, DEPTH, 6 * D]))\
                .then_inc(S("bmod_in"), 16)
            act.dma_start(rotc[:, :, :, :], A["rotc"]).then_inc(S("const_in"), 16)
            act.dma_start(tok[:, :], A["tok"]).then_inc(S("const_in"), 16)
            act.dma_start(wr[:, :, :], A["w_router"].rearrange("(k p) e -> p k e", p=P)).then_inc(S("const_in"), 16)
            act.dma_start(br[:, :], A["b_router"].rearrange("(o e) -> o e", o=1).to_broadcast([P, NE])).then_inc(S("const_in"), 16)
            act.dma_start(X[:, 0:NT, :], A["x_prompt"][0].rearrange("(t p) d -> p t d", p=P)).then_inc(S("x_in"), 16)
            act.dma_start(X[0:DEC, NT, :], A["x_sample"].rearrange("b t d -> (b t) d")).then_inc(S("x_in"), 16)
            act.wait_ge(S("c_in"), 32)
            act.activation(CSIL[:, :], CROW[:, :], ACT.Silu).then_inc(S("c_silu"), 1)
            for l in range(DEPTH):
                act.wait_ge(S("mod_ev"), 12 * (l + 1))
                act.dma_start(mod_d[l], MODV[:, :]).then_inc(S("mod_st"), 16)

            modulated(0)
            item = qk = yt = 0
            for hp in range(2):
                if hp == 0:
                    act.wait_ge(S("hn"), TILES)
                else:
                    act.wait_ge(S("y_rdy"), 2 * TILES)
                act.dma_start(GNB, A["gn_ret_g"][0:1, hp * D:(hp + 1) * D].to_broadcast([P, D])).then_inc(S("gn_in"), 16)

                def take_qk():
                    nonlocal qk
                    t = qk % TILES
                    R = rows(t)
                    act.wait_ge(S("qk_ps"), qk + 1)
                    dst = (QT, KT)[(qk // TILES) % 2]
                    act.activation(dst[:, :, cols(t)], bank[2 + qk % 2][:, 0:4 * R].rearrange("p (q r) -> p q r", r=R),
                                   ACT.Copy).then_inc(S("qk_ev"), 1)
                    qk += 1

                for i in range(2 * TILES):
                    t = i % TILES
                    R = rows(t)
                    act.wait_ge(S("ret_mm"), item + 1)
                    if item:
                        act.wait_ge(S("ro_rdy"), hp * 2 * TILES + i)
                    if hp and i == 0:
                        act.wait_ge(S("y_rdy"), 2 * TILES)
                    for hh in range(2):
                        sc_ = C(("qs", "ks")[i // TILES])[0:R, t * RH + 2 * hp + hh:t * RH + 2 * hp + hh + 1]
                        last = act.activation(RT[0:R, hh * RDK:(hh + 1) * RDK],
                                              bank[item % 2][0:R, hh * RDK:(hh + 1) * RDK], ACT.Copy, scale=sc_)
                    last.then_inc(S("ret_ev"), 1)
                    item += 1
                    if i:
                        take_qk()
                for i in range(2 * TILES):
                    hh, t = divmod(i, TILES)
                    act.wait_ge(S("ret_mm"), item + 1)
                    act.activation(V[0:rows(t), t, hh * NB:(hh + 1) * NB], bank[item % 2][0:rows(t), :], ACT.Copy)\
                        .then_inc(S("ret_ev"), 1)
                    item += 1
                    if i == 0:
                        take_qk()
                for i in range(2 * NT):
                    hh, c = divmod(i, NT)
                    rc = hp * 2 * NT + i
                    act.wait_ge(S("u_ps"), rc + 1)
                    act.activation(V[:, c, hh * NB:(hh + 1) * NB], bank[5][:, :], ACT.Copy).then_inc(S("o_ev"), 1)
                for i in range(2 * DEC):
                    b, hh = divmod(i, 2)
                    key = ("state", hp, b // 2)
                    if i % 4 == 0:
                        wait_slot(act, key)
                    st = slot(key)[:, 4 * (b % 2) + 2 * hh:4 * (b % 2) + 2 * hh + 2, :]
                    act.activation(st, st, ACT.Copy, scale=GAMMA[2 * hp + hh]).then_inc(S("st_dec"), 1)
                act.wait_ge(S("os_mm"), 2 * DEC * (hp + 1))
                for hh in range(2):
                    act.activation(V[0:DEC, NT, hh * NB:(hh + 1) * NB], bank[hh][0:DEC, :], ACT.Copy)\
                        .then_inc(S("os_ev"), 1)
                act.wait_ge(S("gn_var"), hp + 1)
                act.activation(gnsd[:, :, :], gnmv[:, :, :, 1], ACT.Sqrt, bias=C("gneps"), scale=1.0).then_inc(S("gn_sd"), 1)

                def take_y():
                    nonlocal yt
                    t = yt % TILES
                    R = rows(t)
                    h = yt // TILES
                    act.wait_ge(S("yt_ps"), yt + 1)
                    act.activation(YT[:, 4 * h:4 * h + 4, cols(t)],
                                   bank[2 + yt % 2][:, 0:4 * R].rearrange("p (q r) -> p q r", r=R), ACT.Copy)\
                        .then_inc(S("yt_ev"), 1)
                    yt += 1

                for i in range(2 * TILES):
                    t = i % TILES
                    act.wait_ge(S("ret_mm"), item + 1)
                    g = hp * 2 * TILES + i
                    if i >= 2:
                        act.wait_ge(S("y_rdy"), g - 1)
                    act.activation(SG[i % 2][0:rows(t), :], bank[item % 2][0:rows(t), :], ACT.Silu).then_inc(S("ret_ev"), 1)
                    item += 1
                    if i:
                        take_y()
                take_y()
            act.wait_ge(S("y_rdy"), 4 * TILES)
            act.wait_ge(S("rp_st"), 16 * RH)
            closing(0)
            roots(0)

            def experts(l):
                m = 2 * l + 1
                modulated(m)
                act.wait_ge(S("hn"), TILES * m + TILES)
                closing(m)
                act.wait_ge(S(f"lg_sub{l}"), 1)
                act.activation(PR, LG, ACT.Exp).then_inc(S(f"lg_exp{l}"), 1)
                act.wait_ge(S(f"tables{l}"), 1)
                first, count = pairs(act, l)
                with act.Fori(0, count) as k:
                    i = first + k
                    def take_rows(j):
                        act.wait_ge(S(f"pe_w_up{j}"), i + 1)
                        for g in range(2):
                            act.wait_ge(S(f"hg_ps{j}"), 2 * i + g + 3)
                            act.activation(HGT[j][:, 4 * g:4 * g + 4, :],
                                           bank[2 * j + g][:, :].rearrange("p (q r) -> p q r", r=P),
                                           ACT.Copy).then_inc(S(f"hgt{j}"), 1)

                    def gate(j):
                        act.wait_ge(S(f"a_rdy{j}"), i + 1)
                        act.wait_ge(S(f"pe_w_gate{j}"), i + 2)
                        act.activation(SGE[j], bank[4 + 2 * j][:, :], ACT.Silu).then_inc(S(f"sg{j}"), 1)

                    def take_a(j):
                        act.wait_ge(S(f"pe_w_down{j}"), i + 1)
                        act.wait_ge(S(f"at_ps{j}"), i + 2)
                        act.activation(AT[j], bank[3 * j][:, :].rearrange("p (q r) -> p q r", r=P), ACT.Copy)\
                            .then_inc(S(f"at_ev{j}"), 1)

                    def take_y2(j):
                        act.wait_ge(S(f"pe_w_down{j}"), i + 2)
                        act.wait_ge(S(f"y_st{j}"), (i + 1) * 16)
                        act.activation(Y[j][:, NB:D], bank[(1, 4)[j] + 1][:, :], ACT.Copy).then_inc(S(f"y_ev_a{j}"), 1)
                        act.wait_ge(S(f"y_ev_d{j}"), i + 2)
                        act.wait_ge(S(f"y_ev_a{j}"), i + 2)
                        act.dma_start(y_d[bass.ds((k * 2 + j) * P, P), :], Y[j]).then_inc(S(f"y_st{j}"), 16)

                    take_rows(0)
                    take_rows(1)
                    gate(0)
                    gate(1)
                    take_a(0)
                    take_y2(0)
                    take_a(1)
                    take_y2(1)
                roots(m)

            experts(0)

            modulated(2)

            def take_d(i):
                n, t = divmod(i, TILES)
                R = rows(t)
                act.wait_ge(S("d_tp"), i + 1)
                dst = (DQT[:, 0:4], DQT[:, 4:8], DKT, QIT[:, 0:4], QIT[:, 4:8], None)[n]
                if n == 5:
                    act.activation(KIT[:, cols(t)], bank[2 + i % 2][:, 0:R], ACT.Copy).then_inc(S("d_tev"), 1)
                else:
                    nq = dst.shape[1]
                    act.activation(dst[:, :, cols(t)], bank[2 + i % 2][:, 0:nq * R].rearrange("p (q r) -> p q r", r=R),
                                   ACT.Copy).then_inc(S("d_tev"), 1)

            for i in range(6 * TILES):
                n, t = divmod(i, TILES)
                R = rows(t)
                act.wait_ge(S("d_mm"), i + 1)
                if i >= 2:
                    act.wait_ge(S("d_tp"), i - 1)
                w = min(NB, DSA_IN - n * NB)
                dst = KV[0:R, t, :] if n == 2 else KIW[0:R, t, :] if n == 5 else DRT[i % 2][0:R, :]
                act.activation(dst, bank[i % 2][0:R, 0:w], ACT.Copy).then_inc(S("d_ev"), 1)
                if i:
                    take_d(i - 1)
            take_d(6 * TILES - 1)
            ix = 0
            SCALE = HD ** -0.5
            for t in range(NT):
                L = (t + 1) * P
                if t:
                    for h in range(IH):
                        act.wait_ge(S("ix_ps"), ix + 1)
                        if ix >= 2:
                            act.wait_ge(S("ix_acc"), ix - 1)
                        act.activation(RL[ix % 2][:, 0:L], bank[ix % 2][:, 0:L], ACT.Relu, scale=ID ** -0.5)\
                            .then_inc(S("ix_rl"), 1)
                        ix += 1

                def take_p(h):
                    a = t * QH + h
                    act.wait_ge(S("pt_ps"), a + 1)
                    if a >= 2:
                        act.wait_ge(S("pv_mm"), a - 1)
                    act.activation(PT[a % 2][:, 0:t + 1, :], bank[4 + a % 2][:, 0:L].rearrange("p (q r) -> p q r", r=P),
                                   ACT.Copy).then_inc(S("pt_ev"), 1)

                def take_o(h):
                    a = t * QH + h
                    act.wait_ge(S("pv_mm"), a + 1)
                    act.activation(OT[:, h, cols(t)], bank[6 + a % 2][:, 0:P], ACT.Copy).then_inc(S("ot_ev"), 1)

                for s in range(QH + 3):
                    if s < QH:
                        a = t * QH + s
                        act.wait_ge(S("nb_rdy"), a + 1)
                        act.activation(E[a % 2][:, 0:L], E[a % 2][:, 0:L], ACT.Exp, bias=nbias[:, a % 2:a % 2 + 1],
                                       scale=SCALE, accum_out=esum[:, a % 2:a % 2 + 1]).then_inc(S("e_rdy"), 1)
                    if 2 <= s < QH + 2:
                        take_p(s - 2)
                    if s >= 3:
                        take_o(s - 3)

            for b in range(DEC):
                act.wait_ge(S("ki_t"), b + 1)
                if b >= 2:
                    act.wait_ge(S("s_dot"), b - 1)
                act.activation(KIBT[b % 2][:, 0:PAST], bank[0][:, 0:PAST], ACT.Copy).then_inc(S("ki_ev"), 1)
                for n in range(KVH):
                    act.wait_ge(S("kk_t"), 2 * b + n + 1)
                    act.activation(KBT[:, b, n, 0:PAST], bank[1 + n][:, 0:PAST], ACT.Copy).then_inc(S("kk_ev"), 1)
                act.wait_ge(S("s_dot"), b + 1)
                if b >= 2:
                    act.wait_ge(S("s_sc"), b - 1)
                for par in range(2):
                    last = act.activation(RLS[b % 2][:, par, :], bank[3 + par][0:DEC, 0:LS], ACT.Relu, scale=ID ** -0.5)
                last.then_inc(S("s_rl"), 1)
            for n in range(KVH):
                act.wait_ge(S("s_nb"), n + 1)
                r = DEC * GRP
                act.activation(PS[n][:, :], PS[n][:, :], ACT.Exp, bias=nbias[0:r, n:n + 1], scale=SCALE,
                               accum_out=esum[0:r, n:n + 1]).then_inc(S("s_e"), 1)
            for n in range(KVH):
                act.wait_ge(S("s_pt"), n + 1)
                r = DEC * GRP
                act.activation(PTS[:, n, :, :], bank[2 + n][:, 0:NPG * r].rearrange("p (q r) -> p q r", r=r), ACT.Copy)
                act.activation(PNW[:, n, :], bank[4 + n][0:DEC, 0:r], ACT.Copy).then_inc(S("s_ptev"), 1)
            for n in range(KVH):
                act.wait_ge(S("s_pv"), n + 1)
                act.activation(OT[:, n * GRP:(n + 1) * GRP, SEQ:TOK],
                               bank[6 + n][:, 0:DEC * GRP].rearrange("p (b g) -> p g b", g=GRP), ACT.Copy)\
                    .then_inc(S("s_ot"), 1)
            act.wait_ge(S("hn"), 3 * TILES)
            closing(2)
            roots(2)
            experts(1)
            for t in range(TILES):
                act.wait_ge(S("x_rdy"), 3 * TILES + t + 1)
                dst = O["y_prompt"][0, t * P:(t + 1) * P, :] if t < NT else O["y_sample"].rearrange("b t d -> (b t) d")
                act.dma_start(dst, X[0:rows(t), t, :]).then_inc(S("y_out"), 16)

        @block.gpsimd
        def _(pool):
            for j in range(2):
                pool.engine_nop().then_inc(S(f"slots_used{j}"), 1)
            nc.gpsimd.memset(zero_i[:, :], 0).then_inc(S("zeros"), 1)
            zero_f = HT[:, 0:2, :].rearrange("p k t -> p (k t)")[:, 0:D]
            nc.gpsimd.memset(zero_f, 0.0).then_inc(S("zeros"), 1)
            pool.wait_ge(S("zeros"), 2)
            pool.dma_start(y_d.rearrange("(i p) d -> p i d", p=P),
                           zero_f.rearrange("p (o d) -> p o d", o=1).to_broadcast([P, ITEMS, D])).then_inc(S("y_zero"), 16)
            pool.dma_start(slot_d.rearrange("(p i) o -> p (i o)", p=P), zero_i[:, :]).then_inc(S("slot_zero"), 16)
            for hp in range(2):
                for hh in range(2):
                    h = 2 * hp + hh
                    pool.wait_ge(S("s_rdy"), (h + 1) * NT)
                    pool.dma_start(O["ret_prompt"][0, 0, h].rearrange("(j p) v -> p j v", p=P), STATE[:, hh, :, :])\
                        .then_inc(S("rp_st"), 16)
                for b in range(DEC):
                    n = 2 * DEC * hp + 2 * b + 2
                    pool.wait_ge(S("st_upd"), n)
                    pool.dma_start(O["ret_sample"][0, b, 2 * hp:2 * hp + 2].rearrange("h (j p) v -> p (h j) v", p=P),
                                   slot(("state", hp, b // 2))[:, 4 * (b % 2):4 * (b % 2) + 4, :])\
                        .then_inc(S(f"state_st{place[('state', hp, b // 2)][1]}"), 16)

            def experts(l):
                m = 2 * l + 1
                for t in range(TILES):
                    pool.wait_ge(S("hn"), TILES * m + t + 1)
                    pool.dma_start(h_d[cols(t), :], HN[t % 2][0:rows(t), :]).then_inc(S(f"h_st{t % 2}"), 16)
                pool.wait_ge(S("slot_zero"), 16)
                pool.wait_ge(S(f"tables{l}"), 1)
                for k in range(2):
                    for t in range(TILES):
                        R = rows(t)
                        pool.indirect_dma_start(out=slot_d, out_offset=bass.IndirectOffsetOnAxis(ap=dest_i[0:R, k, t:t + 1], axis=0),
                                                in_=tok[0:R, t:t + 1], in_offset=None).then_inc(S(f"scattered{l}"), 16)
                for par in range(2):
                    pool.wait_ge(S(f"h_st{par}"), 16 * (l + 1) * tiles_of[par])
                first, count = pairs(pool, l)
                with pool.Fori(0, count) as k:
                    i = first + k
                    for j in range(2):
                        pool.wait_ge(S(f"slots_in{j}"), (i + 1) * 16)
                        pool.wait_ge(S(f"hg_ps{j}"), 2 * i + 2)
                        nc.gpsimd.tensor_tensor(slot_c[:, j:j + 1], slot_i[:, j:j + 1], zero_i[:, 0:1], ALU.add)\
                            .then_inc(S(f"slots_used{j}"), 1)
                        pool.drain()
                        pool.indirect_dma_start(out=HG[j], out_offset=None, in_=h_d,
                                                in_offset=bass.IndirectOffsetOnAxis(ap=slot_c[:, j:j + 1], axis=0))\
                            .then_inc(S(f"rows_in{j}"), 16)
                for j in range(2):
                    pool.wait_ge(S(f"y_st{j}"), (first + count + 1) * 16)
                nc.gpsimd.tensor_tensor(dest_c[:, :, :], dest_i[:, :, :],
                                        zero_i[:, 0:2 * TILES].rearrange("p (k t) -> p k t", k=2), ALU.add)
                pool.drain()
                for t in range(TILES):
                    R = rows(t)
                    if t >= 2:
                        pool.wait_ge(S(f"cmb{l}"), t - 1)
                    for k in range(2):
                        pool.indirect_dma_start(out=YG[t % 2][k][0:R, :], out_offset=None, in_=y_d,
                                                in_offset=bass.IndirectOffsetOnAxis(ap=dest_c[0:R, k, t:t + 1], axis=0))\
                            .then_inc(S(f"yg_in{t % 2}"), 16)

            experts(0)
            for t in range(TILES):
                R = rows(t)
                pool.wait_ge(S("d_rot"), 2 * TILES + t + 1)
                for src, name in ((KV[0:R, t, 0:KVH * HD], "k"), (KV[0:R, t, KVH * HD:], "v")):
                    dst = O[name + "_prompt"][0, 0, cols(t)] if t < NT else O[name + "_sample"][0, :, 0]
                    pool.dma_start(dst.rearrange("t h d -> t (h d)"), src).then_inc(S("kv_st"), 16)
            for t in range(TILES):
                R = rows(t)
                pool.wait_ge(S("d_rot"), 5 * TILES + t + 1)
                dst = O["kidx_prompt"][0, 0, cols(t)] if t < NT else O["kidx_sample"][0, :, 0]
                pool.dma_start(dst, KIW[0:R, t, 0:ID]).then_inc(S("kv_st"), 16)
            experts(1)

        @block.vector
        def _(dve):
            TS, TT, STT = dve.tensor_scalar, dve.tensor_tensor, dve.scalar_tensor_tensor

            def modulated(m):
                dve.wait_ge(S("bc_in"), 64 * m + 64)
                for t in range(TILES):
                    R = rows(t)
                    sc_, sh = (BC[:, 0, :], BC[:, 1, :]) if t < NT else (SC[:, 0, :], SC[:, 1, :])
                    if t >= 2:
                        dve.wait_ge(S("ht_ps"), 2 * TILES * m + 2 * (t - 1))
                        if m % 2:
                            dve.wait_ge(S(f"h_st{t % 2}"), 16 * ((m // 2) * tiles_of[t % 2] + t // 2))
                    TT(HN[t % 2][0:R, :], X[0:R, t, :], sc_, ALU.mult)
                    dve.drain()
                    TT(HN[t % 2][0:R, :], HN[t % 2][0:R, :], sh, ALU.add).then_inc(S("hn"), 1)

            def norm(m):
                dve.drain()
                for t in range(TILES):
                    for g in range(2):
                        dve.bn_stats(lnst[0:rows(t), t, g, :], X[0:rows(t), t, g * NB:(g + 1) * NB])
                dve.drain()
                for t in range(TILES):
                    last = dve.bn_aggr(lnmv[0:rows(t), t, :], lnst[0:rows(t), t, :, :])
                last.then_inc(S("ln_var"), 1)
                dve.wait_ge(S("ln_sd"), 1 * m + 1)
                dve.reciprocal(lnrs[:, :], lnsd[:, :])
                dve.drain()
                for t in range(TILES):
                    R = rows(t)
                    TS(X[0:R, t, :], X[0:R, t, :], lnmv[0:R, t, 0:1], lnrs[0:R, t:t + 1], ALU.subtract, ALU.mult)
                dve.drain()
                for t in range(TILES):
                    TT(X[0:rows(t), t, :], X[0:rows(t), t, :], BC[0:rows(t), 1, :], ALU.mult)
                dve.drain()
                for t in range(TILES):
                    TT(X[0:rows(t), t, :], X[0:rows(t), t, :], BC[0:rows(t), 2, :], ALU.add).then_inc(S("x_rdy"), 1)
                dve.drain()

            def mixer_close(m):
                T = EPT[m]
                dve.wait_ge(S("ep_in"), 64 * m + 64)
                for n in range(2):
                    for t in range(TILES):
                        R = rows(t)
                        gt = (BC if t < NT else SC)[0:R, 0, n * NB:(n + 1) * NB]
                        dve.wait_ge(S(f"out_mm{m}"), TILES * n + t + 1)
                        TT(T[0:R, :], bank[(TILES * n + t) % 8][0:R, :], gt, ALU.mult).then_inc(S(f"out_ev{m}"), 1)
                        dve.drain()
                        xx = X[0:R, t, n * NB:(n + 1) * NB]
                        STT(xx, xx, ALPHA, T[0:R, :], ALU.mult, ALU.add)
                        dve.drain()
                norm(m)

            for j in range(2):
                for name in ("a_rdy", "y_ev_d"):
                    dve.engine_nop().then_inc(S(f"{name}{j}"), 1)
            dve.memset(gnmv[:, :, :, :], 1.0)
            dve.memset(lnmv[:, :, :], 1.0)
            dve.memset(gates[:, :, :], 0.0)
            dve.memset(qmask[:, :, :, :], 0.0)
            dve.memset(QM[:, :, :, :], 0.0)
            dve.memset(WM[:, :, :, :], 0.0)
            dve.wait_ge(S("const_in"), 16 * N_CONST)
            dve.tensor_copy(bf_cum[:, 0, :], C("cum"))
            dve.tensor_copy(bf_cum[:, 1, :], C("ones"))
            dve.drain()
            dve.wait_ge(S("c_ps"), 1)
            dve.tensor_copy(CT, bank[2][:, 0:KD * (DEC + 1)].rearrange("p (k r) -> p k r", k=KD)).then_inc(S("c_t"), 1)
            dve.wait_ge(S("bmod_in"), 16)
            for l in range(DEPTH):
                for n in range(12):
                    u = 12 * l + n
                    dve.wait_ge(S("mod_mm"), u + 1)
                    if l and n == 0:
                        dve.wait_ge(S("mod_st"), 16)
                    one = 1.0 if n in (2, 3, 8, 9) else 0.0
                    STT(MODV[:, n * NB:(n + 1) * NB], bank[u % 2][0:DEC + 1, :], one, BMOD[:, l, n * NB:(n + 1) * NB],
                        ALU.add, ALU.add).then_inc(S("mod_ev"), 1)

            dve.wait_ge(S("x_in"), 32)
            modulated(0)
            si = 0
            for hp in range(2):
                for i in range(2 * TILES):
                    g = hp * 2 * TILES + i
                    isk, t = divmod(i, TILES)
                    R = rows(t)
                    dve.wait_ge(S("ret_ev"), hp * 6 * TILES + i + 1)
                    if g:
                        dve.wait_ge(S("qk_ps"), g)
                    dst = KN[:, t, :] if isk and t < NT else RO
                    x4 = RT[0:R, :].rearrange("p (a d) -> p a d", d=P)
                    x2 = RT[0:R, :].rearrange("p (h a d) -> p h a d", a=2, d=P)
                    d2 = dst[0:R, :].rearrange("p (h a d) -> p h a d", a=2, d=P)
                    t2 = T1[0:R, :].rearrange("p (h a d) -> p h a d", a=2, d=P)
                    cc = rotc[0:R, 0:1, t, :]
                    ss = rotc[0:R, 1:2, t, :].to_broadcast([R, 2, P])
                    TT(T1[0:R, :].rearrange("p (a d) -> p a d", d=P), x4, cc.to_broadcast([R, 4, P]), ALU.mult)
                    TT(d2[:, :, 0, :], x2[:, :, 1, :], ss, ALU.mult)
                    TT(d2[:, :, 1, :], x2[:, :, 0, :], ss, ALU.mult)
                    dve.drain()
                    TT(d2[:, :, 0, :], t2[:, :, 0, :], d2[:, :, 0, :], ALU.subtract)
                    TT(d2[:, :, 1, :], t2[:, :, 1, :], d2[:, :, 1, :], ALU.add).then_inc(S("ro_rdy"), 1)
                    dve.drain()

                def decay_att(i):
                    rc = hp * 2 * NT + i
                    h = 2 * hp + i // NT
                    dve.wait_ge(S("att_ps"), rc + 1)
                    if rc >= 2:
                        dve.wait_ge(S("o_ps"), rc - 1)
                    STT(att[:, rc % 2, :], bank[3 + rc % 2][:, 0:P], float(GAMMA[h] ** -CH), C("tri"), ALU.mult, ALU.mult)\
                        .then_inc(S("att_rdy"), 1)

                decay_att(0)
                for i in range(2 * NT):
                    hh, c = divmod(i, NT)
                    rc = hp * 2 * NT + i
                    if i + 1 < 2 * NT:
                        decay_att(i + 1)
                    dve.wait_ge(S("u_ps"), rc + 1)
                    if c == 0 and hp:
                        dve.wait_ge(S("rp_st"), 32)
                    for j in range(2):
                        st = STATE[:, hh, j, :]
                        if c == 0:
                            last = dve.tensor_copy(st, bank[6 + j][:, :])
                        else:
                            last = STT(st, st, float(GAMMA[2 * hp + hh] ** CH), bank[6 + j][:, :], ALU.mult, ALU.add)
                    last.then_inc(S("s_rdy"), 1)
                    dve.drain()
                for b in range(DEC):
                    dve.tensor_copy(qmask[:, b, :, b], QT[:, :, SEQ + b])
                dve.drain()
                dve.engine_nop().then_inc(S("qm_rdy"), 1)
                for i in range(2 * DEC):
                    si = 2 * DEC * hp + i
                    b, hh = divmod(i, 2)
                    dve.wait_ge(S("vb_ps"), si + 1)
                    dve.wait_ge(S("st_dec"), si + 1)
                    st = slot(("state", hp, b // 2))
                    for j in range(2):
                        sj = st[:, 4 * (b % 2) + 2 * hh + j, :]
                        last = STT(sj, bank[2 + si % 2][:, :], KT[:, 2 * hh + j, SEQ + b:SEQ + b + 1], sj, ALU.mult, ALU.add)
                    last.then_inc(S("st_upd"), 1)
                dve.wait_ge(S("o_ev"), 2 * NT * (hp + 1))
                dve.wait_ge(S("os_ev"), 2 * (hp + 1))
                for hh in range(2):
                    for t in range(TILES):
                        R = rows(t)
                        dve.bn_stats(gnst[0:R, t, :], V[0:R, t, hh * NB:(hh + 1) * NB])
                    dve.drain()
                    for t in range(TILES):
                        last = dve.bn_aggr(gnmv[0:rows(t), hh, t, :], gnst[0:rows(t), t, :])
                    dve.drain()
                dve.engine_nop().then_inc(S("gn_var"), 1)
                dve.wait_ge(S("gn_sd"), hp + 1)
                dve.reciprocal(gnrs[:, :, :], gnsd[:, :, :])
                dve.drain()
                dve.wait_ge(S("gn_in"), 16 * (hp + 1))
                for i in range(2 * TILES):
                    hh, t = divmod(i, TILES)
                    R = rows(t)
                    vv = V[0:R, t, hh * NB:(hh + 1) * NB]
                    TS(vv, vv, gnmv[0:R, hh, t, 0:1], gnrs[0:R, hh, t:t + 1], ALU.subtract, ALU.mult)
                    dve.drain()
                    TT(vv, vv, GNB[0:R, hh * NB:(hh + 1) * NB], ALU.mult)
                    dve.drain()
                    dve.wait_ge(S("ret_ev"), hp * 6 * TILES + 4 * TILES + i + 1)
                    TT(vv, vv, SG[i % 2][0:R, :], ALU.mult).then_inc(S("y_rdy"), 1)
            mixer_close(0)

            def route(l):
                D_ = dve.drain
                dve.memset(LG, 0.0)
                D_()
                dve.wait_ge(S(f"lg_mm{l}"), TILES)
                pl = bank[0][:, 0:TILES * NE].rearrange("p (t e) -> p t e", e=NE)
                b4 = br[:, :].rearrange("p (o e) -> p o e", o=1)
                TT(LG[:, 0:NT, :], pl[:, 0:NT, :], b4.to_broadcast([P, NT, NE]), ALU.add)
                TT(LG[0:DEC, NT, :], pl[0:DEC, NT, :], br[0:DEC, :], ALU.add)
                D_()
                sp3 = lambda v: v.rearrange("p (t o) -> p t o", o=1).to_broadcast([P, TILES, NE])
                dve.tensor_reduce(r1, LG, AX.X, ALU.max)
                D_()
                TT(LG, LG, sp3(r1), ALU.subtract).then_inc(S(f"lg_sub{l}"), 1)
                dve.wait_ge(S(f"lg_exp{l}"), 1)
                dve.tensor_reduce(r1, PR, AX.X, ALU.add)
                D_()
                dve.reciprocal(r2, r1)
                D_()
                TT(PR, PR, sp3(r2), ALU.mult)
                D_()
                g4 = PR.rearrange("p t (g e) -> p (t g) e", e=EPG)
                for at, d_ in ((0, 1), (3, 2), (5, 3)):
                    TT(PAIRS[:, :, at:at + EPG - d_], g4[:, :, 0:EPG - d_], g4[:, :, d_:EPG], ALU.add)
                D_()
                dve.tensor_reduce(GS.rearrange("p t g -> p (t g)"), PAIRS, AX.X, ALU.max)
                D_()
                dve.tensor_reduce(r1, GS, AX.X, ALU.max)
                D_()
                sg = lambda v: v.rearrange("p (t o) -> p t o", o=1).to_broadcast([P, TILES, NG])
                TT(GQ, GS, sg(r1), ALU.is_equal)
                D_()
                TT(GK, GQ, C("w4").rearrange("p (o g) -> p o g", o=1).to_broadcast([P, TILES, NG]), ALU.mult)
                D_()
                dve.tensor_reduce(r1, GK, AX.X, ALU.max)
                D_()
                TT(GQ, GK, sg(r1), ALU.is_equal)
                D_()
                gq = GQ.rearrange("p t (g o) -> p (t g) o", o=1).to_broadcast([P, TILES * NG, EPG])
                pm = PM.rearrange("p t (g e) -> p (t g) e", e=EPG)
                TT(pm, g4, gq, ALU.mult)
                D_()
                TT(pm, pm, gq, ALU.add)
                D_()
                TS(PM, PM, -1.0, None, ALU.add)
                D_()
                w16 = C("w16").rearrange("p (o e) -> p o e", o=1).to_broadcast([P, TILES, NE])
                for k, (Sk, rk) in enumerate(((S1, r3), (S2, r4))):
                    dve.tensor_reduce(rk, PM, AX.X, ALU.max)
                    D_()
                    TT(EQ, PM, sp3(rk), ALU.is_equal)
                    D_()
                    TT(KEY, EQ, w16, ALU.mult)
                    D_()
                    dve.tensor_reduce(r1, KEY, AX.X, ALU.max)
                    D_()
                    TT(Sk, KEY, sp3(r1), ALU.is_equal)
                    D_()
                    if k == 0:
                        STT(PM.rearrange("p t e -> p (t e)"), Sk.rearrange("p t e -> p (t e)"), -4.0,
                            PM.rearrange("p t e -> p (t e)"), ALU.mult, ALU.add)
                        D_()
                for Sk, rk in ((S1, r3), (S2, r4)):
                    TT(EQ, PR, Sk, ALU.mult)
                    D_()
                    dve.tensor_reduce(rk, EQ, AX.X, ALU.add)
                    D_()
                TT(r1, r3, r4, ALU.add)
                D_()
                dve.reciprocal(r2, r1)
                D_()
                TT(gates[:, 0, :], r3, r2, ALU.mult)
                TT(gates[:, 1, :], r4, r2, ALU.mult)
                va = C("valid").rearrange("p (t o) -> p t o", o=1).to_broadcast([P, TILES, NE])
                TT(EQ, S1, S2, ALU.add)
                D_()
                TT(mb[:, :, :], EQ, va, ALU.mult).then_inc(S(f"marks{l}"), 1)
                dve.wait_ge(S(f"rank_mm{l}"), 1)
                rk = bank[1][:, 0:(TILES + 1) * NE].rearrange("p (t e) -> p t e", e=NE)
                dve.tensor_copy(cntv, rk[:, TILES, :])
                D_()
                blk = C("blk").rearrange("p (o j) -> p o j", o=1).to_broadcast([P, NE, MAXB])
                bg = big.rearrange("p i e -> p (i e)")[:, 0:NE * MAXB].rearrange("p (e j) -> p e j", j=MAXB)
                TT(bg, cntv.rearrange("p (e o) -> p e o", o=1).to_broadcast([P, NE, MAXB]), blk, ALU.is_gt)
                D_()
                dve.tensor_reduce(nbk, bg, AX.X, ALU.add)
                D_()
                dve.tensor_tensor_scan(cum, C("ones")[:, 0:NE], nbk, 0.0, ALU.mult, ALU.add)
                D_()
                TT(sta, cum, nbk, ALU.subtract)
                D_()
                TS(sta, sta, float(P), None, ALU.mult)
                D_()
                TT(DST, rk[:, 0:TILES, :], sta.rearrange("p (o e) -> p o e", o=1).to_broadcast([P, TILES, NE]), ALU.add)
                D_()
                for k, Sk in enumerate((S1, S2)):
                    TT(EQ, DST, Sk, ALU.mult)
                    D_()
                    dve.tensor_reduce(r1, EQ, AX.X, ALU.add)
                    D_()
                    dve.tensor_copy(dest_i[:, k, :], r1)
                    D_()
                TT(big, C("item").rearrange("p (i o) -> p i o", o=1).to_broadcast([P, ITEMS, NE]),
                   cum.rearrange("p (o e) -> p o e", o=1).to_broadcast([P, ITEMS, NE]), ALU.is_ge)
                D_()
                dve.tensor_reduce(itf, big, AX.X, ALU.add)
                D_()
                TS(itf, itf, float(NE - 1), None, ALU.min)
                D_()
                dve.tensor_copy(eid_i[:, :], itf)
                TT(big.rearrange("p i e -> p (i e)")[:, 0:ITEMS // 2], C("pair"),
                   cum[:, NE - 1:NE].to_broadcast([P, ITEMS // 2]), ALU.is_lt)
                D_()
                dve.tensor_reduce(r1[:, 0:1], big.rearrange("p i e -> p (i e)")[:, 0:ITEMS // 2], AX.X, ALU.add)
                D_()
                dve.tensor_copy(np_i[:, l:l + 1], r1[:, 0:1])
                D_()
                dve.engine_nop().then_inc(S(f"tables{l}"), 1)

            def experts(l):
                m = 2 * l + 1
                modulated(m)
                route(l)
                first, count = pairs(dve, l)
                with dve.Fori(0, count) as k:
                    i = first + k
                    def act_times_up(j):
                        dve.wait_ge(S(f"sg{j}"), i + 1)
                        dve.wait_ge(S(f"pe_w_up{j}"), i + 2)
                        dve.wait_ge(S(f"at_ps{j}"), i + 1)
                        TT(AE[j], SGE[j], bank[5 + 2 * j][:, :], ALU.mult).then_inc(S(f"a_rdy{j}"), 1)

                    def take_y(j):
                        dve.wait_ge(S(f"y_mm{j}"), i + 1)
                        dve.wait_ge(S(f"y_st{j}"), (i + 1) * 16)
                        dve.tensor_copy(Y[j][:, 0:NB], bank[(1, 4)[j]][:, :]).then_inc(S(f"y_ev_d{j}"), 1)

                    act_times_up(0)
                    act_times_up(1)
                    take_y(0)
                    take_y(1)
                dve.wait_ge(S("ep_in"), 64 * m + 64)
                for t in range(TILES):
                    R = rows(t)
                    y1, y2 = (YG[t % 2][k][0:R, :] for k in range(2))
                    gt = (BC if t < NT else SC)[0:R, 0, :]
                    dve.wait_ge(S(f"yg_in{t % 2}"), 32 * (l * tiles_of[t % 2] + t // 2 + 1))
                    TS(y1, y1, gates[0:R, 0, t:t + 1], None, ALU.mult)
                    dve.drain()
                    STT(y1, y2, gates[0:R, 1, t:t + 1], y1, ALU.mult, ALU.add)
                    dve.drain()
                    TT(y1, y1, gt, ALU.mult)
                    dve.drain()
                    STT(X[0:R, t, :], X[0:R, t, :], ALPHA, y1, ALU.mult, ALU.add).then_inc(S(f"cmb{l}"), 1)
                norm(m)

            experts(0)

            modulated(2)
            for i in range(6 * TILES):
                n, t = divmod(i, TILES)
                R = rows(t)
                dve.wait_ge(S("d_ev"), i + 1)
                nh, w, rot, src, cn, sn = ((4, HD, ROT, DRT[i % 2], "dcos", "dsin"), (4, HD, ROT, DRT[i % 2], "dcos", "dsin"),
                                           (KVH, HD, ROT, KV[:, t, :], "dcos", "dsin"),
                                           (8, ID, IROT, DRT[i % 2], "icos", "isin"), (8, ID, IROT, DRT[i % 2], "icos", "isin"),
                                           (1, ID, IROT, KIW[:, t, :], "icos", "isin"))[n]
                hf = rot // 2
                xv = src[0:R, 0:nh * w].rearrange("p (h d) -> p h d", d=w)
                x1, x2 = xv[:, :, 0:hf], xv[:, :, hf:rot]
                tb = lambda nm: C(nm)[0:R, t * hf:(t + 1) * hf].rearrange("p (o d) -> p o d", o=1).to_broadcast([R, nh, hf])
                rx = [RX[0:R, k, 0:nh * hf].rearrange("p (h d) -> p h d", d=hf) for k in range(4)]
                TT(rx[0], x1, tb(cn), ALU.mult)
                TT(rx[1], x2, tb(sn), ALU.mult)
                TT(rx[2], x1, tb(sn), ALU.mult)
                TT(rx[3], x2, tb(cn), ALU.mult)
                dve.drain()
                TT(x1, rx[0], rx[1], ALU.subtract)
                last = TT(x2, rx[2], rx[3], ALU.add)
                if n == 5:
                    dve.drain()
                    for c in range(2):
                        dve.tensor_copy(KID[0:R, t, c * ID:(c + 1) * ID], KIW[0:R, t, 0:ID])
                    last = TS(WI[0:R, t, :], KIW[0:R, t, ID:ID + IH], IH ** -0.5, None, ALU.mult)
                last.then_inc(S("d_rot"), 1)
                dve.drain()
            ix = 0
            for t in range(NT):
                L = (t + 1) * P
                if t == 0:
                    dve.tensor_copy(BIAS[:, 0:P], C("cbias"))
                else:
                    for h in range(IH):
                        dve.wait_ge(S("ix_rl"), ix + 1)
                        if h == 0:
                            TS(SCORE[:, 0:L], RL[ix % 2][:, 0:L], WI[:, t, 0:1], None, ALU.mult).then_inc(S("ix_acc"), 1)
                        else:
                            STT(SCORE[:, 0:L], RL[ix % 2][:, 0:L], WI[:, t, h:h + 1], SCORE[:, 0:L], ALU.mult, ALU.add)\
                                .then_inc(S("ix_acc"), 1)
                        dve.drain()
                        ix += 1
                    TT(SCORE[:, t * P:L], SCORE[:, t * P:L], C("cbias"), ALU.add)
                    dve.drain()
                    for r in range(TOPK_P // 8):
                        dve.max(m8[:, :], SCORE[:, 0:L])
                        dve.drain()
                        dve.match_replace(out=SCORE[:, 0:L], in_to_replace=m8[:, :], in_values=SCORE[:, 0:L], imm_value=GONE)
                        dve.drain()
                    TS(BIAS[:, 0:L], SCORE[:, 0:L], -2.0e38, NEG, ALU.is_gt, ALU.mult)
                dve.drain()

                def normed(h):
                    a = t * QH + h
                    dve.wait_ge(S("e_rdy"), a + 1)
                    dve.reciprocal(ersum[:, a % 2:a % 2 + 1], esum[:, a % 2:a % 2 + 1])
                    dve.drain()
                    TS(E[a % 2][:, 0:L], E[a % 2][:, 0:L], ersum[:, a % 2:a % 2 + 1], None, ALU.mult).then_inc(S("p_rdy"), 1)

                for s in range(QH + 1):
                    if s < QH:
                        a = t * QH + s
                        dve.wait_ge(S("lg_ps"), a + 1)
                        if a >= 2:
                            dve.wait_ge(S("pt_ps"), a - 1)
                        dve.tensor_tensor_reduce(out=E[a % 2][:, 0:L], in0=bank[2 + a % 2][:, 0:L], in1=BIAS[:, 0:L],
                                                 scale=1.0, scalar=GONE, op0=ALU.add, op1=ALU.max,
                                                 accum_out=mx[:, a % 2:a % 2 + 1]).then_inc(S("lg_ev"), 1)
                        dve.drain()
                        TS(nbias[:, a % 2:a % 2 + 1], mx[:, a % 2:a % 2 + 1], -(HD ** -0.5), None, ALU.mult)\
                            .then_inc(S("nb_rdy"), 1)
                    if s:
                        normed(s - 1)
            dve.wait_ge(S("ot_ev"), NT * QH)
            dve.wait_ge(S("w_t"), 1)
            for b in range(DEC):
                dve.tensor_copy(WM[:, :, b, b], bank[0][0:DEC, 0:2 * DEC].rearrange("p (c b) -> p c b", c=2)[:, :, b])
                for n in range(KVH):
                    dve.tensor_copy(QM[:, b, n, b * GRP:(b + 1) * GRP], DQT[:, n * GRP:(n + 1) * GRP, SEQ + b])
            dve.drain()
            dve.engine_nop().then_inc(S("wm_rdy"), 1)
            for b in range(DEC):
                if b >= 2:
                    dve.wait_ge(S("s_dot"), b - 1)
                dve.tensor_copy(KIBT[b % 2][:, PAST:LS], KIT[:, SEQ + b:SEQ + b + 1]).then_inc(S("ki_rdy"), 1)
                last = dve.tensor_copy(KBT[:, b, :, PAST], DKT[:, :, SEQ + b])
            last.then_inc(S("kn_rdy"), 1)
            dve.wait_ge(S("s_sc"), DEC)
            dve.tensor_copy(SCS, bank[6][0:DEC, 0:LS])
            dve.drain()
            for r in range(TOPK_S // 8):
                dve.max(m8[0:DEC, :], SCS)
                dve.drain()
                dve.match_replace(out=SCS, in_to_replace=m8[0:DEC, :], in_values=SCS, imm_value=GONE)
                dve.drain()
            TS(BIS, SCS, -2.0e38, NEG, ALU.is_gt, ALU.mult).then_inc(S("s_bias"), 1)
            r = DEC * GRP
            for n in range(KVH):
                dve.wait_ge(S("s_lg"), n + 1)
                dve.tensor_copy(PS[n][:, :], bank[n][0:r, 0:LS])
                dve.drain()
                dve.tensor_reduce(mx[0:r, n:n + 1], PS[n][:, :], AX.X, ALU.max)
                dve.drain()
                TS(nbias[0:r, n:n + 1], mx[0:r, n:n + 1], -(HD ** -0.5), None, ALU.mult).then_inc(S("s_nb"), 1)
            for n in range(KVH):
                dve.wait_ge(S("s_e"), n + 1)
                dve.reciprocal(ersum[0:r, n:n + 1], esum[0:r, n:n + 1])
                dve.drain()
                TS(PS[n][:, :], PS[n][:, :], ersum[0:r, n:n + 1], None, ALU.mult)
                dve.drain()
                TS(DG[:, n, :], ident[0:r, 0:r], PS[n][:, PAST:LS], None, ALU.mult).then_inc(S("s_p"), 1)
            mixer_close(2)
            experts(1)


_OUTS = [("y_prompt", (1, SEQ, D)), ("y_sample", (DEC, 1, D)), ("ret_prompt", (1, 1, RH, RDK, RDV)),
         ("ret_sample", (1, DEC, RH, RDK, RDV)), ("k_prompt", (1, 1, SEQ, KVH, HD)), ("v_prompt", (1, 1, SEQ, KVH, HD)),
         ("kidx_prompt", (1, 1, SEQ, ID)), ("k_sample", (1, DEC, 1, KVH, HD)), ("v_sample", (1, DEC, 1, KVH, HD)),
         ("kidx_sample", (1, DEC, 1, ID))]


def kernel(**inputs):
    import concourse.bacc as _bacc
    from concourse.bass_utils import run_bass_kernel_spmd as _run

    nc = _bacc.Bacc("TRN2", target_bir_lowering=False, num_devices=1)
    cst, rotc, tok = constants()
    arrays, args = {}, {}
    for name, a in list(inputs.items()) + [("cst", cst), ("rotc", rotc), ("tok", tok)]:
        a = np.ascontiguousarray(a)
        arrays["in_" + name] = a
        args[name] = nc.dram_tensor("in_" + name, a.shape, mybir.dt.from_np(a.dtype), kind="ExternalInput").ap()
    outs = {name: nc.dram_tensor("out_" + name, shape, F32, kind="ExternalOutput").ap() for name, shape in _OUTS}
    trunk(nc, args, outs)
    r = _run(nc, [arrays], core_ids=[0])
    return tuple(r.results[0]["out_" + name] for name, _ in _OUTS)
```

```python
import math
from contextlib import ExitStack

import numpy as np

import concourse.bass as bass
from concourse import mybir

F32 = mybir.dt.float32
BF16 = mybir.dt.bfloat16
I32 = mybir.dt.int32
F32R = mybir.dt.float32r
ALU = mybir.AluOpType
ACT = mybir.ActivationFunctionType
AX = mybir.AxisListType

P = 128
D = 1024
KD = D // P
SEQ, DEC = 512, 8
NT = SEQ // P
TOK = SEQ + DEC
TILES = NT + 1
DEPTH = 2
ALPHA = (2.0 * DEPTH) ** 0.25
LN_EPS, GN_EPS = 1e-5, 1e-6
NB = 512

RH, RDK, RDV = 4, 256, 512
CH = 128
GAMMA = [1.0 - 2.0 ** (-5.0 - h) for h in range(RH)]

QH, KVH, HD = 8, 2, 128
GRP = QH // KVH
IH, ID = 16, 64
DSA_IN = QH * HD + 2 * KVH * HD + IH * ID + ID + IH
TOPK_P = min(256, SEQ // 4)
PAST, PAGE = 256, 128
NPG = PAST // PAGE
TOPK_S = min(256, (PAST + 1) // 4)
LS = PAST + 1
ROT, IROT = HD // 4, ID // 4
NEG = -1.0e30
GONE = -3.0e38

NE, NG, EPG = 16, 4, 4
FE = 512
MAXB = -(-TOK // P)
ITEMS = 24
assert ITEMS >= NE + (2 * TOK) // P and ITEMS % 2 == 0

N_CONST = 4

_cols = {}
_at = 0
for _n, _w in (("ident", P), ("tri", P), ("cum", P), ("ones", P), ("cbias", P), ("qs", TILES * RH),
               ("ks", TILES * RH), ("item", ITEMS - NE + 2), ("blk", MAXB), ("pair", ITEMS // 2), ("w4", NG),
               ("w16", NE), ("e", NE), ("valid", TILES), ("dcos", TILES * ROT // 2), ("dsin", TILES * ROT // 2),
               ("icos", TILES * IROT // 2), ("isin", TILES * IROT // 2), ("bexp", DEC * GRP),
               ("bsel", DEC), ("lneps", 1), ("gneps", 1)):
    _cols[_n] = (_at, _w)
    _at += _w
CST_W = _at


def constants():
    f = np.float32
    cst = np.zeros((P, CST_W), f)

    def put(name, a):
        o, w = _cols[name]
        cst[:a.shape[0], o:o + w] = a.reshape(a.shape[0], w)

    i = np.arange(P)
    put("ident", np.eye(P, dtype=f))
    put("tri", (i[None, :] >= i[:, None]).astype(f))
    put("cum", (i[:, None] < i[None, :]).astype(f))
    put("ones", np.ones((P, P), f))
    put("cbias", np.where(i[None, :] <= i[:, None], 0.0, NEG).astype(f))
    lg = np.log(f(1.0) - np.power(f(2.0), f(-5.0) - np.arange(RH, dtype=f))).astype(f)
    qs = np.ones((P, TILES, RH), f)
    ks = np.full((P, TILES, RH), RDK ** -0.5, f)
    qs[:, :NT] = np.exp(lg[None, :] * (i[:, None] + 1.0).astype(f))[:, None]
    ks[:, :NT] = (np.exp(lg[None, :] * (CH - 1.0 - i)[:, None].astype(f)) * f(RDK ** -0.5))[:, None]
    put("qs", qs)
    put("ks", ks)
    row = lambda v: np.tile(np.asarray(v, f)[None, :], (P, 1))
    put("item", row(np.arange(ITEMS - NE + 2)))
    put("blk", row(np.arange(MAXB) * P))
    put("pair", row(2 * np.arange(ITEMS // 2)))
    put("w4", row(NG - np.arange(NG)))
    put("w16", row(NE - np.arange(NE)))
    put("e", row(np.arange(NE)))
    valid = np.ones((P, TILES), f)
    valid[DEC:, NT] = 0
    put("valid", valid)
    pos = np.zeros((P, TILES), f)
    pos[:, :NT] = (np.arange(NT) * P)[None, :] + i[:, None]
    pos[:, NT] = PAST

    def table(inv):
        ang = (pos[:, :, None] * inv.astype(f)[None, None, :]).astype(f)
        return np.cos(ang).astype(f), np.sin(ang).astype(f)

    theta = f(500000.0)
    for c, s, rot in (("dcos", "dsin", ROT), ("icos", "isin", IROT)):
        co, si = table(f(1.0) / (theta ** (np.arange(0, rot, 2, dtype=f) / f(rot))))
        put(c, co)
        put(s, si)
    bexp = np.zeros((DEC, DEC * GRP), f)
    for b in range(DEC):
        bexp[b, b * GRP:(b + 1) * GRP] = 1
    put("bexp", bexp)
    bsel = np.zeros((DEC * GRP, DEC), f)
    bsel[np.arange(DEC * GRP), np.arange(DEC * GRP) // GRP] = 1
    put("bsel", bsel)
    put("lneps", np.full((P, 1), LN_EPS, f))
    put("gneps", np.full((P, 1), GN_EPS, f))
    inv = np.power(f(10000.0), -np.linspace(0.0, 1.0, RDK // 2, dtype=f)).astype(f)
    rc, rs = table(inv)
    rot = np.stack([rc, rs], 1)
    tok = np.zeros((P, TILES), np.int32)
    tok[:, :] = (np.arange(TILES) * P)[None, :] + i[:, None]
    return cst, np.ascontiguousarray(rot), tok


def rows(t):
    return P if t < NT else DEC


def cols(t):
    return slice(t * P, t * P + rows(t))


def trunk(nc, A, O):
    ctx = ExitStack()
    with ctx:
        sems = {}

        def S(name):
            if name not in sems:
                sems[name] = ctx.enter_context(nc.semaphore(name))
            return sems[name]

        def sb(name, shape, dt=F32):
            return ctx.enter_context(nc.sbuf_tensor(name, shape, dt))

        def dram(name, shape, dt=F32):
            return nc.dram_tensor(name, shape, dt, kind="Internal").ap()

        bank = [ctx.enter_context(nc.psum_tensor(f"bank{i}", [P, NB], F32)) for i in range(8)]

        mod_d = dram("mod_d", (DEPTH, DEC + 1, 6 * D))
        h_d = dram("h_d", (TOK, D))
        slot_d = dram("slot_d", (P * ITEMS, 1), I32)
        y_d = dram("y_d", (P * ITEMS, D))
        y_items = y_d.rearrange("(p i) d -> p i d", i=ITEMS)

        X = sb("X", [P, TILES, D])
        HT_AT = nc.sbuf_base
        HT = sb("HT", [P, KD, TOK])
        RING = sb("RING", [P, 3, KD * NB])
        MWORDS = 21504
        M_AT = nc.sbuf_base
        M = sb("M", [P, MWORDS])
        BC = sb("BC", [P, 3, D])
        SC = sb("SC", [DEC, 2, D])
        cst = sb("cst", [P, CST_W])
        rotc = sb("rotc", [P, 2, TILES, P])
        tok = sb("tok", [P, TILES], I32)
        zero_i = sb("zero_i", [P, ITEMS], I32)
        bf_cum = sb("bf_cum", [P, 2, P], BF16)
        wr = sb("wr", [P, KD, NE])
        br = sb("br", [P, NE])
        lnst = sb("lnst", [P, TILES, 2, 6])
        lnmv = sb("lnmv", [P, TILES, 2])
        lnsd = sb("lnsd", [P, TILES])
        lnrs = sb("lnrs", [P, TILES])
        gates = sb("gates", [P, 2, TILES])
        dest_i = sb("dest_i", [P, 2, TILES], I32)
        eid_i = sb("eid_i", [P, ITEMS + 2], I32)
        np_i = sb("np_i", [P, DEPTH], I32)
        slot_i = sb("slot_i", [P, ITEMS], I32)
        slot_c = sb("slot_c", [P, 2], I32)
        dest_c = sb("dest_c", [P, 2, TILES], I32)
        primer = sb("primer", [P, 2], I32)
        ptab = sb("ptab", [1, DEC * NPG], I32)

        def C(name, r=P):
            o, w = _cols[name]
            return cst[0:r, o:o + w]

        def view(off, *shape, r=P, region=None):
            n = int(np.prod(shape))
            assert off + n <= MWORDS
            v = M[0:r, off:off + n]
            if len(shape) == 1:
                return v
            names = "abcd"[:len(shape)]
            return v.rearrange(f"p ({' '.join(names)}) -> p {' '.join(names)}",
                               **{k: s for k, s in zip(names[1:], shape[1:])})

        ident = C("ident")


        stream, state_uses = [], [0] * 3
        for n in range(12):
            stream.append((("mod", 0, n), [("mod_mm", n + 1)]))
        for hp in range(2):
            ret = lambda i: [("ret_mm", (6 * hp + i + 1) * TILES)]
            stream += [(("q", hp), ret(0)), (("k", hp), ret(1)), (("v", hp, 0), ret(2)), (("v", hp, 1), ret(3))]
            for b2 in range(4):
                n = 4 * hp + b2 + 1
                s = len(stream) % 3
                state_uses[s] += 1
                stream.append((("state", hp, b2), [("os_mm", 4 * n), (f"state_st{s}", 32 * state_uses[s])]))
            stream += [(("g", hp, 0), ret(4)), (("g", hp, 1), ret(5))]
        for n in range(2):
            stream.append((("out0", n, 0), [("out_half0", TILES * (n + 1))]))
            stream.append((("out0", n, 1), [("out_mm0", TILES * (n + 1))]))
        for n in range(12):
            stream.append((("mod", 1, n), [("mod_mm", 12 + n + 1)]))
        N_FIRST = len(stream)
        for n in range(6):
            stream.append((("din", n), [("d_mm", TILES * (n + 1))]))
        stream += [(("ipg",), [("ki_t", DEC)]), (("kpg",), [("kk_t", 2 * DEC)]), (("vpg",), [("s_pv", KVH)])]
        for n in range(2):
            stream.append((("out2", n, 0), [("out_mm2", TILES * (n + 1))]))
        N_LOADS = {"state": 2, "kpg": DEC * NPG, "vpg": DEC * NPG, "ipg": 2 * DEC * NPG}
        place, brought = {}, [0] * 3
        for i, (key, _) in enumerate(stream):
            brought[i % 3] += 16 * N_LOADS.get(key[0], 1)
            place[key] = (i, i % 3, brought[i % 3])

        def slot(key, k=KD, n=NB):
            return RING[:, place[key][1], 0:k * n].rearrange("p (k n) -> p k n", n=n)

        def wait_slot(eng, key):
            eng.wait_ge(S(f"ring_full{place[key][1]}"), place[key][2])

        tiles_of = [(TILES + 1) // 2, TILES // 2]

        UNITS = [(j, w, h) for j, w in ((0, "w_gate"), (0, "w_up"), (1, "w_gate"), (1, "w_up"), (0, "w_down"),
                                        (1, "w_down")) for h in range(2)]
        RAW, SPLIT = 6, 4
        UW = 4 * NB
        UNIT0 = 8

        CROW = view(0, D, r=DEC + 1)
        CSIL = view(D, D, r=DEC + 1)
        BMOD = view(2 * D, 6 * D, r=DEC + 1)
        MODV = view(8 * D, 6 * D, r=DEC + 1)
        CT = sb("CT", [P, KD, DEC + 1])
        BM1 = rotc[:, :, :, :].rearrange("p a t d -> p (a t d)")[0:DEC + 1, 0:NB]
        MS1 = rotc[:, :, :, :].rearrange("p a t d -> p (a t d)")[0:DEC + 1, NB:2 * NB]
        o = 0
        YT = view(o, 16, TOK)
        o += 16 * TOK
        QT = view(o, 4, TOK)
        KT = view(o + 4 * TOK, 4, TOK)
        o += 8 * TOK
        KN = view(o, NT, NB)
        o += NT * NB
        V = view(o, TILES, 2 * NB)
        o += TILES * 2 * NB
        RT, T1, RO = view(o, NB), view(o + NB, NB), view(o + 2 * NB, NB)
        SG = [RT, T1]
        GNB = BC[:, 0, :]
        STATE = BC[:, 1:3, :].rearrange("p h (j v) -> p h j v", j=2)
        ATT_AT = -(-nc.sbuf_base // 32) * 32
        att = sb("att", [P, 2, P])
        qmask = sb("qmask", [P, DEC, 4, DEC])
        gnst = sb("gnst", [P, TILES, 6])
        gnmv = sb("gnmv", [P, 2, TILES, 2])
        gnsd = sb("gnsd", [P, 2, TILES])
        gnrs = sb("gnrs", [P, 2, TILES])
        EPT = {0: RT, 2: view(0, NB)}

        o = NB
        DRT = [view(o, NB), view(o + NB, NB)]
        o += 2 * NB
        RX = view(o, 4, 64)
        o += 256
        DQT = view(o, QH, TOK)
        o += QH * TOK
        QIT = view(o, IH // 2, TOK)
        o += QH * TOK
        DKT = view(o, KVH, TOK)
        o += KVH * TOK
        KIT = view(o, TOK)
        o += TOK
        KV = view(o, TILES, 2 * KVH * HD)
        o += TILES * 2 * KVH * HD
        KIW = view(o, TILES, ID + IH)
        o += TILES * (ID + IH)
        KID = view(o, TILES, 2 * ID)
        o += TILES * 2 * ID
        WI = view(o, TILES, IH)
        o += TILES * IH
        o_late = o
        SCORE, BIAS = view(o, NB), view(o + NB, NB)
        o += 2 * NB
        RL = [view(o, NB), view(o + NB, NB)]
        o += 2 * NB
        E = [view(o, NB), view(o + NB, NB)]
        o += 2 * NB
        PT = [view(o, NT, P), view(o + NB, NT, P)]
        o += 2 * NB
        m8 = sb("m8", [P, 8])
        mx = sb("mx", [P, 2])
        nbias = sb("nbias", [P, 2])
        esum = sb("esum", [P, 2])
        ersum = sb("ersum", [P, 2])
        OT = HT
        o = o_late
        KBT = view(o, DEC, KVH, LS)
        o += DEC * KVH * LS
        KIBT = [view(o, LS), view(o + LS, LS)]
        o += 2 * LS
        assert o <= MWORDS, o
        o = 0
        RLS = [view(0, 2, LS, r=DEC), view(2 * LS, 2, LS, r=DEC)]
        SCS, BIS = view(4 * LS, LS, r=DEC), view(5 * LS, LS, r=DEC)
        assert 6 * LS <= 3 * NB + 256
        QM_AT = -(-nc.sbuf_base // 32) * 32
        QM = sb("QM", [P, DEC, KVH, DEC * GRP])
        WM = sb("WM", [DEC, 2, DEC, DEC])
        PS = [sb(f"PS{n}", [DEC * GRP, LS]) for n in range(KVH)]
        PTS = sb("PTS", [P, KVH, NPG, DEC * GRP])
        PNW = sb("PNW", [DEC, KVH, DEC * GRP])
        DG = sb("DG", [DEC * GRP, KVH, DEC * GRP])

        def over(name, shape, dt, base, words):
            return nc.alloc_sbuf_tensor_at(name, shape, dt, offset=base + 4 * words)

        WH = over("WH", [P, SPLIT, 4, NB], F32R, M_AT, 0)
        WL = over("WL", [P, SPLIT, 4, NB], F32R, M_AT, SPLIT * UW)
        HGH = over("HGH", [P, 2, KD, P], F32R, HT_AT, 0)
        HGL = over("HGL", [P, 2, KD, P], F32R, HT_AT, 2 * D)
        o = 2 * SPLIT * UW
        HG = [view(o, D), rotc[:, :, :, :].rearrange("p a t d -> p (a t d)")[:, 0:D]]
        o += D
        SGE = view(o, FE)
        o += FE
        AE = view(o, FE)
        o += FE
        ATH = over("ATH", [P, 2, FE // P, P], F32R, M_AT, o)
        o += 2 * FE
        ATL = over("ATL", [P, 2, FE // P, P], F32R, M_AT, o)
        o += 2 * FE
        Y = [view(o, D), over("Y1", [P, D], F32, QM_AT, 0)]
        o += D
        assert o <= MWORDS, o
        HN = [view(2 * SPLIT * UW, D), view(2 * SPLIT * UW + D, D)]
        ro = [2 * SPLIT * UW + 2 * D]

        def rview(*shape):
            ro[0] += int(np.prod(shape))
            assert ro[0] <= MWORDS
            return view(ro[0] - int(np.prod(shape)), *shape)

        LG, PR, KEY, EQ, S1, S2, PM, DST = [rview(TILES, NE) for _ in range(8)]
        PAIRS = rview(TILES * NG, 6)
        GS, GK, GQ = [rview(TILES, NG) for _ in range(3)]
        r1, r2, r3, r4 = [rview(TILES) for _ in range(4)]
        cntv, nbk, cum, sta = [rview(NE) for _ in range(4)]
        big = rview(ITEMS - NE + 2, NE)
        itf = rview(ITEMS - NE + 2)
        mb = over("mb", [P, TILES, NE], BF16, ATT_AT, 0)
        YG = [[view((2 * b + k) * D, D) for k in range(2)] for b in range(2)]
        EPM = view(4 * D, D)

        out_waits = [("rp_st", 16 * RH), *[(f"state_st{s}", 32 * state_uses[s]) for s in range(3)], ("kv_st", 16 * 3 * TILES), ("y_out", 16 * TILES)]

        def pairs_before(eng, l):
            first = 0
            for k in range(l):
                first = first + (eng.value_load(np_i[0:1, k:k + 1], min_val=NE // 2 - 1, max_val=ITEMS // 2 - 1) + 1)
            return first

        def pairs(eng, l):
            return pairs_before(eng, l), eng.value_load(np_i[0:1, l:l + 1], min_val=NE // 2 - 1, max_val=ITEMS // 2 - 1)

        def raw(s):
            return RING[:, :, :].rearrange("p a w -> p (a w)")[:, s * UW:(s + 1) * UW].rearrange("p (k n) -> p k n", n=NB)

        def raw_count(i, u):
            return (i * (len(UNITS) // RAW) + u // RAW + 1) * 16

        block = ctx.enter_context(nc.Block())

        @block.sync
        def _(sp):
            def kpn(w, at, n):
                return w.rearrange("(k p) n -> p k n", p=P)[:, :, at:at + n]

            def wait_free(i):
                if i >= 3:
                    for name, v in stream[i - 3][1]:
                        sp.wait_ge(S(name), v)

            def load(key):
                i, s, _ = place[key]
                wait_free(i)
                kind = key[0]
                dst = slot(key)
                if kind == "state":
                    _, hp, b2 = key
                    for bb in range(2):
                        sp.dma_start(dst[:, 4 * bb:4 * bb + 4, :],
                                     A["state_ret"][0, 2 * b2 + bb, 2 * hp:2 * hp + 2]
                                     .rearrange("h (j p) v -> p (h j) v", p=P)).then_inc(S(f"ring_full{s}"), 16)
                    return
                if kind == "mod":
                    src = kpn(A["w_mod"][key[1]], key[2] * NB, NB)
                elif kind in ("q", "k"):
                    src = kpn(A["w_in_ret"][0], {"q": 0, "k": RH * RDK}[kind] + key[1] * NB, NB)
                elif kind in ("v", "g"):
                    at = {"v": 2 * RH * RDK, "g": 2 * RH * RDK + RH * RDV}[kind]
                    src = kpn(A["w_in_ret"][0], at + (2 * key[1] + key[2]) * NB, NB)
                elif kind == "out0":
                    src = kpn(A["w_out_ret"][0, key[2] * D:(key[2] + 1) * D, :], key[1] * NB, NB)
                elif kind == "out2":
                    src = kpn(A["w_out_dsa"][0], key[1] * NB, NB)
                else:
                    w = min(NB, DSA_IN - key[1] * NB)
                    src = kpn(A["w_in_dsa"][0], key[1] * NB, w)
                    dst = slot(key, KD, w)
                sp.dma_start(dst, src).then_inc(S(f"ring_full{s}"), 16)

            def load_pages(key):
                i, s, _ = place[(key,)]
                wait_free(i)
                src = A[{"kpg": "cache_k", "vpg": "cache_v", "ipg": "cache_kidx"}[key]]
                dst = RING[:, s, :]
                for i in range(DEC * NPG):
                    pg = sp.value_load(ptab[0:1, i:i + 1], min_val=0, max_val=src.shape[1] - 1)
                    if key == "ipg":
                        for c in range(2):
                            sp.dma_start(dst[:, i * P + c * ID:i * P + (c + 1) * ID],
                                         src[0, bass.ds(pg, 1)].rearrange("o t d -> (o t) d"))\
                                .then_inc(S(f"ring_full{s}"), 16)
                    else:
                        sp.dma_start(dst[:, i * KVH * HD:(i + 1) * KVH * HD],
                                     src[0, bass.ds(pg, 1)].rearrange("o t h d -> (o t) (h d)"))\
                            .then_inc(S(f"ring_full{s}"), 16)

            def load_unit(l, e, unit, s):
                _, w, h = unit
                src = A[w][l, e].rearrange("o (k p) n -> p (o k) n", p=P)
                src = src[:, :, h * NB:(h + 1) * NB] if w == "w_down" else src[:, 4 * h:4 * h + 4, :]
                sp.dma_start(raw(s), src).then_inc(S(f"raw_in{s}"), 16)

            def moe_loads(l):
                last = N_FIRST if l == 0 else len(stream)
                for i in range(last, last + 3):
                    wait_free(i)
                for u in range(RAW):
                    load_unit(l, slice(UNITS[u][0], UNITS[u][0] + 1), UNITS[u], u)
                sp.wait_ge(S(f"tables{l}"), 1)
                first, last = pairs(sp, l)

                def pair(k, upto):
                    item = None
                    for u in range(RAW, upto):
                        unit = UNITS[u % len(UNITS)]
                        if item != (unit[0], u // len(UNITS)):
                            item = (unit[0], u // len(UNITS))
                            at = k * 2 + item[0] + 2 * item[1]
                            e = sp.value_load(eid_i[0:1, bass.ds(at, 1)], min_val=0, max_val=NE - 1)
                        sp.wait_ge(S("lo_rdy"), (first + k) * len(UNITS) + (UNIT0 + u - RAW + 1))
                        load_unit(l, bass.ds(e, 1), unit, u % RAW)

                with sp.Fori(0, last) as k:
                    pair(k, RAW + len(UNITS))
                pair(last, len(UNITS))
                if l == 0:
                    sp.wait_ge(S("lo_rdy"), (first + last) * len(UNITS) + (len(UNITS) + UNIT0))

            def loads(part):
                for key, _ in part:
                    if key[0].endswith("pg"):
                        load_pages(key[0])
                    else:
                        load(key)

            sp.dma_start(ptab[0:1, :], A["page_table"].rearrange("(o b) j -> o (b j)", o=1)).then_inc(S("ptab_in"), 16)
            sp.wait_ge(S("ptab_in"), 16)
            loads(stream[:N_FIRST])
            moe_loads(0)
            loads(stream[N_FIRST:])
            moe_loads(1)
            for name, v in out_waits:
                sp.wait_ge(S(name), v)

        @block.tensor
        def _(pe):
            def transposes(dst, srcs, sem):
                for d_, s_ in zip(dst, srcs):
                    r = s_.shape[0]
                    last = pe.transpose(d_, s_, ident[0:r, 0:r])
                last.then_inc(S(sem), 1)

            def rhs_mm(out, lhs, w, sem, start=True, stop=True):
                K = lhs.shape[1]
                for k in range(K):
                    last = pe.matmul(out, lhs[:, k, :], w[:, k, :], start=start and k == 0, stop=stop and k == K - 1)
                last.then_inc(S(sem), 1)

            def modulated(m):
                for t in range(TILES):
                    R = rows(t)
                    pe.wait_ge(S("hn"), TILES * m + t + 1)
                    for g in range(2):
                        if t:
                            pe.wait_ge(S("ht_ev"), 2 * TILES * m + 2 * (t - 1) + g + 1)
                        transposes([bank[6 + g][:, q * R:(q + 1) * R] for q in range(4)],
                                   [HN[t % 2][0:R, (4 * g + q) * P:(4 * g + q + 1) * P] for q in range(4)], "ht_ps")
                pe.wait_ge(S("ht_ev"), 2 * TILES * m + 2 * TILES)

            def out_product(m, src, halves):
                for n in range(2):
                    for kh in range(halves):
                        wait_slot(pe, (f"out{m}", n, kh))
                        for t in range(TILES):
                            if kh == 0 and n == 1 and t >= 3:
                                pe.wait_ge(S(f"out_ev{m}"), t - 2)
                            rhs_mm(bank[(TILES * n + t) % 8][0:rows(t), :], src[:, kh * KD:(kh + 1) * KD, cols(t)],
                                   slot((f"out{m}", n, kh)), f"out_mm{m}" if kh == halves - 1 else f"out_half{m}",
                                   start=kh == 0, stop=kh == halves - 1)

            pe.nop().then_inc(S("unit_used"), UNIT0)
            for j in range(2):
                pe.nop().then_inc(S(f"at_ps{j}"), 1)
                pe.nop().then_inc(S(f"hg_ps{j}"), 2)
            pe.wait_ge(S("cst_in"), 16)
            pe.wait_ge(S("c_silu"), 1)
            R = DEC + 1
            transposes([bank[2][:, k * R:(k + 1) * R] for k in range(KD)],
                       [CSIL[:, k * P:(k + 1) * P] for k in range(KD)], "c_ps")
            pe.wait_ge(S("c_t"), 1)
            for n in range(12):
                wait_slot(pe, ("mod", 0, n))
                if n >= 2:
                    pe.wait_ge(S("mod_ev"), n - 1)
                rhs_mm(bank[n % 2][0:R, :], CT, slot(("mod", 0, n)), "mod_mm")

            def mod1(part):
                for n in part:
                    wait_slot(pe, ("mod", 1, n))
                    if n == 0:
                        pe.wait_ge(S("out_ev0"), 2 * TILES)
                    if n >= 4:
                        pe.wait_ge(S("mod_ev"), 12 + n - 3)
                    rhs_mm(bank[2 + n % 4][0:DEC + 1, :], CT, slot(("mod", 1, n)), "mod_mm")

            modulated(0)
            item = 0

            def ret_product(w_key, t):
                nonlocal item
                if t == 0:
                    wait_slot(pe, w_key)
                if item >= 2:
                    pe.wait_ge(S("ret_ev"), item - 1)
                rhs_mm(bank[item % 2][0:rows(t), :], HT[:, :, cols(t)], slot(w_key), "ret_mm")
                item += 1

            qk = 0
            yt = 0
            for hp in range(2):
                def turn_qk():
                    nonlocal qk
                    t = qk % TILES
                    R = rows(t)
                    pe.wait_ge(S("ro_rdy"), qk + 1)
                    if qk >= 2:
                        pe.wait_ge(S("qk_ev"), qk - 1)
                    isk = (qk // TILES) % 2
                    src = KN[:, t, :] if isk and t < NT else RO
                    transposes([bank[2 + qk % 2][:, q * R:(q + 1) * R] for q in range(4)],
                               [src[0:R, q * P:(q + 1) * P] for q in range(4)], "qk_ps")
                    qk += 1

                for i in range(2 * TILES):
                    ret_product((("q", "k")[i // TILES], hp), i % TILES)
                    if i:
                        turn_qk()
                ret_product(("v", hp, 0), 0)
                turn_qk()
                for i in range(1, 2 * TILES):
                    ret_product(("v", hp, i // TILES), i % TILES)
                pe.wait_ge(S("qk_ev"), qk)
                pe.wait_ge(S("ret_ev"), item)

                def attend(i):
                    hh, c = divmod(i, NT)
                    rc = hp * 2 * NT + i
                    if rc >= 2:
                        pe.wait_ge(S("att_rdy"), rc - 1)
                    for j in range(2):
                        last = pe.matmul(bank[3 + rc % 2][:, 0:P], KT[:, 2 * hh + j, cols(c)], QT[:, 2 * hh + j, cols(c)],
                                         start=j == 0, stop=j == 1)
                    last.then_inc(S("att_ps"), 1)

                attend(0)
                for i in range(2 * NT):
                    hh, c = divmod(i, NT)
                    rc = hp * 2 * NT + i
                    if i + 1 < 2 * NT:
                        attend(i + 1)
                    pe.wait_ge(S("att_rdy"), rc + 1)
                    if rc:
                        pe.wait_ge(S("s_rdy"), rc)
                        pe.wait_ge(S("o_ev"), rc)
                    vv = V[:, c, hh * NB:(hh + 1) * NB]
                    last = pe.matmul(bank[5][:, :], att[:, rc % 2, :], vv, start=True, stop=c == 0)
                    if c:
                        for j in range(2):
                            last = pe.matmul(bank[5][:, :], QT[:, 2 * hh + j, cols(c)], STATE[:, hh, j, :],
                                             start=False, stop=j == 1)
                    last.then_inc(S("o_ps"), 1)
                    for j in range(2):
                        last = pe.matmul(bank[6 + j][:, :], KN[:, c, (2 * hh + j) * P:(2 * hh + j + 1) * P], vv,
                                         start=True, stop=True)
                    last.then_inc(S("u_ps"), 1)

                def spread(i):
                    si = 2 * DEC * hp + i
                    if si >= 2:
                        pe.wait_ge(S("st_upd"), si - 1)
                    b, hh = divmod(i, 2)
                    pe.matmul(bank[2 + si % 2][:, :], ident[0:DEC, b:b + 1].to_broadcast([DEC, P]),
                              V[0:DEC, NT, hh * NB:(hh + 1) * NB], start=True, stop=True).then_inc(S("vb_ps"), 1)

                spread(0)
                pe.wait_ge(S("qm_rdy"), hp + 1)
                for i in range(2 * DEC):
                    si = 2 * DEC * hp + i
                    b, hh = divmod(i, 2)
                    if i + 1 < 2 * DEC:
                        spread(i + 1)
                    pe.wait_ge(S("st_upd"), si + 1)
                    st = slot(("state", hp, b // 2))
                    for j in range(2):
                        last = pe.matmul(bank[hh][0:DEC, :], qmask[:, b, 2 * hh + j, :],
                                         st[:, 4 * (b % 2) + 2 * hh + j, :], start=b == 0 and j == 0,
                                         stop=b == DEC - 1 and j == 1)
                    last.then_inc(S("os_mm"), 1)
                pe.wait_ge(S("os_ev"), 2 * (hp + 1))

                def turn_y():
                    nonlocal yt
                    t = yt % TILES
                    R = rows(t)
                    hh = (yt // TILES) % 2
                    pe.wait_ge(S("y_rdy"), yt + 1)
                    if yt >= 2:
                        pe.wait_ge(S("yt_ev"), yt - 1)
                    transposes([bank[2 + yt % 2][:, q * R:(q + 1) * R] for q in range(4)],
                               [V[0:R, t, hh * NB + q * P:hh * NB + (q + 1) * P] for q in range(4)], "yt_ps")
                    yt += 1

                for i in range(2 * TILES):
                    ret_product(("g", hp, i // TILES), i % TILES)
                    if i:
                        turn_y()
                turn_y()
            pe.wait_ge(S("yt_ev"), yt)
            pe.wait_ge(S("ret_ev"), item)
            out_product(0, YT, 2)

            def experts(l):
                m = 2 * l + 1
                if l == 0:
                    mod1(range(0, 6))
                modulated(m)
                for t in range(TILES):
                    rhs_mm(bank[0][0:rows(t), t * NE:(t + 1) * NE], HT[:, :, cols(t)], wr[:, :, :], f"lg_mm{l}")
                if l == 0:
                    mod1(range(6, 8))
                pe.wait_ge(S(f"marks{l}"), 1)
                for t in range(TILES + 1):
                    for t2 in range(min(t, TILES - 1) + 1):
                        last = pe.matmul(bank[1][:, t * NE:(t + 1) * NE], bf_cum[:, 0 if t2 == t else 1, :], mb[:, t2, :],
                                         start=t2 == 0, stop=t2 == min(t, TILES - 1))
                last.then_inc(S(f"rank_mm{l}"), 1)
                if l == 0:
                    mod1(range(8, 12))
                    pe.wait_ge(S("mod_ev"), 24)
                pe.wait_ge(S(f"tables{l}"), 1)
                first, last = pairs(pe, l)

                def turn_rows(j, i):
                    pe.wait_ge(S(f"rows_in{j}"), (i + 1) * 16)
                    pe.wait_ge(S(f"at_lo{j}"), i + 1)
                    for g in range(2):
                        transposes([bank[2 * j + g][:, q * P:(q + 1) * P] for q in range(4)],
                                   [HG[j][:, (4 * g + q) * P:(4 * g + q + 1) * P] for q in range(4)], f"hg_ps{j}")

                def pair(i, end):
                    def split_mm(out, xh, xl, u, start, stop):
                        pe.wait_ge(S("lo_rdy"), i * len(UNITS) + (UNIT0 + u + 1))
                        for c in range(4):
                            for n, (x_, w_) in enumerate(((xh, WH), (xh, WL), (xl, WH))):
                                done = pe.matmul(out, x_[:, c, :], w_[:, u % SPLIT, c, :], start=start and c == n == 0,
                                                 stop=stop and c == 3 and n == 2)
                        done.then_inc(S("unit_used"), 1)

                    def up(j, c, u):
                        for h in range(2):
                            split_mm(bank[4 + 2 * j + c][:, :], HGH[:, j, 4 * h:4 * h + 4, :], HGL[:, j, 4 * h:4 * h + 4, :],
                                     u + h, h == 0, h == 1)

                    def turn_a(j):
                        pe.wait_ge(S(f"a_rdy{j}"), i + 2)
                        transposes([bank[2 * j][:, q * P:(q + 1) * P] for q in range(4)],
                                   [AE[:, q * P:(q + 1) * P] for q in range(4)], f"at_ps{j}")

                    def down(j, h, u):
                        split_mm(bank[4 + 2 * j + h][:, :], ATH[:, j, :, :], ATL[:, j, :, :], u, True, True)

                    pe.wait_ge(S("hg_lo0"), 2 * (i + 1))
                    pe.wait_ge(S("y_ev_d0"), i + 1)
                    up(0, 0, 0)
                    turn_rows(1, i)
                    pe.wait_ge(S("y_ev_a0"), i + 1)
                    up(0, 1, 2)
                    pe.wait_ge(S("hg_lo1"), 2 * (i + 1))
                    pe.wait_ge(S("y_ev_d1"), i + 1)
                    up(1, 0, 4)
                    turn_a(0)
                    pe.wait_ge(S("y_ev_a1"), i + 1)
                    up(1, 1, 6)
                    pe.wait_ge(S("at_lo0"), i + 2)
                    down(0, 0, 8)
                    turn_a(1)
                    down(0, 1, 9)
                    if not end:
                        turn_rows(0, i + 1)
                    pe.wait_ge(S("at_lo1"), i + 2)
                    down(1, 0, 10)
                    down(1, 1, 11)

                turn_rows(0, first)
                with pe.Fori(0, last) as k:
                    pair(first + k, False)
                pair(first + last, True)

            experts(0)

            modulated(2)
            dt = 0

            def turn_d():
                nonlocal dt
                n, t = divmod(dt, TILES)
                R = rows(t)
                pe.wait_ge(S("d_rot"), dt + 1)
                if dt >= 2:
                    pe.wait_ge(S("d_tev"), dt - 1)
                src, nq = ((DRT[dt % 2], 4), (DRT[dt % 2], 4), (KV[:, t, :], 2), (DRT[dt % 2], 4), (DRT[dt % 2], 4),
                           (KID[:, t, :], 1))[n]
                transposes([bank[2 + dt % 2][:, q * R:(q + 1) * R] for q in range(nq)],
                           [src[0:R, q * P:(q + 1) * P] for q in range(nq)], "d_tp")
                dt += 1

            for i in range(6 * TILES):
                n, t = divmod(i, TILES)
                if t == 0:
                    wait_slot(pe, ("din", n))
                if i >= 2:
                    pe.wait_ge(S("d_ev"), i - 1)
                w = min(NB, DSA_IN - n * NB)
                rhs_mm(bank[i % 2][0:rows(t), 0:w], HT[:, :, cols(t)], slot(("din", n), KD, w), "d_mm")
                if i:
                    turn_d()
            turn_d()
            pe.wait_ge(S("d_tev"), 6 * TILES)
            pe.wait_ge(S("d_ev"), 6 * TILES)
            ix = 0
            for t in range(NT):
                L = (t + 1) * P
                if t:
                    for h in range(IH):
                        if ix >= 2:
                            pe.wait_ge(S("ix_rl"), ix - 1)
                        o64 = ID * (h % 2)
                        pe.matmul(bank[ix % 2][:, 0:L], QIT[o64:o64 + ID, h // 2, cols(t)], KIT[o64:o64 + ID, 0:L],
                                  start=True, stop=True).then_inc(S("ix_ps"), 1)
                        ix += 1

                def logits(h):
                    a = t * QH + h
                    if a >= 2:
                        pe.wait_ge(S("lg_ev"), a - 1)
                    pe.matmul(bank[2 + a % 2][:, 0:L], DQT[:, h, cols(t)], DKT[:, h // GRP, 0:L],
                              start=True, stop=True).then_inc(S("lg_ps"), 1)

                def turn_p(h):
                    a = t * QH + h
                    pe.wait_ge(S("p_rdy"), a + 1)
                    if a >= 2:
                        pe.wait_ge(S("pt_ev"), a - 1)
                    transposes([bank[4 + a % 2][:, q * P:(q + 1) * P] for q in range(t + 1)],
                               [E[a % 2][:, q * P:(q + 1) * P] for q in range(t + 1)], "pt_ps")

                def pv(h):
                    a = t * QH + h
                    pe.wait_ge(S("pt_ev"), a + 1)
                    if a >= 2:
                        pe.wait_ge(S("ot_ev"), a - 1)
                    n = h // GRP
                    for c in range(t + 1):
                        last = pe.matmul(bank[6 + a % 2][:, 0:P], KV[:, c, KVH * HD + n * HD:KVH * HD + (n + 1) * HD],
                                         PT[a % 2][:, c, :], start=c == 0, stop=c == t)
                    last.then_inc(S("pv_mm"), 1)

                for s in range(QH + 3):
                    if s < QH:
                        logits(s)
                    if 2 <= s < QH + 2:
                        turn_p(s - 2)
                    if s >= 3:
                        pv(s - 3)

            transposes([bank[0][0:DEC, par * DEC:(par + 1) * DEC] for par in range(2)],
                       [WI[0:DEC, NT, :].rearrange("p (h two) -> p two h", two=2)[:, par, :] for par in range(2)], "w_t")
            wait_slot(pe, ("ipg",))
            wait_slot(pe, ("kpg",))
            pe.wait_ge(S("ot_ev"), NT * QH)
            pe.wait_ge(S("wm_rdy"), 1)
            ipg = RING[:, place[("ipg",)][1], 0:DEC * NPG * P].rearrange("p (i d) -> p i d", d=P)
            kpg = RING[:, place[("kpg",)][1], :].rearrange("p (i n d) -> p i n d", n=KVH, d=HD)
            vpg = RING[:, place[("vpg",)][1], :].rearrange("p (i n d) -> p i n d", n=KVH, d=HD)

            def s_score(b):
                pe.wait_ge(S("s_rl"), b + 1)
                for par in range(2):
                    last = pe.matmul(bank[6][0:DEC, 0:LS], WM[:, par, b, :], RLS[b % 2][:, par, :],
                                     start=b == 0 and par == 0, stop=b == DEC - 1 and par == 1)
                last.then_inc(S("s_sc"), 1)

            for b in range(DEC):
                if b:
                    pe.wait_ge(S("ki_ev"), b)
                transposes([bank[0][:, q * P:(q + 1) * P] for q in range(NPG)],
                           [ipg[:, b * NPG + q, :] for q in range(NPG)], "ki_t")
                for n in range(KVH):
                    if b:
                        pe.wait_ge(S("kk_ev"), 2 * (b - 1) + n + 1)
                    transposes([bank[1 + n][:, q * P:(q + 1) * P] for q in range(NPG)],
                               [kpg[:, b * NPG + q, n, :] for q in range(NPG)], "kk_t")
                pe.wait_ge(S("ki_rdy"), b + 1)
                pe.wait_ge(S("ki_ev"), b + 1)
                if b:
                    pe.wait_ge(S("s_rl"), b)
                for par in range(2):
                    last = pe.matmul(bank[3 + par][0:DEC, 0:LS],
                                     QIT[par * ID:(par + 1) * ID, :, SEQ + b], KIBT[b % 2][par * ID:(par + 1) * ID, :],
                                     start=True, stop=True)
                last.then_inc(S("s_dot"), 1)
                if b:
                    s_score(b - 1)
            s_score(DEC - 1)
            pe.wait_ge(S("s_bias"), 1)
            pe.wait_ge(S("kk_ev"), 2 * DEC)
            pe.wait_ge(S("kn_rdy"), 1)
            for n in range(KVH):
                pe.matmul(bank[n][0:DEC * GRP, 0:LS], C("bexp", DEC), BIS[0:DEC, :], start=True, stop=False)
                for b in range(DEC):
                    last = pe.matmul(bank[n][0:DEC * GRP, 0:LS], QM[:, b, n, :], KBT[:, b, n, :], start=False,
                                     stop=b == DEC - 1)
                last.then_inc(S("s_lg"), 1)
            wait_slot(pe, ("vpg",))
            for n in range(KVH):
                pe.wait_ge(S("s_p"), n + 1)
                r = DEC * GRP
                for q in range(NPG):
                    pe.transpose(bank[2 + n][:, q * r:(q + 1) * r], PS[n][:, q * P:(q + 1) * P], ident[0:r, 0:r])
                pe.matmul(bank[4 + n][0:DEC, 0:r], C("bsel", r), DG[:, n, :], start=True, stop=True).then_inc(S("s_pt"), 1)
            for n in range(KVH):
                pe.wait_ge(S("s_ptev"), n + 1)
                out = bank[6 + n]
                pe.matmul(out[:, 0:DEC * GRP], KV[0:DEC, NT, (KVH + n) * HD:(KVH + n + 1) * HD], PNW[:, n, :],
                          start=True, stop=False)
                for b in range(DEC):
                    for q in range(NPG):
                        last = pe.matmul(out[:, b * GRP:(b + 1) * GRP], vpg[:, b * NPG + q, n, :],
                                         PTS[:, n, q, b * GRP:(b + 1) * GRP], start=False,
                                         stop=b == DEC - 1 and q == NPG - 1)
                last.then_inc(S("s_pv"), 1)
            pe.wait_ge(S("s_ot"), KVH)
            pe.wait_ge(S("ot_ev"), NT * QH)
            out_product(2, OT, 1)
            experts(1)

        @block.scalar
        def _(act):
            def vectors(m, n, parts, sample):
                l, half = divmod(m, 2)
                for i, p_ in parts:
                    at = (3 * half + p_) * D
                    act.dma_start(BC[:, i, :], mod_d[l, DEC:DEC + 1, at:at + D].to_broadcast([P, D])).then_inc(S(n), 16)
                    act.dma_start(SC[:, i, :], mod_d[l, 0:DEC, at:at + D]).then_inc(S(n), 16)

            def modulated(m):
                if m:
                    act.wait_ge(S("x_rdy"), TILES * m)
                act.wait_ge(S(f"mod_st{m // 2}"), 16 if m < 2 else 16 * 12)
                vectors(m, "bc_in", ((0, 1), (1, 0)), True)
                if m == 0:
                    act.wait_ge(S("y_zero"), 16)
                for t in range(TILES):
                    R = rows(t)
                    for g in range(2):
                        act.wait_ge(S("ht_ps"), 2 * TILES * m + 2 * t + g + 1)
                        act.activation(HT[:, 4 * g:4 * g + 4, cols(t)],
                                       bank[6 + g][:, 0:4 * R].rearrange("p (q r) -> p q r", r=R),
                                       ACT.Copy).then_inc(S("ht_ev"), 1)

            def closing(m):
                l, half = divmod(m, 2)
                vectors(m, "ep_in", ((0, 2),), True)
                for i, w in ((1, ("ln1_g", "ln2_g")[half]), (2, ("ln1_b", "ln2_b")[half])):
                    act.dma_start(BC[:, i, :], A[w][l:l + 1, :].to_broadcast([P, D])).then_inc(S("ep_in"), 16)

            def roots(m):
                act.wait_ge(S("ln_var"), 1 * m + 1)
                act.activation(lnsd[:, :], lnmv[:, :, 1], ACT.Sqrt, bias=C("lneps"), scale=1.0).then_inc(S("ln_sd"), 1)

            act.dma_start(CROW[0:DEC, :], A["c_sample"]).then_inc(S("c_in"), 16)
            act.dma_start(CROW[DEC:DEC + 1, :], A["c_prompt"]).then_inc(S("c_in"), 16)
            act.dma_start(cst[:, :], A["cst"]).then_inc(S("cst_in"), 16)
            act.dma_start(BMOD[:, :], A["b_mod"][0:1, :].to_broadcast([DEC + 1, 6 * D]))\
                .then_inc(S("bmod_in"), 16)
            act.dma_start(rotc[:, :, :, :], A["rotc"]).then_inc(S("const_in"), 16)
            act.dma_start(tok[:, :], A["tok"]).then_inc(S("const_in"), 16)
            act.dma_start(wr[:, :, :], A["w_router"].rearrange("(k p) e -> p k e", p=P)).then_inc(S("const_in"), 16)
            act.dma_start(br[:, :], A["b_router"].rearrange("(o e) -> o e", o=1).to_broadcast([P, NE])).then_inc(S("const_in"), 16)
            act.dma_start(X[:, 0:NT, :], A["x_prompt"][0].rearrange("(t p) d -> p t d", p=P)).then_inc(S("x_in"), 16)
            act.dma_start(X[0:DEC, NT, :], A["x_sample"].rearrange("b t d -> (b t) d")).then_inc(S("x_in"), 16)
            act.wait_ge(S("c_in"), 32)
            for j in range(2):
                act.nop().then_inc(S(f"y_ev_a{j}"), 1)
            act.activation(CSIL[:, :], CROW[:, :], ACT.Silu).then_inc(S("c_silu"), 1)
            act.wait_ge(S("mod_ev"), 12)
            act.dma_start(mod_d[0], MODV[:, :]).then_inc(S("mod_st0"), 16)

            def mod1(part):
                for n in part:
                    act.wait_ge(S("mod_mm"), 12 + n + 1)
                    if n:
                        act.wait_ge(S("mod_st1"), 16 * n)
                    act.activation(MS1, bank[2 + n % 4][0:DEC + 1, :], ACT.Copy).then_inc(S("mod_ev"), 1)

            modulated(0)
            item = qk = yt = 0
            for hp in range(2):
                if hp == 0:
                    act.wait_ge(S("hn"), TILES)
                else:
                    act.wait_ge(S("y_rdy"), 2 * TILES)
                act.dma_start(GNB, A["gn_ret_g"][0:1, hp * D:(hp + 1) * D].to_broadcast([P, D])).then_inc(S("gn_in"), 16)

                def take_qk():
                    nonlocal qk
                    t = qk % TILES
                    R = rows(t)
                    act.wait_ge(S("qk_ps"), qk + 1)
                    dst = (QT, KT)[(qk // TILES) % 2]
                    act.activation(dst[:, :, cols(t)], bank[2 + qk % 2][:, 0:4 * R].rearrange("p (q r) -> p q r", r=R),
                                   ACT.Copy).then_inc(S("qk_ev"), 1)
                    qk += 1

                for i in range(2 * TILES):
                    t = i % TILES
                    R = rows(t)
                    act.wait_ge(S("ret_mm"), item + 1)
                    if item:
                        act.wait_ge(S("ro_rdy"), hp * 2 * TILES + i)
                    if hp and i == 0:
                        act.wait_ge(S("y_rdy"), 2 * TILES)
                    for hh in range(2):
                        sc_ = C(("qs", "ks")[i // TILES])[0:R, t * RH + 2 * hp + hh:t * RH + 2 * hp + hh + 1]
                        last = act.activation(RT[0:R, hh * RDK:(hh + 1) * RDK],
                                              bank[item % 2][0:R, hh * RDK:(hh + 1) * RDK], ACT.Copy, scale=sc_)
                    last.then_inc(S("ret_ev"), 1)
                    item += 1
                    if i:
                        take_qk()
                for i in range(2 * TILES):
                    hh, t = divmod(i, TILES)
                    act.wait_ge(S("ret_mm"), item + 1)
                    act.activation(V[0:rows(t), t, hh * NB:(hh + 1) * NB], bank[item % 2][0:rows(t), :], ACT.Copy)\
                        .then_inc(S("ret_ev"), 1)
                    item += 1
                    if i == 0:
                        take_qk()
                for i in range(2 * NT):
                    hh, c = divmod(i, NT)
                    rc = hp * 2 * NT + i
                    act.wait_ge(S("u_ps"), rc + 1)
                    act.activation(V[:, c, hh * NB:(hh + 1) * NB], bank[5][:, :], ACT.Copy).then_inc(S("o_ev"), 1)
                for i in range(2 * DEC):
                    b, hh = divmod(i, 2)
                    key = ("state", hp, b // 2)
                    if i % 4 == 0:
                        wait_slot(act, key)
                    st = slot(key)[:, 4 * (b % 2) + 2 * hh:4 * (b % 2) + 2 * hh + 2, :]
                    act.activation(st, st, ACT.Copy, scale=GAMMA[2 * hp + hh]).then_inc(S("st_dec"), 1)
                act.wait_ge(S("os_mm"), 2 * DEC * (hp + 1))
                for hh in range(2):
                    act.activation(V[0:DEC, NT, hh * NB:(hh + 1) * NB], bank[hh][0:DEC, :], ACT.Copy)\
                        .then_inc(S("os_ev"), 1)
                act.wait_ge(S("gn_var"), hp + 1)
                act.activation(gnsd[:, :, :], gnmv[:, :, :, 1], ACT.Sqrt, bias=C("gneps"), scale=1.0).then_inc(S("gn_sd"), 1)

                def take_y():
                    nonlocal yt
                    t = yt % TILES
                    R = rows(t)
                    h = yt // TILES
                    act.wait_ge(S("yt_ps"), yt + 1)
                    act.activation(YT[:, 4 * h:4 * h + 4, cols(t)],
                                   bank[2 + yt % 2][:, 0:4 * R].rearrange("p (q r) -> p q r", r=R), ACT.Copy)\
                        .then_inc(S("yt_ev"), 1)
                    yt += 1

                for i in range(2 * TILES):
                    t = i % TILES
                    act.wait_ge(S("ret_mm"), item + 1)
                    g = hp * 2 * TILES + i
                    if i >= 2:
                        act.wait_ge(S("y_rdy"), g - 1)
                    act.activation(SG[i % 2][0:rows(t), :], bank[item % 2][0:rows(t), :], ACT.Silu).then_inc(S("ret_ev"), 1)
                    item += 1
                    if i:
                        take_y()
                take_y()
            act.wait_ge(S("y_rdy"), 4 * TILES)
            act.wait_ge(S("rp_st"), 16 * RH)
            closing(0)
            roots(0)

            def experts(l):
                m = 2 * l + 1
                if l == 0:
                    mod1(range(0, 6))
                modulated(m)
                act.wait_ge(S("hn"), TILES * m + TILES)
                closing(m)
                act.wait_ge(S(f"lg_sub{l}"), 1)
                act.activation(PR, LG, ACT.Exp).then_inc(S(f"lg_exp{l}"), 1)
                if l == 0:
                    mod1(range(6, 12))

                def high(i, u):
                    act.wait_ge(S(f"raw_in{u % RAW}"), raw_count(i, u))
                    act.wait_ge(S("unit_used"), i * len(UNITS) + (UNIT0 + u - SPLIT + 1))
                    act.activation(WH[:, u % SPLIT, :, :], raw(u % RAW), ACT.Copy).then_inc(S("hi_rdy"), 1)

                first = pairs_before(act, l)
                for u in range(SPLIT):
                    high(first, u)
                act.wait_ge(S(f"tables{l}"), 1)
                first, last = pairs(act, l)

                def take_rows(j, i):
                    for g in range(2):
                        act.wait_ge(S(f"hg_ps{j}"), 2 * i + (g + 3))
                        act.activation(HGH[:, j, 4 * g:4 * g + 4, :], bank[2 * j + g][:, :].rearrange("p (q r) -> p q r", r=P),
                                       ACT.Copy).then_inc(S(f"hg_hi{j}"), 1)

                def pair(i, end):
                    def used(u):
                        act.wait_ge(S("unit_used"), i * len(UNITS) + (UNIT0 + u + 1))

                    def gate(j, u):
                        used(u)
                        act.wait_ge(S("at_ps1" if j == 0 else "at_ps0"), i + 1 + j)
                        act.activation(SGE, bank[4 + 2 * j][:, :], ACT.Silu).then_inc(S(f"sg{j}"), 1)

                    def take_a(j):
                        act.wait_ge(S(f"at_ps{j}"), i + 2)
                        act.activation(ATH[:, j, :, :], bank[2 * j][:, :].rearrange("p (q r) -> p q r", r=P), ACT.Copy)\
                            .then_inc(S(f"at_hi{j}"), 1)

                    def take_y(j, u):
                        used(u)
                        act.wait_ge(S(f"y_st{j}"), (i + 1) * 16)
                        act.activation(Y[j][:, NB:D], bank[5 + 2 * j][:, :], ACT.Copy).then_inc(S(f"y_ev_a{j}"), 1)

                    for u in range(SPLIT, SPLIT + len(UNITS)):
                        if not end or u < len(UNITS):
                            high(i, u)
                        if u == 5:
                            take_rows(1, i)
                            gate(0, 1)
                        if u == 9:
                            gate(1, 5)
                            take_a(0)
                        if u == 12:
                            take_a(1)
                        if u == 13:
                            if not end:
                                take_rows(0, i + 1)
                            take_y(0, 9)
                        if u == 15:
                            take_y(1, 11)

                take_rows(0, first)
                with act.Fori(0, last) as k:
                    pair(first + k, False)
                pair(first + last, True)
                roots(m)

            experts(0)

            modulated(2)

            def take_d(i):
                n, t = divmod(i, TILES)
                R = rows(t)
                act.wait_ge(S("d_tp"), i + 1)
                dst = (DQT[:, 0:4], DQT[:, 4:8], DKT, QIT[:, 0:4], QIT[:, 4:8], None)[n]
                if n == 5:
                    act.activation(KIT[:, cols(t)], bank[2 + i % 2][:, 0:R], ACT.Copy).then_inc(S("d_tev"), 1)
                else:
                    nq = dst.shape[1]
                    act.activation(dst[:, :, cols(t)], bank[2 + i % 2][:, 0:nq * R].rearrange("p (q r) -> p q r", r=R),
                                   ACT.Copy).then_inc(S("d_tev"), 1)

            for i in range(6 * TILES):
                n, t = divmod(i, TILES)
                R = rows(t)
                act.wait_ge(S("d_mm"), i + 1)
                if i >= 2:
                    act.wait_ge(S("d_tp"), i - 1)
                w = min(NB, DSA_IN - n * NB)
                dst = KV[0:R, t, :] if n == 2 else KIW[0:R, t, :] if n == 5 else DRT[i % 2][0:R, :]
                act.activation(dst, bank[i % 2][0:R, 0:w], ACT.Copy).then_inc(S("d_ev"), 1)
                if i:
                    take_d(i - 1)
            take_d(6 * TILES - 1)
            ix = 0
            SCALE = HD ** -0.5
            for t in range(NT):
                L = (t + 1) * P
                if t:
                    for h in range(IH):
                        act.wait_ge(S("ix_ps"), ix + 1)
                        if ix >= 2:
                            act.wait_ge(S("ix_acc"), ix - 1)
                        act.activation(RL[ix % 2][:, 0:L], bank[ix % 2][:, 0:L], ACT.Relu, scale=ID ** -0.5)\
                            .then_inc(S("ix_rl"), 1)
                        ix += 1

                def take_p(h):
                    a = t * QH + h
                    act.wait_ge(S("pt_ps"), a + 1)
                    if a >= 2:
                        act.wait_ge(S("pv_mm"), a - 1)
                    act.activation(PT[a % 2][:, 0:t + 1, :], bank[4 + a % 2][:, 0:L].rearrange("p (q r) -> p q r", r=P),
                                   ACT.Copy).then_inc(S("pt_ev"), 1)

                def take_o(h):
                    a = t * QH + h
                    act.wait_ge(S("pv_mm"), a + 1)
                    act.activation(OT[:, h, cols(t)], bank[6 + a % 2][:, 0:P], ACT.Copy).then_inc(S("ot_ev"), 1)

                for s in range(QH + 3):
                    if s < QH:
                        a = t * QH + s
                        act.wait_ge(S("nb_rdy"), a + 1)
                        act.activation(E[a % 2][:, 0:L], E[a % 2][:, 0:L], ACT.Exp, bias=nbias[:, a % 2:a % 2 + 1],
                                       scale=SCALE, accum_out=esum[:, a % 2:a % 2 + 1]).then_inc(S("e_rdy"), 1)
                    if 2 <= s < QH + 2:
                        take_p(s - 2)
                    if s >= 3:
                        take_o(s - 3)

            for b in range(DEC):
                act.wait_ge(S("ki_t"), b + 1)
                if b >= 2:
                    act.wait_ge(S("s_dot"), b - 1)
                act.activation(KIBT[b % 2][:, 0:PAST], bank[0][:, 0:PAST], ACT.Copy).then_inc(S("ki_ev"), 1)
                for n in range(KVH):
                    act.wait_ge(S("kk_t"), 2 * b + n + 1)
                    act.activation(KBT[:, b, n, 0:PAST], bank[1 + n][:, 0:PAST], ACT.Copy).then_inc(S("kk_ev"), 1)
                act.wait_ge(S("s_dot"), b + 1)
                if b >= 2:
                    act.wait_ge(S("s_sc"), b - 1)
                for par in range(2):
                    last = act.activation(RLS[b % 2][:, par, :], bank[3 + par][0:DEC, 0:LS], ACT.Relu, scale=ID ** -0.5)
                last.then_inc(S("s_rl"), 1)
            for n in range(KVH):
                act.wait_ge(S("s_nb"), n + 1)
                r = DEC * GRP
                act.activation(PS[n][:, :], PS[n][:, :], ACT.Exp, bias=nbias[0:r, n:n + 1], scale=SCALE,
                               accum_out=esum[0:r, n:n + 1]).then_inc(S("s_e"), 1)
            for n in range(KVH):
                act.wait_ge(S("s_pt"), n + 1)
                r = DEC * GRP
                act.activation(PTS[:, n, :, :], bank[2 + n][:, 0:NPG * r].rearrange("p (q r) -> p q r", r=r), ACT.Copy)
                act.activation(PNW[:, n, :], bank[4 + n][0:DEC, 0:r], ACT.Copy).then_inc(S("s_ptev"), 1)
            for n in range(KVH):
                act.wait_ge(S("s_pv"), n + 1)
                act.activation(OT[:, n * GRP:(n + 1) * GRP, SEQ:TOK],
                               bank[6 + n][:, 0:DEC * GRP].rearrange("p (b g) -> p g b", g=GRP), ACT.Copy)\
                    .then_inc(S("s_ot"), 1)
            act.wait_ge(S("hn"), 3 * TILES)
            closing(2)
            roots(2)
            experts(1)
            for t in range(TILES):
                act.wait_ge(S("x_rdy"), 3 * TILES + t + 1)
                dst = O["y_prompt"][0, t * P:(t + 1) * P, :] if t < NT else O["y_sample"].rearrange("b t d -> (b t) d")
                act.dma_start(dst, X[0:rows(t), t, :]).then_inc(S("y_out"), 16)

        @block.gpsimd
        def _(pool):
            for j in range(2):
                pool.dma_start(primer[j:j + 1, :], A["tok"][j:j + 1, 0:2]).then_inc(S(f"y_st{j}"), 16)
            nc.gpsimd.memset(zero_i[:, :], 0).then_inc(S("zeros"), 1)
            pool.wait_ge(S("c_t"), 1)
            zero_f = HT[:, 0:2, :].rearrange("p k t -> p (k t)")[:, 0:D]
            nc.gpsimd.memset(zero_f, 0.0).then_inc(S("zeros"), 1)
            pool.wait_ge(S("zeros"), 2)
            pool.dma_start(y_items[:, NE:, :],
                           zero_f.rearrange("p (o d) -> p o d", o=1).to_broadcast([P, ITEMS - NE, D])).then_inc(S("y_zero"), 16)
            pool.dma_start(slot_d.rearrange("(p i) o -> p (i o)", p=P), zero_i[:, :]).then_inc(S("slot_zero"), 16)
            for hp in range(2):
                for hh in range(2):
                    h = 2 * hp + hh
                    pool.wait_ge(S("s_rdy"), (h + 1) * NT)
                    pool.dma_start(O["ret_prompt"][0, 0, h].rearrange("(j p) v -> p j v", p=P), STATE[:, hh, :, :])\
                        .then_inc(S("rp_st"), 16)
                for b in range(DEC):
                    n = 2 * DEC * hp + 2 * b + 2
                    pool.wait_ge(S("st_upd"), n)
                    pool.dma_start(O["ret_sample"][0, b, 2 * hp:2 * hp + 2].rearrange("h (j p) v -> p (h j) v", p=P),
                                   slot(("state", hp, b // 2))[:, 4 * (b % 2):4 * (b % 2) + 4, :])\
                        .then_inc(S(f"state_st{place[('state', hp, b // 2)][1]}"), 16)

            def mod1(part):
                for n in part:
                    pool.dma_start(BM1, A["b_mod"][1:2, n * NB:(n + 1) * NB].to_broadcast([DEC + 1, NB]))\
                        .then_inc(S("bm_in"), 16)
                    pool.wait_ge(S("bm_in"), 16 * (n + 1))
                    pool.wait_ge(S("mod_ev"), 12 + n + 1)
                    nc.gpsimd.tensor_tensor(MS1, MS1, BM1, ALU.add)
                    pool.drain()
                    if n in (2, 3, 8, 9):
                        nc.gpsimd.tensor_scalar(MS1, MS1, 1.0, 0.0, ALU.add, ALU.add)
                        pool.drain()
                    pool.dma_start(mod_d[1][:, n * NB:(n + 1) * NB], MS1).then_inc(S("mod_st1"), 16)

            def experts(l):
                m = 2 * l + 1
                if l == 0:
                    pool.wait_ge(S("ro_rdy"), 4 * TILES)
                    mod1(range(0, 6))
                for t in range(TILES):
                    pool.wait_ge(S("hn"), TILES * m + t + 1)
                    pool.dma_start(h_d[cols(t), :], HN[t % 2][0:rows(t), :]).then_inc(S(f"h_st{t % 2}"), 16)
                if l == 0:
                    mod1(range(6, 8))
                pool.wait_ge(S("slot_zero"), 16)
                pool.wait_ge(S(f"tables{l}"), 1)
                for k in range(2):
                    for t in range(TILES):
                        R = rows(t)
                        pool.indirect_dma_start(out=slot_d, out_offset=bass.IndirectOffsetOnAxis(ap=dest_i[0:R, k, t:t + 1], axis=0),
                                                in_=tok[0:R, t:t + 1], in_offset=None).then_inc(S(f"scattered{l}"), 16)
                if l == 0:
                    mod1(range(8, 12))
                pool.wait_ge(S(f"scattered{l}"), 16 * 2 * TILES)
                pool.dma_start(slot_i[:, :], slot_d.rearrange("(p i) o -> p (i o)", i=ITEMS)).then_inc(S("slots_in"), 16)
                for par in range(2):
                    pool.wait_ge(S(f"h_st{par}"), 16 * (l + 1) * tiles_of[par])
                pool.wait_ge(S("mod_st1"), 16 * 12)
                pool.wait_ge(S("slots_in"), 16 * (l + 1))
                first, last = pairs(pool, l)

                def gather(j, k):
                    pool.wait_ge(S(f"hg_ps{j}"), (first + k) * 2 + 2)
                    nc.gpsimd.tensor_tensor(slot_c[:, j:j + 1], slot_i[:, bass.ds(k * 2 + j, 1)], zero_i[:, 0:1], ALU.add)
                    pool.drain()
                    pool.indirect_dma_start(out=HG[j], out_offset=None, in_=h_d,
                                            in_offset=bass.IndirectOffsetOnAxis(ap=slot_c[:, j:j + 1], axis=0))\
                        .then_inc(S(f"rows_in{j}"), 16)

                def store(j, k):
                    pool.wait_ge(S(f"y_ev_d{j}"), (first + k) + 2)
                    pool.wait_ge(S(f"y_ev_a{j}"), (first + k) + 2)
                    pool.dma_start(y_items[:, bass.ds(k * 2 + j, 1), :].rearrange("p o d -> p (o d)"), Y[j][:, :])\
                        .then_inc(S(f"y_st{j}"), 16)

                gather(0, 0)
                gather(1, 0)
                with pool.Fori(0, last) as k:
                    gather(0, k + 1)
                    gather(1, k + 1)
                    store(0, k)
                    store(1, k)
                store(0, last)
                store(1, last)
                for j in range(2):
                    pool.wait_ge(S(f"y_st{j}"), ((first + last) + 2) * 16)
                nc.gpsimd.tensor_tensor(dest_c[:, :, :], dest_i[:, :, :],
                                        zero_i[:, 0:2 * TILES].rearrange("p (k t) -> p k t", k=2), ALU.add)
                pool.drain()
                for t in range(TILES):
                    R = rows(t)
                    if t >= 2:
                        pool.wait_ge(S(f"cmb{l}"), t - 1)
                    for k in range(2):
                        pool.indirect_dma_start(out=YG[t % 2][k][0:R, :], out_offset=None, in_=y_d,
                                                in_offset=bass.IndirectOffsetOnAxis(ap=dest_c[0:R, k, t:t + 1], axis=0))\
                            .then_inc(S(f"yg_in{t % 2}"), 16)

            experts(0)
            nc.gpsimd.memset(QM[:, :, :, :], 0.0).then_inc(S("mask_zero"), 1)
            nc.gpsimd.memset(WM[:, :, :, :], 0.0).then_inc(S("mask_zero"), 1)
            for t in range(TILES):
                R = rows(t)
                pool.wait_ge(S("d_rot"), 2 * TILES + t + 1)
                for src, name in ((KV[0:R, t, 0:KVH * HD], "k"), (KV[0:R, t, KVH * HD:], "v")):
                    dst = O[name + "_prompt"][0, 0, cols(t)] if t < NT else O[name + "_sample"][0, :, 0]
                    pool.dma_start(dst.rearrange("t h d -> t (h d)"), src).then_inc(S("kv_st"), 16)
            for t in range(TILES):
                R = rows(t)
                pool.wait_ge(S("d_rot"), 5 * TILES + t + 1)
                dst = O["kidx_prompt"][0, 0, cols(t)] if t < NT else O["kidx_sample"][0, :, 0]
                pool.dma_start(dst, KIW[0:R, t, 0:ID]).then_inc(S("kv_st"), 16)
            experts(1)

        @block.vector
        def _(dve):
            TS, TT, STT = dve.tensor_scalar, dve.tensor_tensor, dve.scalar_tensor_tensor

            def modulated(m):
                dve.wait_ge(S("bc_in"), 64 * m + 64)
                for t in range(TILES):
                    R = rows(t)
                    sc_, sh = (BC[:, 0, :], BC[:, 1, :]) if t < NT else (SC[:, 0, :], SC[:, 1, :])
                    if t >= 2:
                        dve.wait_ge(S("ht_ps"), 2 * TILES * m + 2 * (t - 1))
                        if m % 2:
                            dve.wait_ge(S(f"h_st{t % 2}"), 16 * ((m // 2) * tiles_of[t % 2] + t // 2))
                    TT(HN[t % 2][0:R, :], X[0:R, t, :], sc_, ALU.mult)
                    dve.drain()
                    TT(HN[t % 2][0:R, :], HN[t % 2][0:R, :], sh, ALU.add).then_inc(S("hn"), 1)

            def norm(m):
                dve.drain()
                for t in range(TILES):
                    for g in range(2):
                        dve.bn_stats(lnst[0:rows(t), t, g, :], X[0:rows(t), t, g * NB:(g + 1) * NB])
                dve.drain()
                for t in range(TILES):
                    last = dve.bn_aggr(lnmv[0:rows(t), t, :], lnst[0:rows(t), t, :, :])
                last.then_inc(S("ln_var"), 1)
                dve.wait_ge(S("ln_sd"), 1 * m + 1)
                dve.reciprocal(lnrs[:, :], lnsd[:, :])
                dve.drain()
                for t in range(TILES):
                    R = rows(t)
                    TS(X[0:R, t, :], X[0:R, t, :], lnmv[0:R, t, 0:1], lnrs[0:R, t:t + 1], ALU.subtract, ALU.mult)
                dve.drain()
                for t in range(TILES):
                    TT(X[0:rows(t), t, :], X[0:rows(t), t, :], BC[0:rows(t), 1, :], ALU.mult)
                dve.drain()
                for t in range(TILES):
                    TT(X[0:rows(t), t, :], X[0:rows(t), t, :], BC[0:rows(t), 2, :], ALU.add).then_inc(S("x_rdy"), 1)
                dve.drain()

            def mixer_close(m):
                T = EPT[m]
                dve.wait_ge(S("ep_in"), 64 * m + 64)
                for n in range(2):
                    for t in range(TILES):
                        R = rows(t)
                        gt = (BC if t < NT else SC)[0:R, 0, n * NB:(n + 1) * NB]
                        dve.wait_ge(S(f"out_mm{m}"), TILES * n + t + 1)
                        TT(T[0:R, :], bank[(TILES * n + t) % 8][0:R, :], gt, ALU.mult).then_inc(S(f"out_ev{m}"), 1)
                        dve.drain()
                        xx = X[0:R, t, n * NB:(n + 1) * NB]
                        STT(xx, xx, ALPHA, T[0:R, :], ALU.mult, ALU.add)
                        dve.drain()
                norm(m)

            for j in range(2):
                for name in ("a_rdy", "y_ev_d", "at_lo"):
                    dve.engine_nop().then_inc(S(f"{name}{j}"), 1)
            dve.engine_nop().then_inc(S("lo_rdy"), UNIT0)
            dve.memset(gnmv[:, :, :, :], 1.0)
            dve.memset(lnmv[:, :, :], 1.0)
            dve.memset(gates[:, :, :], 0.0)
            dve.memset(qmask[:, :, :, :], 0.0)
            dve.wait_ge(S("cst_in"), 16)
            dve.tensor_copy(bf_cum[:, 0, :], C("cum"))
            dve.tensor_copy(bf_cum[:, 1, :], C("ones"))
            dve.drain()
            dve.wait_ge(S("c_ps"), 1)
            dve.tensor_copy(CT[:, :, :], bank[2][:, 0:KD * (DEC + 1)].rearrange("p (k r) -> p k r", k=KD)).then_inc(S("c_t"), 1)
            dve.wait_ge(S("bmod_in"), 16)
            for n in range(12):
                dve.wait_ge(S("mod_mm"), n + 1)
                one = 1.0 if n in (2, 3, 8, 9) else 0.0
                STT(MODV[:, n * NB:(n + 1) * NB], bank[n % 2][0:DEC + 1, :], one, BMOD[:, n * NB:(n + 1) * NB],
                    ALU.add, ALU.add).then_inc(S("mod_ev"), 1)

            dve.wait_ge(S("x_in"), 32)
            dve.wait_ge(S("const_in"), 16 * N_CONST)
            modulated(0)
            si = 0
            for hp in range(2):
                for i in range(2 * TILES):
                    g = hp * 2 * TILES + i
                    isk, t = divmod(i, TILES)
                    R = rows(t)
                    dve.wait_ge(S("ret_ev"), hp * 6 * TILES + i + 1)
                    if g:
                        dve.wait_ge(S("qk_ps"), g)
                    dst = KN[:, t, :] if isk and t < NT else RO
                    x4 = RT[0:R, :].rearrange("p (a d) -> p a d", d=P)
                    x2 = RT[0:R, :].rearrange("p (h a d) -> p h a d", a=2, d=P)
                    d2 = dst[0:R, :].rearrange("p (h a d) -> p h a d", a=2, d=P)
                    t2 = T1[0:R, :].rearrange("p (h a d) -> p h a d", a=2, d=P)
                    cc = rotc[0:R, 0:1, t, :]
                    ss = rotc[0:R, 1:2, t, :].to_broadcast([R, 2, P])
                    TT(T1[0:R, :].rearrange("p (a d) -> p a d", d=P), x4, cc.to_broadcast([R, 4, P]), ALU.mult)
                    TT(d2[:, :, 0, :], x2[:, :, 1, :], ss, ALU.mult)
                    TT(d2[:, :, 1, :], x2[:, :, 0, :], ss, ALU.mult)
                    dve.drain()
                    TT(d2[:, :, 0, :], t2[:, :, 0, :], d2[:, :, 0, :], ALU.subtract)
                    TT(d2[:, :, 1, :], t2[:, :, 1, :], d2[:, :, 1, :], ALU.add).then_inc(S("ro_rdy"), 1)
                    dve.drain()

                def decay_att(i):
                    rc = hp * 2 * NT + i
                    h = 2 * hp + i // NT
                    dve.wait_ge(S("att_ps"), rc + 1)
                    if rc >= 2:
                        dve.wait_ge(S("o_ps"), rc - 1)
                    STT(att[:, rc % 2, :], bank[3 + rc % 2][:, 0:P], float(GAMMA[h] ** -CH), C("tri"), ALU.mult, ALU.mult)\
                        .then_inc(S("att_rdy"), 1)

                decay_att(0)
                for i in range(2 * NT):
                    hh, c = divmod(i, NT)
                    rc = hp * 2 * NT + i
                    if i + 1 < 2 * NT:
                        decay_att(i + 1)
                    dve.wait_ge(S("u_ps"), rc + 1)
                    if c == 0 and hp:
                        dve.wait_ge(S("rp_st"), 32)
                    for j in range(2):
                        st = STATE[:, hh, j, :]
                        if c == 0:
                            last = dve.tensor_copy(st, bank[6 + j][:, :])
                        else:
                            last = STT(st, st, float(GAMMA[2 * hp + hh] ** CH), bank[6 + j][:, :], ALU.mult, ALU.add)
                    last.then_inc(S("s_rdy"), 1)
                    dve.drain()
                for b in range(DEC):
                    dve.tensor_copy(qmask[:, b, :, b], QT[:, :, SEQ + b])
                dve.drain()
                dve.engine_nop().then_inc(S("qm_rdy"), 1)
                for i in range(2 * DEC):
                    si = 2 * DEC * hp + i
                    b, hh = divmod(i, 2)
                    dve.wait_ge(S("vb_ps"), si + 1)
                    dve.wait_ge(S("st_dec"), si + 1)
                    st = slot(("state", hp, b // 2))
                    for j in range(2):
                        sj = st[:, 4 * (b % 2) + 2 * hh + j, :]
                        last = STT(sj, bank[2 + si % 2][:, :], KT[:, 2 * hh + j, SEQ + b:SEQ + b + 1], sj, ALU.mult, ALU.add)
                    last.then_inc(S("st_upd"), 1)
                dve.wait_ge(S("o_ev"), 2 * NT * (hp + 1))
                dve.wait_ge(S("os_ev"), 2 * (hp + 1))
                for hh in range(2):
                    for t in range(TILES):
                        R = rows(t)
                        dve.bn_stats(gnst[0:R, t, :], V[0:R, t, hh * NB:(hh + 1) * NB])
                    dve.drain()
                    for t in range(TILES):
                        last = dve.bn_aggr(gnmv[0:rows(t), hh, t, :], gnst[0:rows(t), t, :])
                    dve.drain()
                dve.engine_nop().then_inc(S("gn_var"), 1)
                dve.wait_ge(S("gn_sd"), hp + 1)
                dve.reciprocal(gnrs[:, :, :], gnsd[:, :, :])
                dve.drain()
                dve.wait_ge(S("gn_in"), 16 * (hp + 1))
                for i in range(2 * TILES):
                    hh, t = divmod(i, TILES)
                    R = rows(t)
                    vv = V[0:R, t, hh * NB:(hh + 1) * NB]
                    TS(vv, vv, gnmv[0:R, hh, t, 0:1], gnrs[0:R, hh, t:t + 1], ALU.subtract, ALU.mult)
                    dve.drain()
                    TT(vv, vv, GNB[0:R, hh * NB:(hh + 1) * NB], ALU.mult)
                    dve.drain()
                    dve.wait_ge(S("ret_ev"), hp * 6 * TILES + 4 * TILES + i + 1)
                    TT(vv, vv, SG[i % 2][0:R, :], ALU.mult).then_inc(S("y_rdy"), 1)
            mixer_close(0)

            def route(l):
                D_ = dve.drain
                flat = lambda v: v.rearrange("p t e -> p (t e)")
                dve.memset(LG, 0.0)
                D_()
                dve.wait_ge(S(f"lg_mm{l}"), TILES)
                pl = bank[0][:, 0:TILES * NE].rearrange("p (t e) -> p t e", e=NE)
                b4 = br[:, :].rearrange("p (o e) -> p o e", o=1)
                TT(LG[:, 0:NT, :], pl[:, 0:NT, :], b4.to_broadcast([P, NT, NE]), ALU.add)
                TT(LG[0:DEC, NT, :], pl[0:DEC, NT, :], br[0:DEC, :], ALU.add)
                D_()
                sp3 = lambda v: v.rearrange("p (t o) -> p t o", o=1).to_broadcast([P, TILES, NE])
                dve.tensor_reduce(r1, LG, AX.X, ALU.max)
                D_()
                TT(LG, LG, sp3(r1), ALU.subtract).then_inc(S(f"lg_sub{l}"), 1)
                dve.wait_ge(S(f"lg_exp{l}"), 1)
                dve.tensor_reduce(r1, PR, AX.X, ALU.add)
                D_()
                dve.reciprocal(r2, r1)
                D_()
                TT(PR, PR, sp3(r2), ALU.mult)
                D_()
                g4 = PR.rearrange("p t (g e) -> p (t g) e", e=EPG)
                for at, d_ in ((0, 1), (3, 2), (5, 3)):
                    TT(PAIRS[:, :, at:at + EPG - d_], g4[:, :, 0:EPG - d_], g4[:, :, d_:EPG], ALU.add)
                D_()
                dve.tensor_reduce(GS.rearrange("p t g -> p (t g)"), PAIRS, AX.X, ALU.max)
                D_()
                dve.tensor_reduce(r1, GS, AX.X, ALU.max)
                D_()
                sg = lambda v: v.rearrange("p (t o) -> p t o", o=1).to_broadcast([P, TILES, NG])
                TT(GQ, GS, sg(r1), ALU.is_equal)
                D_()
                TT(GK, GQ, C("w4").rearrange("p (o g) -> p o g", o=1).to_broadcast([P, TILES, NG]), ALU.mult)
                D_()
                dve.tensor_reduce(r1, GK, AX.X, ALU.max)
                D_()
                TT(GQ, GK, sg(r1), ALU.is_equal)
                D_()
                gq = GQ.rearrange("p t (g o) -> p (t g) o", o=1).to_broadcast([P, TILES * NG, EPG])
                pm = PM.rearrange("p t (g e) -> p (t g) e", e=EPG)
                TT(pm, g4, gq, ALU.mult)
                D_()
                TT(pm, pm, gq, ALU.add)
                D_()
                TS(PM, PM, -1.0, None, ALU.add)
                D_()
                w16 = C("w16").rearrange("p (o e) -> p o e", o=1).to_broadcast([P, TILES, NE])
                for k, (Sk, rk) in enumerate(((S1, r3), (S2, r4))):
                    dve.tensor_reduce(rk, PM, AX.X, ALU.max)
                    D_()
                    TT(EQ, PM, sp3(rk), ALU.is_equal)
                    D_()
                    TT(KEY, EQ, w16, ALU.mult)
                    D_()
                    dve.tensor_reduce(r1, KEY, AX.X, ALU.max)
                    D_()
                    TT(Sk, KEY, sp3(r1), ALU.is_equal)
                    D_()
                    if k == 0:
                        STT(PM.rearrange("p t e -> p (t e)"), Sk.rearrange("p t e -> p (t e)"), -4.0,
                            PM.rearrange("p t e -> p (t e)"), ALU.mult, ALU.add)
                        D_()
                for Sk, rk in ((S1, r3), (S2, r4)):
                    TT(EQ, PR, Sk, ALU.mult)
                    D_()
                    dve.tensor_reduce(rk, EQ, AX.X, ALU.add)
                    D_()
                TT(r1, r3, r4, ALU.add)
                D_()
                dve.reciprocal(r2, r1)
                D_()
                TT(gates[:, 0, :], r3, r2, ALU.mult)
                TT(gates[:, 1, :], r4, r2, ALU.mult)
                va = C("valid").rearrange("p (t o) -> p t o", o=1).to_broadcast([P, TILES, NE])
                TT(EQ, S1, S2, ALU.add)
                D_()
                TT(mb[:, :, :], EQ, va, ALU.mult).then_inc(S(f"marks{l}"), 1)
                dve.wait_ge(S(f"rank_mm{l}"), 1)
                rk = bank[1][:, 0:(TILES + 1) * NE].rearrange("p (t e) -> p t e", e=NE)
                dve.tensor_copy(cntv, rk[:, TILES, :])
                D_()
                blk = C("blk").rearrange("p (o j) -> p o j", o=1).to_broadcast([P, NE, MAXB])
                bg = big.rearrange("p i e -> p (i e)")[:, 0:NE * MAXB].rearrange("p (e j) -> p e j", j=MAXB)
                TT(bg, cntv.rearrange("p (e o) -> p e o", o=1).to_broadcast([P, NE, MAXB]), blk, ALU.is_gt)
                D_()
                dve.tensor_reduce(nbk, bg, AX.X, ALU.add)
                D_()
                TS(nbk, nbk, -1.0, 0.0, ALU.add, ALU.max)
                D_()
                dve.tensor_tensor_scan(cum, C("ones")[:, 0:NE], nbk, 0.0, ALU.mult, ALU.add)
                D_()
                TT(sta, cum, nbk, ALU.subtract)
                D_()
                STT(sta, sta, float(NE - 1), C("e"), ALU.add, ALU.subtract)
                rr = rk[:, 0:TILES, :]
                TS(KEY, rr, float(P), None, ALU.is_ge)
                D_()
                TT(EQ, KEY, sta.rearrange("p (o e) -> p o e", o=1).to_broadcast([P, TILES, NE]), ALU.mult)
                for b_ in range(2, MAXB):
                    STT(flat(KEY), bank[1][:, 0:TILES * NE], float(b_ * P), flat(KEY), ALU.is_ge, ALU.add)
                    D_()
                STT(flat(DST), bank[1][:, 0:TILES * NE], float(ITEMS), flat(EQ), ALU.mult, ALU.add)
                D_()
                STT(flat(DST), flat(KEY), float(1 - P * ITEMS), flat(DST), ALU.mult, ALU.add)
                D_()
                TT(DST, DST, C("e").rearrange("p (o e) -> p o e", o=1).to_broadcast([P, TILES, NE]), ALU.add)
                D_()
                for k, Sk in enumerate((S1, S2)):
                    TT(EQ, DST, Sk, ALU.mult)
                    D_()
                    dve.tensor_reduce(r1, EQ, AX.X, ALU.add)
                    D_()
                    dve.tensor_copy(dest_i[:, k, :], r1)
                    D_()
                W_ = ITEMS - NE + 2
                TT(big, C("item").rearrange("p (i o) -> p i o", o=1).to_broadcast([P, W_, NE]),
                   cum.rearrange("p (o e) -> p o e", o=1).to_broadcast([P, W_, NE]), ALU.is_ge)
                D_()
                dve.tensor_reduce(itf, big, AX.X, ALU.add)
                D_()
                TS(itf, itf, float(NE - 1), None, ALU.min)
                dve.tensor_copy(eid_i[:, 0:NE], C("e"))
                D_()
                dve.tensor_copy(eid_i[:, NE:], itf)
                PW = (ITEMS - NE) // 2
                b2 = big.rearrange("p i e -> p (i e)")[:, 0:PW]
                TT(b2, C("pair")[:, 0:PW], cum[:, NE - 1:NE].to_broadcast([P, PW]), ALU.is_lt)
                D_()
                dve.tensor_reduce(r1[:, 0:1], b2, AX.X, ALU.add)
                D_()
                TS(r1[:, 0:1], r1[:, 0:1], float(NE // 2 - 1), None, ALU.add)
                D_()
                dve.tensor_copy(np_i[:, l:l + 1], r1[:, 0:1])
                D_()
                dve.engine_nop().then_inc(S(f"tables{l}"), 1)

            def experts(l):
                m = 2 * l + 1
                modulated(m)
                route(l)

                def low(i, u):
                    dve.wait_ge(S("hi_rdy"), i * len(UNITS) + (u + 1))
                    TT(WL[:, u % SPLIT, :, :], raw(u % RAW), WH[:, u % SPLIT, :, :].bitcast(F32), ALU.subtract)\
                        .then_inc(S("lo_rdy"), 1)

                first = pairs_before(dve, l)
                for u in range(SPLIT):
                    low(first, u)
                first, last = pairs(dve, l)

                def take_rows(j, i):
                    for g in range(2):
                        dve.wait_ge(S(f"hg_hi{j}"), 2 * i + (g + 1))
                        TT(HGL[:, j, 4 * g:4 * g + 4, :], bank[2 * j + g][:, :].rearrange("p (q r) -> p q r", r=P),
                           HGH[:, j, 4 * g:4 * g + 4, :].bitcast(F32), ALU.subtract).then_inc(S(f"hg_lo{j}"), 1)

                def pair(i, end):
                    def used(u):
                        dve.wait_ge(S("unit_used"), i * len(UNITS) + (UNIT0 + u + 1))

                    def act_times_up(j, u):
                        dve.wait_ge(S(f"sg{j}"), i + 1)
                        used(u)
                        TT(AE, SGE, bank[5 + 2 * j][:, :], ALU.mult).then_inc(S(f"a_rdy{j}"), 1)

                    def take_a(j):
                        dve.wait_ge(S(f"at_hi{j}"), i + 1)
                        TT(ATL[:, j, :, :], bank[2 * j][:, :].rearrange("p (q r) -> p q r", r=P),
                           ATH[:, j, :, :].bitcast(F32), ALU.subtract).then_inc(S(f"at_lo{j}"), 1)

                    def take_y(j, u):
                        used(u)
                        dve.wait_ge(S(f"y_st{j}"), (i + 1) * 16)
                        dve.tensor_copy(Y[j][:, 0:NB], bank[4 + 2 * j][:, :]).then_inc(S(f"y_ev_d{j}"), 1)

                    for u in range(SPLIT, SPLIT + len(UNITS)):
                        if u == 7:
                            act_times_up(0, 3)
                        if u == 11:
                            act_times_up(1, 7)
                        if not end or u < len(UNITS):
                            low(i, u)
                        if u == 5:
                            take_rows(1, i)
                        if u == 9:
                            take_a(0)
                        if u == 12:
                            take_a(1)
                        if u == 13:
                            if not end:
                                take_rows(0, i + 1)
                            take_y(0, 9)
                        if u == 15:
                            take_y(1, 11)

                take_rows(0, first)
                with dve.Fori(0, last) as k:
                    pair(first + k, False)
                pair(first + last, True)
                dve.wait_ge(S("ep_in"), 64 * m + 64)
                for t in range(TILES):
                    R = rows(t)
                    y1, y2 = (YG[t % 2][k][0:R, :] for k in range(2))
                    gt = (BC if t < NT else SC)[0:R, 0, :]
                    dve.wait_ge(S(f"yg_in{t % 2}"), 32 * (l * tiles_of[t % 2] + t // 2 + 1))
                    TS(y1, y1, gates[0:R, 0, t:t + 1], None, ALU.mult)
                    dve.drain()
                    STT(y1, y2, gates[0:R, 1, t:t + 1], y1, ALU.mult, ALU.add)
                    dve.drain()
                    TT(y1, y1, gt, ALU.mult)
                    dve.drain()
                    STT(X[0:R, t, :], X[0:R, t, :], ALPHA, y1, ALU.mult, ALU.add).then_inc(S(f"cmb{l}"), 1)
                norm(m)

            experts(0)

            modulated(2)
            for i in range(6 * TILES):
                n, t = divmod(i, TILES)
                R = rows(t)
                dve.wait_ge(S("d_ev"), i + 1)
                nh, w, rot, src, cn, sn = ((4, HD, ROT, DRT[i % 2], "dcos", "dsin"), (4, HD, ROT, DRT[i % 2], "dcos", "dsin"),
                                           (KVH, HD, ROT, KV[:, t, :], "dcos", "dsin"),
                                           (8, ID, IROT, DRT[i % 2], "icos", "isin"), (8, ID, IROT, DRT[i % 2], "icos", "isin"),
                                           (1, ID, IROT, KIW[:, t, :], "icos", "isin"))[n]
                hf = rot // 2
                xv = src[0:R, 0:nh * w].rearrange("p (h d) -> p h d", d=w)
                x1, x2 = xv[:, :, 0:hf], xv[:, :, hf:rot]
                tb = lambda nm: C(nm)[0:R, t * hf:(t + 1) * hf].rearrange("p (o d) -> p o d", o=1).to_broadcast([R, nh, hf])
                rx = [RX[0:R, k, 0:nh * hf].rearrange("p (h d) -> p h d", d=hf) for k in range(4)]
                TT(rx[0], x1, tb(cn), ALU.mult)
                TT(rx[1], x2, tb(sn), ALU.mult)
                TT(rx[2], x1, tb(sn), ALU.mult)
                TT(rx[3], x2, tb(cn), ALU.mult)
                dve.drain()
                TT(x1, rx[0], rx[1], ALU.subtract)
                last = TT(x2, rx[2], rx[3], ALU.add)
                if n == 5:
                    dve.drain()
                    for c in range(2):
                        dve.tensor_copy(KID[0:R, t, c * ID:(c + 1) * ID], KIW[0:R, t, 0:ID])
                    last = TS(WI[0:R, t, :], KIW[0:R, t, ID:ID + IH], IH ** -0.5, None, ALU.mult)
                last.then_inc(S("d_rot"), 1)
                dve.drain()
            ix = 0
            for t in range(NT):
                L = (t + 1) * P
                if t == 0:
                    dve.tensor_copy(BIAS[:, 0:P], C("cbias"))
                else:
                    for h in range(IH):
                        dve.wait_ge(S("ix_rl"), ix + 1)
                        if h == 0:
                            TS(SCORE[:, 0:L], RL[ix % 2][:, 0:L], WI[:, t, 0:1], None, ALU.mult).then_inc(S("ix_acc"), 1)
                        else:
                            STT(SCORE[:, 0:L], RL[ix % 2][:, 0:L], WI[:, t, h:h + 1], SCORE[:, 0:L], ALU.mult, ALU.add)\
                                .then_inc(S("ix_acc"), 1)
                        dve.drain()
                        ix += 1
                    TT(SCORE[:, t * P:L], SCORE[:, t * P:L], C("cbias"), ALU.add)
                    dve.drain()
                    for r in range(TOPK_P // 8):
                        dve.max(m8[:, :], SCORE[:, 0:L])
                        dve.drain()
                        dve.match_replace(out=SCORE[:, 0:L], in_to_replace=m8[:, :], in_values=SCORE[:, 0:L], imm_value=GONE)
                        dve.drain()
                    TS(BIAS[:, 0:L], SCORE[:, 0:L], -2.0e38, NEG, ALU.is_gt, ALU.mult)
                dve.drain()

                def normed(h):
                    a = t * QH + h
                    dve.wait_ge(S("e_rdy"), a + 1)
                    dve.reciprocal(ersum[:, a % 2:a % 2 + 1], esum[:, a % 2:a % 2 + 1])
                    dve.drain()
                    TS(E[a % 2][:, 0:L], E[a % 2][:, 0:L], ersum[:, a % 2:a % 2 + 1], None, ALU.mult).then_inc(S("p_rdy"), 1)

                for s in range(QH + 1):
                    if s < QH:
                        a = t * QH + s
                        dve.wait_ge(S("lg_ps"), a + 1)
                        if a >= 2:
                            dve.wait_ge(S("pt_ps"), a - 1)
                        dve.tensor_tensor_reduce(out=E[a % 2][:, 0:L], in0=bank[2 + a % 2][:, 0:L], in1=BIAS[:, 0:L],
                                                 scale=1.0, scalar=GONE, op0=ALU.add, op1=ALU.max,
                                                 accum_out=mx[:, a % 2:a % 2 + 1]).then_inc(S("lg_ev"), 1)
                        dve.drain()
                        TS(nbias[:, a % 2:a % 2 + 1], mx[:, a % 2:a % 2 + 1], -(HD ** -0.5), None, ALU.mult)\
                            .then_inc(S("nb_rdy"), 1)
                    if s:
                        normed(s - 1)
            dve.wait_ge(S("ot_ev"), NT * QH)
            dve.wait_ge(S("w_t"), 1)
            dve.wait_ge(S("mask_zero"), 2)
            for b in range(DEC):
                dve.tensor_copy(WM[:, :, b, b], bank[0][0:DEC, 0:2 * DEC].rearrange("p (c b) -> p c b", c=2)[:, :, b])
                for n in range(KVH):
                    dve.tensor_copy(QM[:, b, n, b * GRP:(b + 1) * GRP], DQT[:, n * GRP:(n + 1) * GRP, SEQ + b])
            dve.drain()
            dve.engine_nop().then_inc(S("wm_rdy"), 1)
            for b in range(DEC):
                if b >= 2:
                    dve.wait_ge(S("s_dot"), b - 1)
                dve.tensor_copy(KIBT[b % 2][:, PAST:LS], KIT[:, SEQ + b:SEQ + b + 1]).then_inc(S("ki_rdy"), 1)
                last = dve.tensor_copy(KBT[:, b, :, PAST], DKT[:, :, SEQ + b])
            last.then_inc(S("kn_rdy"), 1)
            dve.wait_ge(S("s_sc"), DEC)
            dve.tensor_copy(SCS, bank[6][0:DEC, 0:LS])
            dve.drain()
            for r in range(TOPK_S // 8):
                dve.max(m8[0:DEC, :], SCS)
                dve.drain()
                dve.match_replace(out=SCS, in_to_replace=m8[0:DEC, :], in_values=SCS, imm_value=GONE)
                dve.drain()
            TS(BIS, SCS, -2.0e38, NEG, ALU.is_gt, ALU.mult).then_inc(S("s_bias"), 1)
            r = DEC * GRP
            for n in range(KVH):
                dve.wait_ge(S("s_lg"), n + 1)
                dve.tensor_copy(PS[n][:, :], bank[n][0:r, 0:LS])
                dve.drain()
                dve.tensor_reduce(mx[0:r, n:n + 1], PS[n][:, :], AX.X, ALU.max)
                dve.drain()
                TS(nbias[0:r, n:n + 1], mx[0:r, n:n + 1], -(HD ** -0.5), None, ALU.mult).then_inc(S("s_nb"), 1)
            for n in range(KVH):
                dve.wait_ge(S("s_e"), n + 1)
                dve.reciprocal(ersum[0:r, n:n + 1], esum[0:r, n:n + 1])
                dve.drain()
                TS(PS[n][:, :], PS[n][:, :], ersum[0:r, n:n + 1], None, ALU.mult)
                dve.drain()
                TS(DG[:, n, :], ident[0:r, 0:r], PS[n][:, PAST:LS], None, ALU.mult).then_inc(S("s_p"), 1)
            mixer_close(2)
            experts(1)


_OUTS = [("y_prompt", (1, SEQ, D)), ("y_sample", (DEC, 1, D)), ("ret_prompt", (1, 1, RH, RDK, RDV)),
         ("ret_sample", (1, DEC, RH, RDK, RDV)), ("k_prompt", (1, 1, SEQ, KVH, HD)), ("v_prompt", (1, 1, SEQ, KVH, HD)),
         ("kidx_prompt", (1, 1, SEQ, ID)), ("k_sample", (1, DEC, 1, KVH, HD)), ("v_sample", (1, DEC, 1, KVH, HD)),
         ("kidx_sample", (1, DEC, 1, ID))]


def kernel(**inputs):
    import concourse.bacc as _bacc
    from concourse.bass_utils import run_bass_kernel_spmd as _run

    nc = _bacc.Bacc("TRN2", target_bir_lowering=False, num_devices=1)
    cst, rotc, tok = constants()
    arrays, args = {}, {}
    for name, a in list(inputs.items()) + [("cst", cst), ("rotc", rotc), ("tok", tok)]:
        a = np.ascontiguousarray(a)
        arrays["in_" + name] = a
        args[name] = nc.dram_tensor("in_" + name, a.shape, mybir.dt.from_np(a.dtype), kind="ExternalInput").ap()
    outs = {name: nc.dram_tensor("out_" + name, shape, F32, kind="ExternalOutput").ap() for name, shape in _OUTS}
    trunk(nc, args, outs)
    r = _run(nc, [arrays], core_ids=[0])
    return tuple(r.results[0]["out_" + name] for name, _ in _OUTS)
```

```python
import math
from contextlib import ExitStack

import numpy as np

import concourse.bass as bass
from concourse import mybir

F32 = mybir.dt.float32
BF16 = mybir.dt.bfloat16
I32 = mybir.dt.int32
F32R = mybir.dt.float32r
ALU = mybir.AluOpType
ACT = mybir.ActivationFunctionType
AX = mybir.AxisListType

P = 128
D = 1024
KD = D // P
SEQ, DEC = 512, 8
NT = SEQ // P
TOK = SEQ + DEC
TILES = NT + 1
DEPTH = 2
ALPHA = (2.0 * DEPTH) ** 0.25
LN_EPS, GN_EPS = 1e-5, 1e-6
NB = 512

RH, RDK, RDV = 4, 256, 512
CH = 128
GAMMA = [1.0 - 2.0 ** (-5.0 - h) for h in range(RH)]

QH, KVH, HD = 8, 2, 128
GRP = QH // KVH
IH, ID = 16, 64
DSA_IN = QH * HD + 2 * KVH * HD + IH * ID + ID + IH
LAG = 3
TOPK_P = min(256, SEQ // 4)
PAST, PAGE = 256, 128
NPG = PAST // PAGE
TOPK_S = min(256, (PAST + 1) // 4)
LS = PAST + 1
ROT, IROT = HD // 4, ID // 4
NEG = -1.0e30
GONE = -3.0e38

NE, NG, EPG = 16, 4, 4
FE = 512
MAXB = -(-TOK // P)
ITEMS = 24
assert ITEMS >= NE + (2 * TOK) // P and ITEMS % 2 == 0

MOD_AHEAD = 9
N_CONST = 4

_cols = {}
_at = 0
for _n, _w in (("ident", P), ("tri", P), ("cum", P), ("ones", P), ("cbias", P), ("qs", TILES * RH),
               ("ks", TILES * RH), ("item", ITEMS - NE + 2), ("blk", MAXB), ("pair", ITEMS // 2), ("w4", NG),
               ("w16", NE), ("e", NE), ("valid", TILES), ("dcos", TILES * ROT // 2), ("dsin", TILES * ROT // 2),
               ("icos", TILES * IROT // 2), ("isin", TILES * IROT // 2), ("bexp", DEC * GRP),
               ("bsel", DEC), ("lneps", 1), ("gneps", 1)):
    _cols[_n] = (_at, _w)
    _at += _w
CST_W = _at


def constants():
    f = np.float32
    cst = np.zeros((P, CST_W), f)

    def put(name, a):
        o, w = _cols[name]
        cst[:a.shape[0], o:o + w] = a.reshape(a.shape[0], w)

    i = np.arange(P)
    put("ident", np.eye(P, dtype=f))
    put("tri", (i[None, :] >= i[:, None]).astype(f))
    put("cum", (i[:, None] < i[None, :]).astype(f))
    put("ones", np.ones((P, P), f))
    put("cbias", np.where(i[None, :] <= i[:, None], 0.0, NEG).astype(f))
    lg = np.log(f(1.0) - np.power(f(2.0), f(-5.0) - np.arange(RH, dtype=f))).astype(f)
    qs = np.ones((P, TILES, RH), f)
    ks = np.full((P, TILES, RH), RDK ** -0.5, f)
    qs[:, :NT] = np.exp(lg[None, :] * (i[:, None] + 1.0).astype(f))[:, None]
    ks[:, :NT] = (np.exp(lg[None, :] * (CH - 1.0 - i)[:, None].astype(f)) * f(RDK ** -0.5))[:, None]
    put("qs", qs)
    put("ks", ks)
    row = lambda v: np.tile(np.asarray(v, f)[None, :], (P, 1))
    put("item", row(np.arange(ITEMS - NE + 2)))
    put("blk", row(np.arange(MAXB) * P))
    put("pair", row(2 * np.arange(ITEMS // 2)))
    put("w4", row(NG - np.arange(NG)))
    put("w16", row(NE - np.arange(NE)))
    put("e", row(np.arange(NE)))
    valid = np.ones((P, TILES), f)
    valid[DEC:, NT] = 0
    put("valid", valid)
    pos = np.zeros((P, TILES), f)
    pos[:, :NT] = (np.arange(NT) * P)[None, :] + i[:, None]
    pos[:, NT] = PAST

    def table(inv):
        ang = (pos[:, :, None] * inv.astype(f)[None, None, :]).astype(f)
        return np.cos(ang).astype(f), np.sin(ang).astype(f)

    theta = f(500000.0)
    for c, s, rot in (("dcos", "dsin", ROT), ("icos", "isin", IROT)):
        co, si = table(f(1.0) / (theta ** (np.arange(0, rot, 2, dtype=f) / f(rot))))
        put(c, co)
        put(s, si)
    bexp = np.zeros((DEC, DEC * GRP), f)
    for b in range(DEC):
        bexp[b, b * GRP:(b + 1) * GRP] = 1
    put("bexp", bexp)
    bsel = np.zeros((DEC * GRP, DEC), f)
    bsel[np.arange(DEC * GRP), np.arange(DEC * GRP) // GRP] = 1
    put("bsel", bsel)
    put("lneps", np.full((P, 1), LN_EPS, f))
    put("gneps", np.full((P, 1), GN_EPS, f))
    inv = np.power(f(10000.0), -np.linspace(0.0, 1.0, RDK // 2, dtype=f)).astype(f)
    rc, rs = table(inv)
    rot = np.stack([rc, rs], 1)
    tok = np.zeros((P, TILES), np.int32)
    tok[:, :] = (np.arange(TILES) * P)[None, :] + i[:, None]
    return cst, np.ascontiguousarray(rot), tok


def rows(t):
    return P if t < NT else DEC


def cols(t):
    return slice(t * P, t * P + rows(t))


def trunk(nc, A, O):
    ctx = ExitStack()
    with ctx:
        sems = {}

        def S(name):
            if name not in sems:
                sems[name] = ctx.enter_context(nc.semaphore(name))
            return sems[name]

        def sb(name, shape, dt=F32):
            return ctx.enter_context(nc.sbuf_tensor(name, shape, dt))

        def dram(name, shape, dt=F32):
            return nc.dram_tensor(name, shape, dt, kind="Internal").ap()

        bank = [ctx.enter_context(nc.psum_tensor(f"bank{i}", [P, NB], F32)) for i in range(8)]

        mod_d = dram("mod_d", (DEPTH, DEC + 1, 6 * D))
        h_d = dram("h_d", (TOK, D))
        slot_d = dram("slot_d", (P * ITEMS, 1), I32)
        y_d = dram("y_d", (P * ITEMS, D))
        y_items = y_d.rearrange("(p i) d -> p i d", i=ITEMS)

        X = sb("X", [P, TILES, D])
        HT_AT = nc.sbuf_base
        HT = sb("HT", [P, KD, TOK])
        RING = sb("RING", [P, 3, KD * NB])
        MWORDS = 21504
        M_AT = nc.sbuf_base
        M = sb("M", [P, MWORDS])
        BC = sb("BC", [P, 3, D])
        SC_AT = nc.sbuf_base
        SC = sb("SC", [DEC, 2, D])
        cst = sb("cst", [P, CST_W])
        rotc = sb("rotc", [P, 2, TILES, P])
        tok = sb("tok", [P, TILES], I32)
        zero_i = sb("zero_i", [P, ITEMS], I32)
        bf_cum = sb("bf_cum", [P, 2, P], BF16)
        wr = sb("wr", [P, KD, NE])
        br = sb("br", [P, NE])
        lnst = sb("lnst", [P, TILES, 2, 6])
        lnmv = sb("lnmv", [P, TILES, 2])
        lnsd = sb("lnsd", [P, TILES])
        lnrs = sb("lnrs", [P, TILES])
        gates = sb("gates", [P, 2, TILES])
        dest_i = sb("dest_i", [P, 2, TILES], I32)
        eid_i = sb("eid_i", [P, ITEMS + 2], I32)
        np_i = sb("np_i", [P, DEPTH], I32)
        slot_i = sb("slot_i", [P, ITEMS], I32)
        slot_c = sb("slot_c", [P, 2], I32)
        dest_c = sb("dest_c", [P, 2, TILES], I32)
        primer = sb("primer", [P, 2], I32)
        ptab = sb("ptab", [1, DEC * NPG], I32)

        def C(name, r=P):
            o, w = _cols[name]
            return cst[0:r, o:o + w]

        def view(off, *shape, r=P, region=None):
            n = int(np.prod(shape))
            assert off + n <= MWORDS
            v = M[0:r, off:off + n]
            if len(shape) == 1:
                return v
            names = "abcd"[:len(shape)]
            return v.rearrange(f"p ({' '.join(names)}) -> p {' '.join(names)}",
                               **{k: s for k, s in zip(names[1:], shape[1:])})

        ident = C("ident")

        stream, state_uses = [], [0] * 3
        for n in range(12):
            stream.append((("mod", 0, n), [("mod_mm", n + 1)]))
        for hp in range(2):
            ret = lambda i: [("ret_mm", (6 * hp + i + 1) * TILES)]
            stream += [(("q", hp), ret(0)), (("k", hp), ret(1)), (("v", hp, 0), ret(2)), (("v", hp, 1), ret(3))]
            for b2 in range(4):
                n = 4 * hp + b2 + 1
                s = len(stream) % 3
                state_uses[s] += 1
                stream.append((("state", hp, b2), [("os_mm", 4 * n), (f"state_st{s}", 32 * state_uses[s])]))
            stream += [(("g", hp, 0), ret(4)), (("g", hp, 1), ret(5))]
        for n in range(2):
            stream.append((("out0", n, 0), [("out_half0", TILES * (n + 1))]))
            stream.append((("out0", n, 1), [("out_mm0", TILES * (n + 1))]))
        for n in range(12):
            stream.append((("mod", 1, n), [("mod_mm", 12 + n + 1)]))
        N_FIRST = len(stream)
        for n in range(6):
            stream.append((("din", n), [("d_mm", TILES * (n + 1))]))
        stream += [(("ipg",), [("ki_t", DEC)]), (("kpg",), [("kk_t", 2 * DEC)]), (("vpg",), [("s_pv", KVH)])]
        for n in range(2):
            stream.append((("out2", n, 0), [("out_mm2", TILES * (n + 1))]))
        N_LOADS = {"state": 2, "kpg": DEC * NPG, "vpg": DEC * NPG, "ipg": 2 * DEC * NPG}
        place, brought = {}, [0] * 3
        for i, (key, _) in enumerate(stream):
            brought[i % 3] += 16 * N_LOADS.get(key[0], 1)
            place[key] = (i, i % 3, brought[i % 3])

        def slot(key, k=KD, n=NB):
            return RING[:, place[key][1], 0:k * n].rearrange("p (k n) -> p k n", n=n)

        def wait_slot(eng, key):
            eng.wait_ge(S(f"ring_full{place[key][1]}"), place[key][2])

        def d_bank(i):
            return bank[(0, 1, 4, 5)[i] if i < NT else i % 2]

        tiles_of = [(TILES + 1) // 2, TILES // 2]

        UNITS = [(j, w, h) for j, w in ((0, "w_gate"), (0, "w_up"), (1, "w_gate"), (1, "w_up"), (0, "w_down"),
                                        (1, "w_down")) for h in range(2)]
        RAW, SPLIT = 6, 4
        UW = 4 * NB
        UNIT0 = 8

        CROW = view(0, D, r=DEC + 1)
        CSIL = view(D, D, r=DEC + 1)
        BMOD = view(2 * D, 6 * D, r=DEC + 1)
        MODV = view(8 * D, 6 * D, r=DEC + 1)
        CT = sb("CT", [P, KD, DEC + 1])
        o = 0
        YT = view(o, 16, TOK)
        o += 16 * TOK
        QT = view(o, 4, TOK)
        KT = view(o + 4 * TOK, 4, TOK)
        o += 8 * TOK
        KN = view(o, NT, NB)
        o += NT * NB
        V = view(o, TILES, 2 * NB)
        o += TILES * 2 * NB
        RT, T1, RO = view(o, NB), view(o + NB, NB), view(o + 2 * NB, NB)
        SG = [RT, T1]
        MS1 = [BC[0:DEC + 1, :, :].rearrange("p a d -> p (a d)")[:, i * NB:(i + 1) * NB] for i in range(6)]
        SGATE = view(16 * TOK, D, r=DEC)
        GNB = BC[:, 0, :]
        STATE = BC[:, 1:3, :].rearrange("p h (j v) -> p h j v", j=2)
        ATT_AT = -(-nc.sbuf_base // 32) * 32
        att = sb("att", [P, 2, P])
        qmask = sb("qmask", [P, DEC, 4, DEC])
        gnst = sb("gnst", [P, TILES, 6])
        gnmv = sb("gnmv", [P, 2, TILES, 2])
        gnsd = sb("gnsd", [P, 2, TILES])
        gnrs = sb("gnrs", [P, 2, TILES])
        EPT = {0: RT, 2: view(0, NB)}

        o = NB
        DRT = [view(o, NB), view(o + NB, NB)]
        o += 2 * NB
        RX = view(o, 4, 64)
        o += 256
        DQT = view(o, QH, TOK)
        o += QH * TOK
        QIT = view(o, IH // 2, TOK)
        o += QH * TOK
        DKT = view(o, KVH, TOK)
        o += KVH * TOK
        KIT = view(o, TOK)
        o += TOK
        KV = view(o, TILES, 2 * KVH * HD)
        o += TILES * 2 * KVH * HD
        KIW = view(o, TILES, ID + IH)
        o += TILES * (ID + IH)
        KID = view(o, TILES, 2 * ID)
        o += TILES * 2 * ID
        WI = view(o, TILES, IH)
        o += TILES * IH
        o_late = o
        SCORE, BIAS = view(o, NB), [view(o + NB, NB), view(0, NB)]
        o += 2 * NB
        RL = [view(o, NB), view(o + NB, NB), *DRT]
        o += 2 * NB
        E = [view(o, NB), view(o + NB, NB),
             *[rotc[:, :, :, :].rearrange("p a t d -> p (a t d)")[:, i * NB:(i + 1) * NB] for i in range(2)]]
        o += 2 * NB
        PT = [view(o, NT, P), view(o + NB, NT, P)]
        o += 2 * NB
        m8 = sb("m8", [P, 8])
        mx = sb("mx", [P, 2])
        nbias = sb("nbias", [P, 2])
        esum = sb("esum", [P, 2])
        ersum = sb("ersum", [P, 2])
        OT = HT
        o = o_late
        KBT = view(o, DEC, KVH, LS)
        o += DEC * KVH * LS
        KIBT = [view(o, LS), view(o + LS, LS)]
        o += 2 * LS
        assert o <= MWORDS, o
        o = 0
        RLS = [view(0, 2, LS, r=DEC), view(2 * LS, 2, LS, r=DEC)]
        SCS, BIS = view(4 * LS, LS, r=DEC), view(5 * LS, LS, r=DEC)
        assert 6 * LS <= 3 * NB + 256
        QM_AT = -(-nc.sbuf_base // 32) * 32
        QM = sb("QM", [P, DEC, KVH, DEC * GRP])
        WM = sb("WM", [DEC, 2, DEC, DEC])
        PS = [sb(f"PS{n}", [DEC * GRP, LS]) for n in range(KVH)]
        PTS = sb("PTS", [P, KVH, NPG, DEC * GRP])
        PNW = sb("PNW", [DEC, KVH, DEC * GRP])
        DG = sb("DG", [DEC * GRP, KVH, DEC * GRP])

        def over(name, shape, dt, base, words):
            return nc.alloc_sbuf_tensor_at(name, shape, dt, offset=base + 4 * words)

        WH = over("WH", [P, SPLIT, 4, NB], F32R, M_AT, 0)
        WL = over("WL", [P, SPLIT, 4, NB], F32R, M_AT, SPLIT * UW)
        HGH = over("HGH", [P, 2, KD, P], F32R, HT_AT, 0)
        HGL = over("HGL", [P, 2, KD, P], F32R, HT_AT, 2 * D)
        o = 2 * SPLIT * UW
        HG = [view(o, D), rotc[:, :, :, :].rearrange("p a t d -> p (a t d)")[:, 0:D]]
        o += D
        SGE = view(o, FE)
        o += FE
        AE = view(o, FE)
        o += FE
        ATH = over("ATH", [P, 2, FE // P, P], F32R, M_AT, o)
        o += 2 * FE
        ATL = over("ATL", [P, 2, FE // P, P], F32R, M_AT, o)
        o += 2 * FE
        Y = [view(o, D), over("Y1", [P, D], F32, QM_AT, 0)]
        bias1 = over("bias1", [DEC + 1, 4, NB], F32, SC_AT, 0)
        SCALE_SHIFT = [HG[1], Y[1][:, :]]
        o += D
        assert o <= MWORDS, o
        HN = [view(2 * SPLIT * UW, D), view(2 * SPLIT * UW + D, D)]
        ro = [2 * SPLIT * UW + 2 * D]

        def rview(*shape):
            ro[0] += int(np.prod(shape))
            assert ro[0] <= MWORDS
            return view(ro[0] - int(np.prod(shape)), *shape)

        LG, PR, KEY, EQ, S1, S2, PM, DST = [rview(TILES, NE) for _ in range(8)]
        PAIRS = rview(TILES * NG, 6)
        GS, GK, GQ = [rview(TILES, NG) for _ in range(3)]
        r1, r2, r3, r4 = [rview(TILES) for _ in range(4)]
        cntv, nbk, cum, sta = [rview(NE) for _ in range(4)]
        big = rview(ITEMS - NE + 2, NE)
        itf = rview(ITEMS - NE + 2)
        mb = over("mb", [P, TILES, NE], BF16, ATT_AT, 0)
        YG = [[view((2 * b + k) * D, D) for k in range(2)] for b in range(2)]

        out_waits = [("rp_st", 16 * RH), *[(f"state_st{s}", 32 * state_uses[s]) for s in range(3)],
                     ("kv_st", 16 * 3 * TILES), ("y_out", 16 * TILES)]

        def pairs_before(eng, l):
            first = 0
            for k in range(l):
                first = first + (eng.value_load(np_i[0:1, k:k + 1], min_val=NE // 2 - 1, max_val=ITEMS // 2 - 1) + 1)
            return first

        def pairs(eng, l):
            return pairs_before(eng, l), eng.value_load(np_i[0:1, l:l + 1], min_val=NE // 2 - 1, max_val=ITEMS // 2 - 1)

        def raw(s):
            return RING[:, :, :].rearrange("p a w -> p (a w)")[:, s * UW:(s + 1) * UW].rearrange("p (k n) -> p k n", n=NB)

        def raw_count(i, u):
            return (i * (len(UNITS) // RAW) + u // RAW + 1) * 16

        block = ctx.enter_context(nc.Block())

        @block.sync
        def _(sp):
            def kpn(w, at, n):
                return w.rearrange("(k p) n -> p k n", p=P)[:, :, at:at + n]

            def wait_free(i):
                if i >= 3:
                    for name, v in stream[i - 3][1]:
                        sp.wait_ge(S(name), v)

            def load(key):
                i, s, _ = place[key]
                wait_free(i)
                kind = key[0]
                dst = slot(key)
                if kind == "state":
                    _, hp, b2 = key
                    for bb in range(2):
                        sp.dma_start(dst[:, 4 * bb:4 * bb + 4, :],
                                     A["state_ret"][0, 2 * b2 + bb, 2 * hp:2 * hp + 2]
                                     .rearrange("h (j p) v -> p (h j) v", p=P)).then_inc(S(f"ring_full{s}"), 16)
                    return
                if kind == "mod":
                    src = kpn(A["w_mod"][key[1]], key[2] * NB, NB)
                elif kind in ("q", "k"):
                    src = kpn(A["w_in_ret"][0], {"q": 0, "k": RH * RDK}[kind] + key[1] * NB, NB)
                elif kind in ("v", "g"):
                    at = {"v": 2 * RH * RDK, "g": 2 * RH * RDK + RH * RDV}[kind]
                    src = kpn(A["w_in_ret"][0], at + (2 * key[1] + key[2]) * NB, NB)
                elif kind == "out0":
                    src = kpn(A["w_out_ret"][0, key[2] * D:(key[2] + 1) * D, :], key[1] * NB, NB)
                elif kind == "out2":
                    src = kpn(A["w_out_dsa"][0], key[1] * NB, NB)
                else:
                    w = min(NB, DSA_IN - key[1] * NB)
                    src = kpn(A["w_in_dsa"][0], key[1] * NB, w)
                    dst = slot(key, KD, w)
                sp.dma_start(dst, src).then_inc(S(f"ring_full{s}"), 16)

            def load_pages(key):
                i, s, _ = place[(key,)]
                wait_free(i)
                src = A[{"kpg": "cache_k", "vpg": "cache_v", "ipg": "cache_kidx"}[key]]
                dst = RING[:, s, :]
                for i in range(DEC * NPG):
                    pg = sp.value_load(ptab[0:1, i:i + 1], min_val=0, max_val=src.shape[1] - 1)
                    if key == "ipg":
                        for c in range(2):
                            sp.dma_start(dst[:, i * P + c * ID:i * P + (c + 1) * ID],
                                         src[0, bass.ds(pg, 1)].rearrange("o t d -> (o t) d"))\
                                .then_inc(S(f"ring_full{s}"), 16)
                    else:
                        sp.dma_start(dst[:, i * KVH * HD:(i + 1) * KVH * HD],
                                     src[0, bass.ds(pg, 1)].rearrange("o t h d -> (o t) (h d)"))\
                            .then_inc(S(f"ring_full{s}"), 16)

            def load_unit(l, e, unit, s):
                _, w, h = unit
                src = A[w][l, e].rearrange("o (k p) n -> p (o k) n", p=P)
                src = src[:, :, h * NB:(h + 1) * NB] if w == "w_down" else src[:, 4 * h:4 * h + 4, :]
                sp.dma_start(raw(s), src).then_inc(S(f"raw_in{s}"), 16)

            def moe_loads(l):
                last = N_FIRST if l == 0 else len(stream)
                for u in range(RAW):
                    if u % 2 == 0:
                        wait_free(last + (u // 2 - last) % 3)
                    load_unit(l, slice(UNITS[u][0], UNITS[u][0] + 1), UNITS[u], u)
                sp.wait_ge(S("tables"), l + 1)
                first, last = pairs(sp, l)

                def pair(k, upto):
                    item = None
                    for u in range(RAW, upto):
                        unit = UNITS[u % len(UNITS)]
                        if item != (unit[0], u // len(UNITS)):
                            item = (unit[0], u // len(UNITS))
                            at = k * 2 + item[0] + 2 * item[1]
                            e = sp.value_load(eid_i[0:1, bass.ds(at, 1)], min_val=0, max_val=NE - 1)
                        sp.wait_ge(S("lo_rdy"), (first + k) * len(UNITS) + (UNIT0 + u - RAW + 1))
                        load_unit(l, bass.ds(e, 1), unit, u % RAW)

                with sp.Fori(0, last) as k:
                    pair(k, RAW + len(UNITS))
                pair(last, len(UNITS))
                if l == 0:
                    sp.wait_ge(S("lo_rdy"), (first + last) * len(UNITS) + (len(UNITS) + UNIT0))
                    load(stream[N_FIRST][0])
                    sp.wait_ge(S("cmb0"), TILES - 1)

            def loads(part):
                for key, _ in part:
                    if key[0].endswith("pg"):
                        load_pages(key[0])
                    else:
                        load(key)

            sp.dma_start(ptab[0:1, :], A["page_table"].rearrange("(o b) j -> o (b j)", o=1)).then_inc(S("ptab_in"), 16)
            sp.wait_ge(S("ptab_in"), 16)
            loads(stream[:N_FIRST])
            moe_loads(0)
            loads(stream[N_FIRST + 1:])
            moe_loads(1)
            for name, v in out_waits:
                sp.wait_ge(S(name), v)

        @block.tensor
        def _(pe):
            def transposes(dst, srcs, sem):
                for d_, s_ in zip(dst, srcs):
                    r = s_.shape[0]
                    last = pe.transpose(d_, s_, ident[0:r, 0:r])
                last.then_inc(S(sem), 1)

            def rhs_mm(out, lhs, w, sem, start=True, stop=True):
                K = lhs.shape[1]
                for k in range(K):
                    last = pe.matmul(out, lhs[:, k, :], w[:, k, :], start=start and k == 0, stop=stop and k == K - 1)
                last.then_inc(S(sem), 1)

            def modulated(m):
                if m % 2:
                    pe.wait_ge(S(f"out_ev{m - 1}"), 2 * TILES)
                for t in range(TILES):
                    R = rows(t)
                    pe.wait_ge(S("hn"), TILES * m + t + 1)
                    for g in range(2):
                        if t:
                            pe.wait_ge(S("ht_ev"), 2 * TILES * m + 2 * (t - 1) + g + 1)
                        transposes([bank[6 + g][:, q * R:(q + 1) * R] for q in range(4)],
                                   [HN[t % 2][0:R, (4 * g + q) * P:(4 * g + q + 1) * P] for q in range(4)], "ht_ps")
                    if m % 2 and t:
                        router(m, t - 1)
                    if m == 2 and t < NT:
                        d_product(t)
                if m % 2:
                    router(m, NT)
                else:
                    pe.wait_ge(S("ht_ev"), 2 * TILES * m + 2 * TILES)

            def d_product(i):
                n, t = divmod(i, TILES)
                if t == 0:
                    wait_slot(pe, ("din", n))
                if i == NT:
                    pe.wait_ge(S("d_ev"), 1)
                elif i > NT:
                    pe.wait_ge(S("d_ev"), i - 1)
                else:
                    pe.wait_ge(S("ht_ev"), 2 * TILES * 2 + 2 * (t + 1))
                w = min(NB, DSA_IN - n * NB)
                rhs_mm(d_bank(i)[0:rows(t), 0:w], HT[:, :, cols(t)], slot(("din", n), KD, w), "d_mm")

            def router(m, t):
                pe.wait_ge(S("ht_ev"), 2 * TILES * m + 2 * (t + 1))
                rhs_mm(bank[0][0:rows(t), t * NE:(t + 1) * NE], HT[:, :, cols(t)], wr[:, :, :], f"lg_mm{m // 2}")

            def out_product(m, src, halves):
                for n in range(2):
                    for kh in range(halves):
                        wait_slot(pe, (f"out{m}", n, kh))
                        for t in range(TILES):
                            if kh == 0 and n == 1 and t >= 3:
                                pe.wait_ge(S(f"out_ev{m}"), t - 2)
                            rhs_mm(bank[(TILES * n + t) % 8][0:rows(t), :], src[:, kh * KD:(kh + 1) * KD, cols(t)],
                                   slot((f"out{m}", n, kh)), f"out_mm{m}" if kh == halves - 1 else f"out_half{m}",
                                   start=kh == 0, stop=kh == halves - 1)

            pe.nop().then_inc(S("unit_used"), UNIT0)
            for j in range(2):
                pe.nop().then_inc(S(f"at_ps{j}"), 1)
                pe.nop().then_inc(S(f"hg_ps{j}"), 2)
            pe.wait_ge(S("cst_in"), 16)
            pe.wait_ge(S("c_silu"), 1)
            R = DEC + 1
            transposes([bank[2][:, k * R:(k + 1) * R] for k in range(KD)],
                       [CSIL[:, k * P:(k + 1) * P] for k in range(KD)], "c_ps")
            pe.wait_ge(S("c_t"), 1)
            for n in range(12):
                wait_slot(pe, ("mod", 0, n))
                if n >= 2:
                    pe.wait_ge(S("mod_ev"), n - 1)
                rhs_mm(bank[n % 2][0:R, :], CT, slot(("mod", 0, n)), "mod_mm")

            def mod1(part):
                for n in part:
                    wait_slot(pe, ("mod", 1, n))
                    if n == 0:
                        pe.wait_ge(S("out_ev0"), 2 * TILES)
                    if n >= 4:
                        pe.wait_ge(S("mod_ev"), 12 + n - 3)
                    rhs_mm(bank[2 + n % 4][0:DEC + 1, :], CT, slot(("mod", 1, n)), "mod_mm")

            modulated(0)
            item = 0

            def ret_product(w_key, t):
                nonlocal item
                if t == 0:
                    wait_slot(pe, w_key)
                if item >= 2:
                    pe.wait_ge(S("ret_ev"), item - 1)
                rhs_mm(bank[item % 2][0:rows(t), :], HT[:, :, cols(t)], slot(w_key), "ret_mm")
                item += 1

            qk = 0
            yt = 0
            for hp in range(2):
                def turn_qk():
                    nonlocal qk
                    t = qk % TILES
                    R = rows(t)
                    pe.wait_ge(S("ro_rdy"), qk + 1)
                    if qk >= 2:
                        pe.wait_ge(S("qk_ev"), qk - 1)
                    isk = (qk // TILES) % 2
                    src = KN[:, t, :] if isk and t < NT else RO
                    transposes([bank[2 + qk % 2][:, q * R:(q + 1) * R] for q in range(4)],
                               [src[0:R, q * P:(q + 1) * P] for q in range(4)], "qk_ps")
                    qk += 1

                for i in range(2 * TILES):
                    ret_product((("q", "k")[i // TILES], hp), i % TILES)
                    if i:
                        turn_qk()
                ret_product(("v", hp, 0), 0)
                turn_qk()
                for i in range(1, 2 * TILES):
                    ret_product(("v", hp, i // TILES), i % TILES)
                pe.wait_ge(S("qk_ev"), qk)
                pe.wait_ge(S("ret_ev"), item)

                def attend(i):
                    hh, c = divmod(i, NT)
                    rc = hp * 2 * NT + i
                    if rc >= 2:
                        pe.wait_ge(S("att_rdy"), rc - 1)
                    for j in range(2):
                        last = pe.matmul(bank[3 + rc % 2][:, 0:P], KT[:, 2 * hh + j, cols(c)], QT[:, 2 * hh + j, cols(c)],
                                         start=j == 0, stop=j == 1)
                    last.then_inc(S("att_ps"), 1)

                attend(0)
                for i in range(2 * NT):
                    hh, c = divmod(i, NT)
                    rc = hp * 2 * NT + i
                    if i + 1 < 2 * NT:
                        attend(i + 1)
                    pe.wait_ge(S("att_rdy"), rc + 1)
                    if rc:
                        pe.wait_ge(S("s_rdy"), rc)
                        pe.wait_ge(S("o_ev"), rc)
                    vv = V[:, c, hh * NB:(hh + 1) * NB]
                    last = pe.matmul(bank[5][:, :], att[:, rc % 2, :], vv, start=True, stop=c == 0)
                    if c:
                        for j in range(2):
                            last = pe.matmul(bank[5][:, :], QT[:, 2 * hh + j, cols(c)], STATE[:, hh, j, :],
                                             start=False, stop=j == 1)
                    last.then_inc(S("o_ps"), 1)
                    for j in range(2):
                        last = pe.matmul(bank[6 + j][:, :], KN[:, c, (2 * hh + j) * P:(2 * hh + j + 1) * P], vv,
                                         start=True, stop=True)
                    last.then_inc(S("u_ps"), 1)

                def spread(i):
                    si = 2 * DEC * hp + i
                    if si >= 2:
                        pe.wait_ge(S("st_upd"), si - 1)
                    b, hh = divmod(i, 2)
                    pe.matmul(bank[2 + si % 2][:, :], ident[0:DEC, b:b + 1].to_broadcast([DEC, P]),
                              V[0:DEC, NT, hh * NB:(hh + 1) * NB], start=True, stop=True).then_inc(S("vb_ps"), 1)

                spread(0)
                pe.wait_ge(S("qm_rdy"), hp + 1)
                for i in range(2 * DEC):
                    si = 2 * DEC * hp + i
                    b, hh = divmod(i, 2)
                    if i + 1 < 2 * DEC:
                        spread(i + 1)
                    pe.wait_ge(S("st_upd"), si + 1)
                    st = slot(("state", hp, b // 2))
                    for j in range(2):
                        last = pe.matmul(bank[hh][0:DEC, :], qmask[:, b, 2 * hh + j, :],
                                         st[:, 4 * (b % 2) + 2 * hh + j, :], start=b == 0 and j == 0,
                                         stop=b == DEC - 1 and j == 1)
                    last.then_inc(S("os_mm"), 1)
                pe.wait_ge(S("os_ev"), 2 * (hp + 1))

                def turn_y():
                    nonlocal yt
                    t = yt % TILES
                    R = rows(t)
                    hh = (yt // TILES) % 2
                    pe.wait_ge(S("y_rdy"), yt + 1)
                    if yt >= 2:
                        pe.wait_ge(S("yt_ev"), yt - 1)
                    transposes([bank[2 + yt % 2][:, q * R:(q + 1) * R] for q in range(4)],
                               [V[0:R, t, hh * NB + q * P:hh * NB + (q + 1) * P] for q in range(4)], "yt_ps")
                    yt += 1

                for i in range(2 * TILES):
                    ret_product(("g", hp, i // TILES), i % TILES)
                    if i:
                        turn_y()
                turn_y()
            pe.wait_ge(S("yt_ev"), yt)
            pe.wait_ge(S("ret_ev"), item)
            out_product(0, YT, 2)

            def experts(l):
                m = 2 * l + 1
                modulated(m)
                if l == 0:
                    mod1(range(0, 2))
                pe.wait_ge(S("marks"), l + 1)
                for t in range(TILES + 1):
                    for t2 in range(min(t, TILES - 1) + 1):
                        last = pe.matmul(bank[1][:, t * NE:(t + 1) * NE], bf_cum[:, 0 if t2 == t else 1, :], mb[:, t2, :],
                                         start=t2 == 0, stop=t2 == min(t, TILES - 1))
                last.then_inc(S("rank_mm"), 1)
                if l == 0:
                    mod1(range(2, 12))
                    pe.wait_ge(S("mod_ev"), 24)
                pe.wait_ge(S("tables"), l + 1)
                first, last = pairs(pe, l)

                def turn_rows(j, i):
                    pe.wait_ge(S(f"rows_in{j}"), (i + 1) * 16)
                    pe.wait_ge(S(f"at_lo{j}"), i + 1)
                    for g in range(2):
                        transposes([bank[2 * j + g][:, q * P:(q + 1) * P] for q in range(4)],
                                   [HG[j][:, (4 * g + q) * P:(4 * g + q + 1) * P] for q in range(4)], f"hg_ps{j}")

                def pair(i, end):
                    def split_mm(out, xh, xl, u, start, stop):
                        pe.wait_ge(S("lo_rdy"), i * len(UNITS) + (UNIT0 + u + 1))
                        for c in range(4):
                            for n, (x_, w_) in enumerate(((xh, WH), (xh, WL), (xl, WH))):
                                done = pe.matmul(out, x_[:, c, :], w_[:, u % SPLIT, c, :], start=start and c == n == 0,
                                                 stop=stop and c == 3 and n == 2)
                        done.then_inc(S("unit_used"), 1)

                    def up(j, c, u):
                        for h in range(2):
                            split_mm(bank[4 + 2 * j + c][:, :], HGH[:, j, 4 * h:4 * h + 4, :], HGL[:, j, 4 * h:4 * h + 4, :],
                                     u + h, h == 0, h == 1)

                    def turn_a(j):
                        pe.wait_ge(S(f"a_rdy{j}"), i + 2)
                        transposes([bank[2 * j][:, q * P:(q + 1) * P] for q in range(4)],
                                   [AE[:, q * P:(q + 1) * P] for q in range(4)], f"at_ps{j}")

                    def down(j, h, u):
                        split_mm(bank[4 + 2 * j + h][:, :], ATH[:, j, :, :], ATL[:, j, :, :], u, True, True)

                    pe.wait_ge(S("hg_lo0"), 2 * (i + 1))
                    pe.wait_ge(S("y_ev_d0"), i + 1)
                    up(0, 0, 0)
                    turn_rows(1, i)
                    pe.wait_ge(S("y_ev_a0"), i + 1)
                    up(0, 1, 2)
                    pe.wait_ge(S("hg_lo1"), 2 * (i + 1))
                    pe.wait_ge(S("y_ev_d1"), i + 1)
                    up(1, 0, 4)
                    turn_a(0)
                    pe.wait_ge(S("y_ev_a1"), i + 1)
                    up(1, 1, 6)
                    pe.wait_ge(S("at_lo0"), i + 2)
                    down(0, 0, 8)
                    turn_a(1)
                    down(0, 1, 9)
                    if not end:
                        turn_rows(0, i + 1)
                    pe.wait_ge(S("at_lo1"), i + 2)
                    down(1, 0, 10)
                    down(1, 1, 11)

                turn_rows(0, first)
                with pe.Fori(0, last) as k:
                    pair(first + k, False)
                pair(first + last, True)

            experts(0)

            modulated(2)
            dt = 0

            def turn_d():
                nonlocal dt
                n, t = divmod(dt, TILES)
                R = rows(t)
                pe.wait_ge(S("d_rot"), dt + 1)
                if dt >= 2:
                    pe.wait_ge(S("d_tev"), dt - 1)
                src, nq = ((DRT[dt % 2], 4), (DRT[dt % 2], 4), (KV[:, t, :], 2), (DRT[dt % 2], 4), (DRT[dt % 2], 4),
                           (KID[:, t, :], 1))[n]
                transposes([bank[2 + dt % 2][:, q * R:(q + 1) * R] for q in range(nq)],
                           [src[0:R, q * P:(q + 1) * P] for q in range(nq)], "d_tp")
                dt += 1

            turn_d()
            d_product(NT)
            for i in range(1, NT):
                turn_d()
            for i in range(NT + 1, 6 * TILES):
                d_product(i)
                turn_d()
            turn_d()
            pe.wait_ge(S("d_tev"), 6 * TILES)
            pe.wait_ge(S("d_ev"), 6 * TILES)
            ix = 0
            for t in range(NT):
                L = (t + 1) * P

                def index(part):
                    nonlocal ix
                    for h in range(part * IH // 4, (part + 1) * IH // 4):
                        if ix >= 2:
                            pe.wait_ge(S("ix_rl"), ix - 1)
                        o64 = ID * (h % 2)
                        pe.matmul(bank[ix % 2][:, 0:L + P], QIT[o64:o64 + ID, h // 2, cols(t + 1)], KIT[o64:o64 + ID, 0:L + P],
                                  start=True, stop=True).then_inc(S("ix_ps"), 1)
                        ix += 1

                def logits(h):
                    a = t * QH + h
                    if a >= 2:
                        pe.wait_ge(S("lg_ev"), a - 1)
                    pe.matmul(bank[2 + a % 2][:, 0:L], DQT[:, h, cols(t)], DKT[:, h // GRP, 0:L],
                              start=True, stop=True).then_inc(S("lg_ps"), 1)

                def turn_p(h):
                    a = t * QH + h
                    pe.wait_ge(S("p_rdy"), a + 1)
                    if a >= 2:
                        pe.wait_ge(S("pt_ev"), a - 1)
                    transposes([bank[4 + a % 2][:, q * P:(q + 1) * P] for q in range(t + 1)],
                               [E[a % 4][:, q * P:(q + 1) * P] for q in range(t + 1)], "pt_ps")

                def pv(h):
                    a = t * QH + h
                    pe.wait_ge(S("pt_ev"), a + 1)
                    if a >= 2:
                        pe.wait_ge(S("ot_ev"), a - 1)
                    n = h // GRP
                    for c in range(t + 1):
                        last = pe.matmul(bank[6 + a % 2][:, 0:P], KV[:, c, KVH * HD + n * HD:KVH * HD + (n + 1) * HD],
                                         PT[a % 2][:, c, :], start=c == 0, stop=c == t)
                    last.then_inc(S("pv_mm"), 1)

                for s in range(QH + LAG + 1):
                    if s < QH:
                        logits(s)
                    if LAG <= s < QH + LAG:
                        turn_p(s - LAG)
                    if s < 4 and t + 1 < NT:
                        index(s)
                    if s > LAG:
                        pv(s - LAG - 1)

            transposes([bank[0][0:DEC, par * DEC:(par + 1) * DEC] for par in range(2)],
                       [WI[0:DEC, NT, :].rearrange("p (h two) -> p two h", two=2)[:, par, :] for par in range(2)], "w_t")
            wait_slot(pe, ("ipg",))
            wait_slot(pe, ("kpg",))
            pe.wait_ge(S("ot_ev"), NT * QH)
            pe.wait_ge(S("wm_rdy"), 1)
            ipg = RING[:, place[("ipg",)][1], 0:DEC * NPG * P].rearrange("p (i d) -> p i d", d=P)
            kpg = RING[:, place[("kpg",)][1], :].rearrange("p (i n d) -> p i n d", n=KVH, d=HD)
            vpg = RING[:, place[("vpg",)][1], :].rearrange("p (i n d) -> p i n d", n=KVH, d=HD)

            def s_score(b):
                pe.wait_ge(S("s_rl"), b + 1)
                for par in range(2):
                    last = pe.matmul(bank[6][0:DEC, 0:LS], WM[:, par, b, :], RLS[b % 2][:, par, :],
                                     start=b == 0 and par == 0, stop=b == DEC - 1 and par == 1)
                last.then_inc(S("s_sc"), 1)

            for b in range(DEC):
                if b:
                    pe.wait_ge(S("ki_ev"), b)
                transposes([bank[0][:, q * P:(q + 1) * P] for q in range(NPG)],
                           [ipg[:, b * NPG + q, :] for q in range(NPG)], "ki_t")
                pe.wait_ge(S("ki_rdy"), b + 1)
                pe.wait_ge(S("ki_ev"), b + 1)
                if b:
                    pe.wait_ge(S("s_rl"), b)
                for par in range(2):
                    last = pe.matmul(bank[3 + par][0:DEC, 0:LS],
                                     QIT[par * ID:(par + 1) * ID, :, SEQ + b], KIBT[b % 2][par * ID:(par + 1) * ID, :],
                                     start=True, stop=True)
                last.then_inc(S("s_dot"), 1)
                if b:
                    s_score(b - 1)
            s_score(DEC - 1)
            for b in range(DEC):
                for n in range(KVH):
                    if b:
                        pe.wait_ge(S("kk_ev"), 2 * (b - 1) + n + 1)
                    transposes([bank[1 + n][:, q * P:(q + 1) * P] for q in range(NPG)],
                               [kpg[:, b * NPG + q, n, :] for q in range(NPG)], "kk_t")
            pe.wait_ge(S("s_bias"), 1)
            pe.wait_ge(S("kk_ev"), 2 * DEC)
            pe.wait_ge(S("kn_rdy"), 1)
            for n in range(KVH):
                pe.matmul(bank[n][0:DEC * GRP, 0:LS], C("bexp", DEC), BIS[0:DEC, :], start=True, stop=False)
                for b in range(DEC):
                    last = pe.matmul(bank[n][0:DEC * GRP, 0:LS], QM[:, b, n, :], KBT[:, b, n, :], start=False,
                                     stop=b == DEC - 1)
                last.then_inc(S("s_lg"), 1)
            wait_slot(pe, ("vpg",))
            for n in range(KVH):
                pe.wait_ge(S("s_p"), n + 1)
                r = DEC * GRP
                for q in range(NPG):
                    pe.transpose(bank[2 + n][:, q * r:(q + 1) * r], PS[n][:, q * P:(q + 1) * P], ident[0:r, 0:r])
                pe.matmul(bank[4 + n][0:DEC, 0:r], C("bsel", r), DG[:, n, :], start=True, stop=True).then_inc(S("s_pt"), 1)
            for n in range(KVH):
                pe.wait_ge(S("s_ptev"), n + 1)
                out = bank[6 + n]
                pe.matmul(out[:, 0:DEC * GRP], KV[0:DEC, NT, (KVH + n) * HD:(KVH + n + 1) * HD], PNW[:, n, :],
                          start=True, stop=False)
                for b in range(DEC):
                    for q in range(NPG):
                        last = pe.matmul(out[:, b * GRP:(b + 1) * GRP], vpg[:, b * NPG + q, n, :],
                                         PTS[:, n, q, b * GRP:(b + 1) * GRP], start=False,
                                         stop=b == DEC - 1 and q == NPG - 1)
                last.then_inc(S("s_pv"), 1)
            pe.wait_ge(S("s_ot"), KVH)
            pe.wait_ge(S("ot_ev"), NT * QH)
            out_product(2, OT, 1)
            experts(1)

        @block.scalar
        def _(act):
            def scale_shift(m):
                l, half = divmod(m, 2)
                if m:
                    act.wait_ge(S("hn"), TILES * m)
                act.wait_ge(S(f"mod_st{l}"), (16, 32, 16 * 12, 16 * 12)[m])
                for i, p_ in ((0, 1), (1, 0)):
                    at = (3 * half + p_) * D
                    act.dma_start(SCALE_SHIFT[i] if m else BC[:, i, :], mod_d[l, DEC:DEC + 1, at:at + D].to_broadcast([P, D]))\
                        .then_inc(S("bc_in"), 16)
                    act.dma_start(SC[:, i, :], mod_d[l, 0:DEC, at:at + D]).then_inc(S("bc_in"), 16)

            def gate_norm(m):
                l, half = divmod(m, 2)
                if m == 0:
                    act.wait_ge(S("mod_st0"), 32)
                at = (3 * half + 2) * D
                act.dma_start(BC[:, 0, :], mod_d[l, DEC:DEC + 1, at:at + D].to_broadcast([P, D])).then_inc(S("ep_in"), 16)
                for i, w in ((1, ("ln1_g", "ln2_g")[half]), (2, ("ln1_b", "ln2_b")[half])):
                    act.dma_start(BC[:, i, :], A[w][l:l + 1, :].to_broadcast([P, D])).then_inc(S("ep_in"), 16)

            def sample_gate(m):
                l, half = divmod(m, 2)
                at = (3 * half + 2) * D
                act.dma_start(SGATE, mod_d[l, 0:DEC, at:at + D]).then_inc(S("ep_in"), 16)

            def root(m, t):
                act.wait_ge(S("ln_var"), TILES * m + t + 1)
                act.activation(lnsd[:, t:t + 1], lnmv[:, t, 1:2], ACT.Sqrt, bias=C("lneps"), scale=1.0)\
                    .then_inc(S("ln_sd"), 1)

            def turned(m, t):
                for g in range(2):
                    act.wait_ge(S("ht_ps"), 2 * TILES * m + 2 * t + g + 1)
                    act.activation(HT[:, 4 * g:4 * g + 4, cols(t)],
                                   bank[6 + g][:, 0:4 * rows(t)].rearrange("p (q r) -> p q r", r=rows(t)),
                                   ACT.Copy).then_inc(S("ht_ev"), 1)

            act.dma_start(CROW[0:DEC, :], A["c_sample"]).then_inc(S("c_in"), 16)
            act.dma_start(CROW[DEC:DEC + 1, :], A["c_prompt"]).then_inc(S("c_in"), 16)
            act.dma_start(cst[:, :], A["cst"]).then_inc(S("cst_in"), 16)
            act.dma_start(BMOD[:, :], A["b_mod"][0:1, :].to_broadcast([DEC + 1, 6 * D]))\
                .then_inc(S("bmod_in"), 16)
            act.dma_start(rotc[:, :, :, :], A["rotc"]).then_inc(S("const_in"), 16)
            act.dma_start(tok[:, :], A["tok"]).then_inc(S("const_in"), 16)
            act.dma_start(wr[:, :, :], A["w_router"].rearrange("(k p) e -> p k e", p=P)).then_inc(S("const_in"), 16)
            act.dma_start(br[:, :], A["b_router"].rearrange("(o e) -> o e", o=1).to_broadcast([P, NE])).then_inc(S("const_in"), 16)
            act.dma_start(X[:, 0:NT, :], A["x_prompt"][0].rearrange("(t p) d -> p t d", p=P)).then_inc(S("x_in"), 16)
            act.dma_start(X[0:DEC, NT, :], A["x_sample"].rearrange("b t d -> (b t) d")).then_inc(S("x_in"), 16)
            act.wait_ge(S("c_in"), 32)
            for j in range(2):
                act.nop().then_inc(S(f"y_ev_a{j}"), 1)
            act.activation(CSIL[:, :], CROW[:, :], ACT.Silu).then_inc(S("c_silu"), 1)
            act.wait_ge(S("mod_ev"), 4)
            act.dma_start(mod_d[0][:, 0:2 * D], MODV[:, 0:2 * D]).then_inc(S("mod_st0"), 16)
            scale_shift(0)
            act.wait_ge(S("mod_ev"), 12)
            act.dma_start(mod_d[0][:, 2 * D:], MODV[:, 2 * D:]).then_inc(S("mod_st0"), 16)

            def mod1(n):
                act.wait_ge(S("mod_mm"), 12 + n + 1)
                if n >= 6:
                    act.wait_ge(S("mod_st1"), 16 * (n - 5))
                act.activation(MS1[n % 6], bank[2 + n % 4][0:DEC + 1, :], ACT.Copy).then_inc(S("mod_ev"), 1)

            for t in range(TILES):
                turned(0, t)
            act.wait_ge(S("mod_st0"), 32)
            item = qk = yt = 0
            for hp in range(2):
                if hp == 0:
                    act.wait_ge(S("hn"), TILES)
                else:
                    act.wait_ge(S("y_rdy"), 2 * TILES)
                act.dma_start(GNB, A["gn_ret_g"][0:1, hp * D:(hp + 1) * D].to_broadcast([P, D])).then_inc(S("gn_in"), 16)

                def take_qk():
                    nonlocal qk
                    t = qk % TILES
                    R = rows(t)
                    act.wait_ge(S("qk_ps"), qk + 1)
                    dst = (QT, KT)[(qk // TILES) % 2]
                    act.activation(dst[:, :, cols(t)], bank[2 + qk % 2][:, 0:4 * R].rearrange("p (q r) -> p q r", r=R),
                                   ACT.Copy).then_inc(S("qk_ev"), 1)
                    qk += 1

                for i in range(2 * TILES):
                    t = i % TILES
                    R = rows(t)
                    act.wait_ge(S("ret_mm"), item + 1)
                    if item:
                        act.wait_ge(S("ro_rdy"), hp * 2 * TILES + i)
                    if hp and i == 0:
                        act.wait_ge(S("y_rdy"), 2 * TILES)
                    for hh in range(2):
                        sc_ = C(("qs", "ks")[i // TILES])[0:R, t * RH + 2 * hp + hh:t * RH + 2 * hp + hh + 1]
                        last = act.activation(RT[0:R, hh * RDK:(hh + 1) * RDK],
                                              bank[item % 2][0:R, hh * RDK:(hh + 1) * RDK], ACT.Copy, scale=sc_)
                    last.then_inc(S("ret_ev"), 1)
                    item += 1
                    if i:
                        take_qk()
                for i in range(2 * TILES):
                    hh, t = divmod(i, TILES)
                    act.wait_ge(S("ret_mm"), item + 1)
                    act.activation(V[0:rows(t), t, hh * NB:(hh + 1) * NB], bank[item % 2][0:rows(t), :], ACT.Copy)\
                        .then_inc(S("ret_ev"), 1)
                    item += 1
                    if i == 0:
                        take_qk()
                for i in range(2 * NT):
                    hh, c = divmod(i, NT)
                    rc = hp * 2 * NT + i
                    act.wait_ge(S("u_ps"), rc + 1)
                    act.activation(V[:, c, hh * NB:(hh + 1) * NB], bank[5][:, :], ACT.Copy).then_inc(S("o_ev"), 1)
                for i in range(2 * DEC):
                    b, hh = divmod(i, 2)
                    key = ("state", hp, b // 2)
                    if i % 4 == 0:
                        wait_slot(act, key)
                    st = slot(key)[:, 4 * (b % 2) + 2 * hh:4 * (b % 2) + 2 * hh + 2, :]
                    act.activation(st, st, ACT.Copy, scale=GAMMA[2 * hp + hh]).then_inc(S("st_dec"), 1)
                act.wait_ge(S("os_mm"), 2 * DEC * (hp + 1))
                for hh in range(2):
                    act.activation(V[0:DEC, NT, hh * NB:(hh + 1) * NB], bank[hh][0:DEC, :], ACT.Copy)\
                        .then_inc(S("os_ev"), 1)
                act.wait_ge(S("gn_var"), hp + 1)
                act.activation(gnsd[:, :, :], gnmv[:, :, :, 1], ACT.Sqrt, bias=C("gneps"), scale=1.0).then_inc(S("gn_sd"), 1)

                def take_y():
                    nonlocal yt
                    t = yt % TILES
                    R = rows(t)
                    h = yt // TILES
                    act.wait_ge(S("yt_ps"), yt + 1)
                    act.activation(YT[:, 4 * h:4 * h + 4, cols(t)],
                                   bank[2 + yt % 2][:, 0:4 * R].rearrange("p (q r) -> p q r", r=R), ACT.Copy)\
                        .then_inc(S("yt_ev"), 1)
                    yt += 1

                for i in range(2 * TILES):
                    t = i % TILES
                    act.wait_ge(S("ret_mm"), item + 1)
                    g = hp * 2 * TILES + i
                    if i >= 2:
                        act.wait_ge(S("y_rdy"), g - 1)
                    act.activation(SG[i % 2][0:rows(t), :], bank[item % 2][0:rows(t), :], ACT.Silu).then_inc(S("ret_ev"), 1)
                    item += 1
                    if i:
                        take_y()
                take_y()
            act.wait_ge(S("y_rdy"), 4 * TILES)
            act.wait_ge(S("rp_st"), 16 * RH)
            gate_norm(0)
            sample_gate(0)
            act.wait_ge(S("y_zero"), 16)
            scale_shift(1)
            for t in range(TILES):
                root(0, t)

            def experts(l):
                m = 2 * l + 1
                for t in range(TILES):
                    turned(m, t)
                act.wait_ge(S("x_rdy"), TILES * m)
                if l:
                    gate_norm(m)
                act.wait_ge(S("lg_sub"), l + 1)
                act.activation(PR, LG, ACT.Exp).then_inc(S("lg_exp"), 1)
                if l == 0:
                    for n in range(10):
                        mod1(n)

                def high(i, u):
                    act.wait_ge(S(f"raw_in{u % RAW}"), raw_count(i, u))
                    act.wait_ge(S("unit_used"), i * len(UNITS) + (UNIT0 + u - SPLIT + 1))
                    act.activation(WH[:, u % SPLIT, :, :], raw(u % RAW), ACT.Copy).then_inc(S("hi_rdy"), 1)

                first = pairs_before(act, l)
                for u in range(SPLIT):
                    high(first, u)
                    if l == 0 and u < 2:
                        mod1(10 + u)
                act.wait_ge(S("tables"), l + 1)
                first, last = pairs(act, l)

                def take_rows(j, i):
                    for g in range(2):
                        act.wait_ge(S(f"hg_ps{j}"), 2 * i + (g + 3))
                        act.activation(HGH[:, j, 4 * g:4 * g + 4, :], bank[2 * j + g][:, :].rearrange("p (q r) -> p q r", r=P),
                                       ACT.Copy).then_inc(S(f"hg_hi{j}"), 1)

                def pair(i, end):
                    def used(u):
                        act.wait_ge(S("unit_used"), i * len(UNITS) + (UNIT0 + u + 1))

                    def gate(j, u):
                        used(u)
                        act.wait_ge(S("at_ps1" if j == 0 else "at_ps0"), i + 1 + j)
                        act.activation(SGE, bank[4 + 2 * j][:, :], ACT.Silu).then_inc(S(f"sg{j}"), 1)

                    def take_a(j):
                        act.wait_ge(S(f"at_ps{j}"), i + 2)
                        act.activation(ATH[:, j, :, :], bank[2 * j][:, :].rearrange("p (q r) -> p q r", r=P), ACT.Copy)\
                            .then_inc(S(f"at_hi{j}"), 1)

                    def take_y(j, u):
                        used(u)
                        act.wait_ge(S(f"y_st{j}"), (i + 1) * 16)
                        act.activation(Y[j][:, NB:D], bank[5 + 2 * j][:, :], ACT.Copy).then_inc(S(f"y_ev_a{j}"), 1)

                    for u in range(SPLIT, SPLIT + len(UNITS)):
                        if not end or u < len(UNITS):
                            high(i, u)
                        if u == 5:
                            take_rows(1, i)
                            gate(0, 1)
                        if u == 9:
                            gate(1, 5)
                            take_a(0)
                        if u == 12:
                            take_a(1)
                        if u == 13:
                            if not end:
                                take_rows(0, i + 1)
                            take_y(0, 9)
                        if u == 15:
                            take_y(1, 11)

                take_rows(0, first)
                with act.Fori(0, last) as k:
                    pair(first + k, False)
                pair(first + last, True)
                if l == 0:
                    act.wait_ge(S("mod_st1"), 16 * 12)
                    gate_norm(m)
                act.wait_ge(S("unit_used"), (first + last) * len(UNITS) + (UNIT0 + len(UNITS)))
                sample_gate(m)
                if l == 0:
                    act.wait_ge(S("y_st1"), (first + last) * 16 + 32)
                    scale_shift(m + 1)
                for s in range(TILES + 3):
                    if s < TILES:
                        act.wait_ge(S(f"yg_in{s % 2}"), 32 * (l * tiles_of[s % 2] + s // 2 + 1))
                        y1 = YG[s % 2][0][0:rows(s), :]
                        act.activation(y1, y1, ACT.Copy, scale=gates[0:rows(s), 0, s:s + 1]).then_inc(S("y_gated"), 1)
                    if 1 <= s <= TILES:
                        root(m, s - 1)
                    if s >= 3 and l == 0:
                        turned(m + 1, s - 3)

            experts(0)


            def take_d(i):
                n, t = divmod(i, TILES)
                R = rows(t)
                act.wait_ge(S("d_tp"), i + 1)
                dst = (DQT[:, 0:4], DQT[:, 4:8], DKT, QIT[:, 0:4], QIT[:, 4:8], None)[n]
                if n == 5:
                    act.activation(KIT[:, cols(t)], bank[2 + i % 2][:, 0:R], ACT.Copy).then_inc(S("d_tev"), 1)
                else:
                    nq = dst.shape[1]
                    act.activation(dst[:, :, cols(t)], bank[2 + i % 2][:, 0:nq * R].rearrange("p (q r) -> p q r", r=R),
                                   ACT.Copy).then_inc(S("d_tev"), 1)

            for i in range(6 * TILES):
                n, t = divmod(i, TILES)
                R = rows(t)
                act.wait_ge(S("d_mm"), i + 1)
                if i >= 2:
                    act.wait_ge(S("d_tp"), i - 1)
                w = min(NB, DSA_IN - n * NB)
                dst = KV[0:R, t, :] if n == 2 else KIW[0:R, t, :] if n == 5 else DRT[i % 2][0:R, :]
                act.activation(dst, d_bank(i)[0:R, 0:w], ACT.Copy).then_inc(S("d_ev"), 1)
                if i:
                    take_d(i - 1)
            take_d(6 * TILES - 1)
            ix = 0
            SCALE = HD ** -0.5
            for t in range(NT):
                L = (t + 1) * P

                def index():
                    nonlocal ix
                    for h in range(IH // 4):
                        act.wait_ge(S("ix_ps"), ix + 1)
                        if ix >= 4:
                            act.wait_ge(S("ix_acc"), ix - 3)
                        act.activation(RL[ix % 4][:, 0:L + P], bank[ix % 2][:, 0:L + P], ACT.Relu, scale=ID ** -0.5)\
                            .then_inc(S("ix_rl"), 1)
                        ix += 1

                def take_p(h):
                    a = t * QH + h
                    act.wait_ge(S("pt_ps"), a + 1)
                    if a >= 2:
                        act.wait_ge(S("pv_mm"), a - 1)
                    act.activation(PT[a % 2][:, 0:t + 1, :], bank[4 + a % 2][:, 0:L].rearrange("p (q r) -> p q r", r=P),
                                   ACT.Copy).then_inc(S("pt_ev"), 1)

                def take_o(h):
                    a = t * QH + h
                    act.wait_ge(S("pv_mm"), a + 1)
                    act.activation(OT[:, h, cols(t)], bank[6 + a % 2][:, 0:P], ACT.Copy).then_inc(S("ot_ev"), 1)

                for s in range(QH + LAG + 1):
                    if s < 4 and t + 1 < NT:
                        index()
                    if s < QH:
                        a = t * QH + s
                        act.wait_ge(S("nb_rdy"), a + 1)
                        act.activation(E[a % 4][:, 0:L], E[a % 4][:, 0:L], ACT.Exp, bias=nbias[:, a % 2:a % 2 + 1],
                                       scale=SCALE, accum_out=esum[:, a % 2:a % 2 + 1]).then_inc(S("e_rdy"), 1)
                    if 1 <= s < QH + 1:
                        a = t * QH + s - 1
                        act.wait_ge(S("es_rdy"), a + 1)
                        act.activation(E[a % 4][:, 0:L], E[a % 4][:, 0:L], ACT.Copy, scale=ersum[:, a % 2:a % 2 + 1])\
                            .then_inc(S("p_rdy"), 1)
                    if LAG <= s < QH + LAG:
                        take_p(s - LAG)
                    if s > LAG:
                        take_o(s - LAG - 1)

            for b in range(DEC):
                act.wait_ge(S("ki_t"), b + 1)
                if b >= 2:
                    act.wait_ge(S("s_dot"), b - 1)
                act.activation(KIBT[b % 2][:, 0:PAST], bank[0][:, 0:PAST], ACT.Copy).then_inc(S("ki_ev"), 1)
                act.wait_ge(S("s_dot"), b + 1)
                if b >= 2:
                    act.wait_ge(S("s_sc"), b - 1)
                for par in range(2):
                    last = act.activation(RLS[b % 2][:, par, :], bank[3 + par][0:DEC, 0:LS], ACT.Relu, scale=ID ** -0.5)
                last.then_inc(S("s_rl"), 1)
            for b in range(DEC):
                for n in range(KVH):
                    act.wait_ge(S("kk_t"), 2 * b + n + 1)
                    act.activation(KBT[:, b, n, 0:PAST], bank[1 + n][:, 0:PAST], ACT.Copy).then_inc(S("kk_ev"), 1)
            for n in range(KVH):
                act.wait_ge(S("s_nb"), n + 1)
                r = DEC * GRP
                act.activation(PS[n][:, :], PS[n][:, :], ACT.Exp, bias=nbias[0:r, n:n + 1], scale=SCALE,
                               accum_out=esum[0:r, n:n + 1]).then_inc(S("s_e"), 1)
            for n in range(KVH):
                act.wait_ge(S("s_pt"), n + 1)
                r = DEC * GRP
                act.activation(PTS[:, n, :, :], bank[2 + n][:, 0:NPG * r].rearrange("p (q r) -> p q r", r=r), ACT.Copy)
                act.activation(PNW[:, n, :], bank[4 + n][0:DEC, 0:r], ACT.Copy).then_inc(S("s_ptev"), 1)
            for n in range(KVH):
                act.wait_ge(S("s_pv"), n + 1)
                act.activation(OT[:, n * GRP:(n + 1) * GRP, SEQ:TOK],
                               bank[6 + n][:, 0:DEC * GRP].rearrange("p (b g) -> p g b", g=GRP), ACT.Copy)\
                    .then_inc(S("s_ot"), 1)
            act.wait_ge(S("x_rdy"), 2 * TILES)
            gate_norm(2)
            sample_gate(2)
            scale_shift(3)
            for t in range(TILES):
                root(2, t)
            experts(1)
            for t in range(TILES):
                act.wait_ge(S("x_rdy"), 3 * TILES + t + 1)
                dst = O["y_prompt"][0, t * P:(t + 1) * P, :] if t < NT else O["y_sample"].rearrange("b t d -> (b t) d")
                act.dma_start(dst, X[0:rows(t), t, :]).then_inc(S("y_out"), 16)

        @block.gpsimd
        def _(pool):
            for j in range(2):
                pool.dma_start(primer[j:j + 1, :], A["tok"][j:j + 1, 0:2]).then_inc(S(f"y_st{j}"), 16)
            nc.gpsimd.memset(zero_i[:, :], 0).then_inc(S("zeros"), 1)
            zero_f = Y[1][:, :]
            nc.gpsimd.memset(zero_f, 0.0).then_inc(S("zeros"), 1)
            pool.wait_ge(S("zeros"), 2)
            pool.wait_ge(S("hn"), TILES)
            pool.dma_start(y_items[:, NE:, :],
                           zero_f.rearrange("p (o d) -> p o d", o=1).to_broadcast([P, ITEMS - NE, D])).then_inc(S("y_zero"), 16)
            pool.dma_start(slot_d.rearrange("(p i) o -> p (i o)", p=P), zero_i[:, :]).then_inc(S("slot_zero"), 16)
            for hp in range(2):
                for hh in range(2):
                    h = 2 * hp + hh
                    pool.wait_ge(S("s_rdy"), (h + 1) * NT)
                    pool.dma_start(O["ret_prompt"][0, 0, h].rearrange("(j p) v -> p j v", p=P), STATE[:, hh, :, :])\
                        .then_inc(S("rp_st"), 16)
                for b in range(DEC):
                    n = 2 * DEC * hp + 2 * b + 2
                    pool.wait_ge(S("st_upd"), n)
                    pool.dma_start(O["ret_sample"][0, b, 2 * hp:2 * hp + 2].rearrange("h (j p) v -> p (h j) v", p=P),
                                   slot(("state", hp, b // 2))[:, 4 * (b % 2):4 * (b % 2) + 4, :])\
                        .then_inc(S(f"state_st{place[('state', hp, b // 2)][1]}"), 16)

            def bias(n):
                pool.dma_start(bias1[:, n % 4, :], A["b_mod"][1:2, n * NB:(n + 1) * NB].to_broadcast([DEC + 1, NB]))\
                    .then_inc(S(f"bm_in{n % 4}"), 16)

            def mod1():
                own = 0
                for n in range(12):
                    pool.wait_ge(S(f"bm_in{n % 4}"), 16 * (n // 4 + 1))
                    pool.wait_ge(S("mod_ev"), 12 + n + 1)
                    nc.gpsimd.tensor_tensor(MS1[n % 6], MS1[n % 6], bias1[:, n % 4, :], ALU.add).then_inc(S("biased"), 1)
                    own += 1
                    pool.wait_ge(S("biased"), own)
                    if n in (2, 3, 8, 9):
                        nc.gpsimd.tensor_scalar(MS1[n % 6], MS1[n % 6], 1.0, 0.0, ALU.add, ALU.add)\
                            .then_inc(S("biased"), 1)
                        own += 1
                        pool.wait_ge(S("biased"), own)
                    if n:
                        pool.wait_ge(S("mod_st1"), 16 * n)
                    pool.dma_start(mod_d[1][:, n * NB:(n + 1) * NB], MS1[n % 6]).then_inc(S("mod_st1"), 16)
                    if n + 4 < 12:
                        bias(n + 4)

            def experts(l):
                m = 2 * l + 1
                for t in range(TILES):
                    pool.wait_ge(S("hn"), TILES * m + t + 1)
                    pool.dma_start(h_d[cols(t), :], HN[t % 2][0:rows(t), :]).then_inc(S(f"h_st{t % 2}"), 16)
                if l == 0:
                    for n in range(4):
                        bias(n)
                pool.wait_ge(S("slot_zero"), 16)
                pool.wait_ge(S("tables"), l + 1)
                for k in range(2):
                    for t in range(TILES):
                        R = rows(t)
                        pool.indirect_dma_start(out=slot_d, out_offset=bass.IndirectOffsetOnAxis(ap=dest_i[0:R, k, t:t + 1], axis=0),
                                                in_=tok[0:R, t:t + 1], in_offset=None).then_inc(S(f"scattered{l}"), 16)
                pool.wait_ge(S(f"scattered{l}"), 16 * 2 * TILES)
                pool.dma_start(slot_i[:, :], slot_d.rearrange("(p i) o -> p (i o)", i=ITEMS)).then_inc(S("slots_in"), 16)
                for par in range(2):
                    pool.wait_ge(S(f"h_st{par}"), 16 * (l + 1) * tiles_of[par])
                pool.wait_ge(S("slots_in"), 16 * (l + 1))
                first, last = pairs(pool, l)

                def gather(j, k):
                    pool.wait_ge(S(f"hg_ps{j}"), (first + k) * 2 + 2)
                    nc.gpsimd.tensor_tensor(slot_c[:, j:j + 1], slot_i[:, bass.ds(k * 2 + j, 1)], zero_i[:, 0:1], ALU.add)
                    pool.drain()
                    pool.indirect_dma_start(out=HG[j], out_offset=None, in_=h_d,
                                            in_offset=bass.IndirectOffsetOnAxis(ap=slot_c[:, j:j + 1], axis=0))\
                        .then_inc(S(f"rows_in{j}"), 16)

                def store(j, k):
                    pool.wait_ge(S(f"y_ev_d{j}"), (first + k) + 2)
                    pool.wait_ge(S(f"y_ev_a{j}"), (first + k) + 2)
                    pool.dma_start(y_items[:, bass.ds(k * 2 + j, 1), :].rearrange("p o d -> p (o d)"), Y[j][:, :])\
                        .then_inc(S(f"y_st{j}"), 16)

                gather(0, 0)
                gather(1, 0)
                if l == 0:
                    mod1()
                with pool.Fori(0, last) as k:
                    gather(0, k + 1)
                    gather(1, k + 1)
                    store(0, k)
                    store(1, k)
                store(0, last)
                store(1, last)
                for j in range(2):
                    pool.wait_ge(S(f"y_st{j}"), ((first + last) + 2) * 16)
                nc.gpsimd.tensor_tensor(dest_c[:, :, :], dest_i[:, :, :],
                                        zero_i[:, 0:2 * TILES].rearrange("p (k t) -> p k t", k=2), ALU.add)
                pool.drain()
                for t in range(TILES):
                    R = rows(t)
                    if t >= 2:
                        pool.wait_ge(S(f"cmb{l}"), t - 1)
                    for k in range(2):
                        pool.indirect_dma_start(out=YG[t % 2][k][0:R, :], out_offset=None, in_=y_d,
                                                in_offset=bass.IndirectOffsetOnAxis(ap=dest_c[0:R, k, t:t + 1], axis=0))\
                            .then_inc(S(f"yg_in{t % 2}"), 16)

            experts(0)
            pool.wait_ge(S("hn"), 3 * TILES)
            nc.gpsimd.memset(QM[:, :, :, :], 0.0).then_inc(S("mask_zero"), 1)
            nc.gpsimd.memset(WM[:, :, :, :], 0.0).then_inc(S("mask_zero"), 1)
            for t in range(TILES):
                R = rows(t)
                pool.wait_ge(S("d_rot"), 2 * TILES + t + 1)
                for src, name in ((KV[0:R, t, 0:KVH * HD], "k"), (KV[0:R, t, KVH * HD:], "v")):
                    dst = O[name + "_prompt"][0, 0, cols(t)] if t < NT else O[name + "_sample"][0, :, 0]
                    pool.dma_start(dst.rearrange("t h d -> t (h d)"), src).then_inc(S("kv_st"), 16)
            for t in range(TILES):
                R = rows(t)
                pool.wait_ge(S("d_rot"), 5 * TILES + t + 1)
                dst = O["kidx_prompt"][0, 0, cols(t)] if t < NT else O["kidx_sample"][0, :, 0]
                pool.dma_start(dst, KIW[0:R, t, 0:ID]).then_inc(S("kv_st"), 16)
            experts(1)

        @block.vector
        def _(dve):
            TS, TT, STT = dve.tensor_scalar, dve.tensor_tensor, dve.scalar_tensor_tensor

            def modulate(m, t):
                if t == 0:
                    dve.wait_ge(S("bc_in"), 64 * m + 64)
                R = rows(t)
                sc_, sh = (SC[:, 0, :], SC[:, 1, :]) if t == NT else SCALE_SHIFT if m else (BC[:, 0, :], BC[:, 1, :])
                if t >= 2:
                    dve.wait_ge(S("ht_ps"), 2 * TILES * m + 2 * (t - 1))
                    if m % 2:
                        dve.wait_ge(S(f"h_st{t % 2}"), 16 * ((m // 2) * tiles_of[t % 2] + t // 2))
                TT(HN[t % 2][0:R, :], X[0:R, t, :], sc_[0:R, :], ALU.mult)
                dve.drain()
                TT(HN[t % 2][0:R, :], HN[t % 2][0:R, :], sh[0:R, :], ALU.add).then_inc(S("hn"), 1)

            def variance(m, t):
                R = rows(t)
                dve.drain()
                for g in range(2):
                    dve.bn_stats(lnst[0:R, t, g, :], X[0:R, t, g * NB:(g + 1) * NB])
                dve.drain()
                dve.bn_aggr(lnmv[0:R, t, :], lnst[0:R, t, :, :]).then_inc(S("ln_var"), 1)

            def norm(m, t):
                R = rows(t)
                dve.wait_ge(S("ln_sd"), TILES * m + t + 1)
                dve.reciprocal(lnrs[:, t:t + 1], lnsd[:, t:t + 1])
                dve.drain()
                STT(X[0:R, t, :], X[0:R, t, :], lnmv[0:R, t, 0:1], BC[0:R, 1, :], ALU.subtract, ALU.mult)
                dve.drain()
                STT(X[0:R, t, :], X[0:R, t, :], lnrs[0:R, t:t + 1], BC[0:R, 2, :], ALU.mult, ALU.add).then_inc(S("x_rdy"), 1)
                dve.drain()

            def mixer_close(m):
                T = EPT[m]
                dve.wait_ge(S("ep_in"), 64 * m + 64)
                for n in range(2):
                    for t in range(TILES):
                        R = rows(t)
                        gt = (BC[:, 0, :] if t < NT else SGATE)[0:R, n * NB:(n + 1) * NB]
                        dve.wait_ge(S(f"out_mm{m}"), TILES * n + t + 1)
                        TT(T[0:R, :], bank[(TILES * n + t) % 8][0:R, :], gt, ALU.mult).then_inc(S(f"out_ev{m}"), 1)
                        dve.drain()
                        xx = X[0:R, t, n * NB:(n + 1) * NB]
                        STT(xx, xx, ALPHA, T[0:R, :], ALU.mult, ALU.add)
                        dve.drain()
                        if n:
                            variance(m, t)
                            if t:
                                norm(m, t - 1)
                                if t <= 2:
                                    modulate(m + 1, t - 1)
                modulate(m + 1, 2)
                norm(m, NT)
                for t in range(3, TILES):
                    modulate(m + 1, t)

            for j in range(2):
                for name in ("a_rdy", "y_ev_d", "at_lo"):
                    dve.engine_nop().then_inc(S(f"{name}{j}"), 1)
            dve.engine_nop().then_inc(S("lo_rdy"), UNIT0)
            dve.memset(gnmv[:, :, :, :], 1.0)
            dve.memset(lnmv[:, :, :], 1.0)
            dve.memset(gates[:, :, :], 0.0)
            dve.memset(qmask[:, :, :, :], 0.0)
            dve.wait_ge(S("cst_in"), 16)
            dve.tensor_copy(bf_cum[:, 0, :], C("cum"))
            dve.tensor_copy(bf_cum[:, 1, :], C("ones"))
            dve.drain()
            dve.wait_ge(S("c_ps"), 1)
            dve.tensor_copy(CT[:, :, :], bank[2][:, 0:KD * (DEC + 1)].rearrange("p (k r) -> p k r", k=KD)).then_inc(S("c_t"), 1)
            dve.wait_ge(S("bmod_in"), 16)
            for n in range(12):
                dve.wait_ge(S("mod_mm"), n + 1)
                one = 1.0 if n in (2, 3, 8, 9) else 0.0
                STT(MODV[:, n * NB:(n + 1) * NB], bank[n % 2][0:DEC + 1, :], one, BMOD[:, n * NB:(n + 1) * NB],
                    ALU.add, ALU.add).then_inc(S("mod_ev"), 1)
                if n == MOD_AHEAD:
                    dve.wait_ge(S("x_in"), 32)
                    dve.wait_ge(S("const_in"), 16 * N_CONST)
                    for t in range(2):
                        modulate(0, t)

            for t in range(2, TILES):
                modulate(0, t)
            si = 0
            for hp in range(2):
                for i in range(2 * TILES):
                    g = hp * 2 * TILES + i
                    isk, t = divmod(i, TILES)
                    R = rows(t)
                    dve.wait_ge(S("ret_ev"), hp * 6 * TILES + i + 1)
                    if g:
                        dve.wait_ge(S("qk_ps"), g)
                    dst = KN[:, t, :] if isk and t < NT else RO
                    x4 = RT[0:R, :].rearrange("p (a d) -> p a d", d=P)
                    x2 = RT[0:R, :].rearrange("p (h a d) -> p h a d", a=2, d=P)
                    d2 = dst[0:R, :].rearrange("p (h a d) -> p h a d", a=2, d=P)
                    t2 = T1[0:R, :].rearrange("p (h a d) -> p h a d", a=2, d=P)
                    cc = rotc[0:R, 0:1, t, :]
                    ss = rotc[0:R, 1:2, t, :].to_broadcast([R, 2, P])
                    TT(T1[0:R, :].rearrange("p (a d) -> p a d", d=P), x4, cc.to_broadcast([R, 4, P]), ALU.mult)
                    TT(d2[:, :, 0, :], x2[:, :, 1, :], ss, ALU.mult)
                    TT(d2[:, :, 1, :], x2[:, :, 0, :], ss, ALU.mult)
                    dve.drain()
                    TT(d2[:, :, 0, :], t2[:, :, 0, :], d2[:, :, 0, :], ALU.subtract)
                    TT(d2[:, :, 1, :], t2[:, :, 1, :], d2[:, :, 1, :], ALU.add).then_inc(S("ro_rdy"), 1)
                    dve.drain()

                def decay_att(i):
                    rc = hp * 2 * NT + i
                    h = 2 * hp + i // NT
                    dve.wait_ge(S("att_ps"), rc + 1)
                    if rc >= 2:
                        dve.wait_ge(S("o_ps"), rc - 1)
                    STT(att[:, rc % 2, :], bank[3 + rc % 2][:, 0:P], float(GAMMA[h] ** -CH), C("tri"), ALU.mult, ALU.mult)\
                        .then_inc(S("att_rdy"), 1)

                decay_att(0)
                for i in range(2 * NT):
                    hh, c = divmod(i, NT)
                    rc = hp * 2 * NT + i
                    if i + 1 < 2 * NT:
                        decay_att(i + 1)
                    dve.wait_ge(S("u_ps"), rc + 1)
                    if c == 0 and hp:
                        dve.wait_ge(S("rp_st"), 32)
                    for j in range(2):
                        st = STATE[:, hh, j, :]
                        if c == 0:
                            last = dve.tensor_copy(st, bank[6 + j][:, :])
                        else:
                            last = STT(st, st, float(GAMMA[2 * hp + hh] ** CH), bank[6 + j][:, :], ALU.mult, ALU.add)
                    last.then_inc(S("s_rdy"), 1)
                    dve.drain()
                for b in range(DEC):
                    dve.tensor_copy(qmask[:, b, :, b], QT[:, :, SEQ + b])
                dve.drain()
                dve.engine_nop().then_inc(S("qm_rdy"), 1)
                for i in range(2 * DEC):
                    si = 2 * DEC * hp + i
                    b, hh = divmod(i, 2)
                    dve.wait_ge(S("vb_ps"), si + 1)
                    dve.wait_ge(S("st_dec"), si + 1)
                    st = slot(("state", hp, b // 2))
                    for j in range(2):
                        sj = st[:, 4 * (b % 2) + 2 * hh + j, :]
                        last = STT(sj, bank[2 + si % 2][:, :], KT[:, 2 * hh + j, SEQ + b:SEQ + b + 1], sj, ALU.mult, ALU.add)
                    last.then_inc(S("st_upd"), 1)
                dve.wait_ge(S("o_ev"), 2 * NT * (hp + 1))
                dve.wait_ge(S("os_ev"), 2 * (hp + 1))
                for hh in range(2):
                    for t in range(TILES):
                        R = rows(t)
                        dve.bn_stats(gnst[0:R, t, :], V[0:R, t, hh * NB:(hh + 1) * NB])
                    dve.drain()
                    for t in range(TILES):
                        last = dve.bn_aggr(gnmv[0:rows(t), hh, t, :], gnst[0:rows(t), t, :])
                    dve.drain()
                dve.engine_nop().then_inc(S("gn_var"), 1)
                dve.wait_ge(S("gn_sd"), hp + 1)
                dve.reciprocal(gnrs[:, :, :], gnsd[:, :, :])
                dve.drain()
                dve.wait_ge(S("gn_in"), 16 * (hp + 1))
                for i in range(2 * TILES):
                    hh, t = divmod(i, TILES)
                    R = rows(t)
                    vv = V[0:R, t, hh * NB:(hh + 1) * NB]
                    TS(vv, vv, gnmv[0:R, hh, t, 0:1], gnrs[0:R, hh, t:t + 1], ALU.subtract, ALU.mult)
                    dve.drain()
                    TT(vv, vv, GNB[0:R, hh * NB:(hh + 1) * NB], ALU.mult)
                    dve.drain()
                    dve.wait_ge(S("ret_ev"), hp * 6 * TILES + 4 * TILES + i + 1)
                    TT(vv, vv, SG[i % 2][0:R, :], ALU.mult).then_inc(S("y_rdy"), 1)
            mixer_close(0)

            def route(l):
                D_ = dve.drain
                flat = lambda v: v.rearrange("p t e -> p (t e)")
                dve.memset(LG, 0.0)
                D_()
                dve.wait_ge(S(f"lg_mm{l}"), TILES)
                pl = bank[0][:, 0:TILES * NE].rearrange("p (t e) -> p t e", e=NE)
                b4 = br[:, :].rearrange("p (o e) -> p o e", o=1)
                TT(LG[:, 0:NT, :], pl[:, 0:NT, :], b4.to_broadcast([P, NT, NE]), ALU.add)
                TT(LG[0:DEC, NT, :], pl[0:DEC, NT, :], br[0:DEC, :], ALU.add)
                D_()
                sp3 = lambda v: v.rearrange("p (t o) -> p t o", o=1).to_broadcast([P, TILES, NE])
                dve.tensor_reduce(r1, LG, AX.X, ALU.max)
                D_()
                TT(LG, LG, sp3(r1), ALU.subtract).then_inc(S("lg_sub"), 1)
                dve.wait_ge(S("lg_exp"), l + 1)
                dve.tensor_reduce(r1, PR, AX.X, ALU.add)
                D_()
                dve.reciprocal(r2, r1)
                D_()
                TT(PR, PR, sp3(r2), ALU.mult)
                D_()
                g4 = PR.rearrange("p t (g e) -> p (t g) e", e=EPG)
                for at, d_ in ((0, 1), (3, 2), (5, 3)):
                    TT(PAIRS[:, :, at:at + EPG - d_], g4[:, :, 0:EPG - d_], g4[:, :, d_:EPG], ALU.add)
                D_()
                dve.tensor_reduce(GS.rearrange("p t g -> p (t g)"), PAIRS, AX.X, ALU.max)
                D_()
                dve.tensor_reduce(r1, GS, AX.X, ALU.max)
                D_()
                sg = lambda v: v.rearrange("p (t o) -> p t o", o=1).to_broadcast([P, TILES, NG])
                TT(GQ, GS, sg(r1), ALU.is_equal)
                D_()
                TT(GK, GQ, C("w4").rearrange("p (o g) -> p o g", o=1).to_broadcast([P, TILES, NG]), ALU.mult)
                D_()
                dve.tensor_reduce(r1, GK, AX.X, ALU.max)
                D_()
                TT(GQ, GK, sg(r1), ALU.is_equal)
                D_()
                gq = GQ.rearrange("p t (g o) -> p (t g) o", o=1).to_broadcast([P, TILES * NG, EPG])
                pm = PM.rearrange("p t (g e) -> p (t g) e", e=EPG)
                TT(pm, g4, gq, ALU.mult)
                D_()
                TT(pm, pm, gq, ALU.add)
                D_()
                TS(PM, PM, -1.0, None, ALU.add)
                D_()
                w16 = C("w16").rearrange("p (o e) -> p o e", o=1).to_broadcast([P, TILES, NE])
                for k, (Sk, rk) in enumerate(((S1, r3), (S2, r4))):
                    dve.tensor_reduce(rk, PM, AX.X, ALU.max)
                    D_()
                    TT(EQ, PM, sp3(rk), ALU.is_equal)
                    D_()
                    TT(KEY, EQ, w16, ALU.mult)
                    D_()
                    dve.tensor_reduce(r1, KEY, AX.X, ALU.max)
                    D_()
                    TT(Sk, KEY, sp3(r1), ALU.is_equal)
                    D_()
                    if k == 0:
                        STT(PM.rearrange("p t e -> p (t e)"), Sk.rearrange("p t e -> p (t e)"), -4.0,
                            PM.rearrange("p t e -> p (t e)"), ALU.mult, ALU.add)
                        D_()
                for Sk, rk in ((S1, r3), (S2, r4)):
                    TT(EQ, PR, Sk, ALU.mult)
                    D_()
                    dve.tensor_reduce(rk, EQ, AX.X, ALU.add)
                    D_()
                TT(r1, r3, r4, ALU.add)
                D_()
                dve.reciprocal(r2, r1)
                D_()
                TT(gates[:, 0, :], r3, r2, ALU.mult)
                TT(gates[:, 1, :], r4, r2, ALU.mult)
                va = C("valid").rearrange("p (t o) -> p t o", o=1).to_broadcast([P, TILES, NE])
                TT(EQ, S1, S2, ALU.add)
                D_()
                TT(mb[:, :, :], EQ, va, ALU.mult).then_inc(S("marks"), 1)
                dve.wait_ge(S("rank_mm"), l + 1)
                rk = bank[1][:, 0:(TILES + 1) * NE].rearrange("p (t e) -> p t e", e=NE)
                dve.tensor_copy(cntv, rk[:, TILES, :])
                D_()
                blk = C("blk").rearrange("p (o j) -> p o j", o=1).to_broadcast([P, NE, MAXB])
                bg = big.rearrange("p i e -> p (i e)")[:, 0:NE * MAXB].rearrange("p (e j) -> p e j", j=MAXB)
                TT(bg, cntv.rearrange("p (e o) -> p e o", o=1).to_broadcast([P, NE, MAXB]), blk, ALU.is_gt)
                D_()
                dve.tensor_reduce(nbk, bg, AX.X, ALU.add)
                D_()
                TS(nbk, nbk, -1.0, 0.0, ALU.add, ALU.max)
                D_()
                dve.tensor_tensor_scan(cum, C("ones")[:, 0:NE], nbk, 0.0, ALU.mult, ALU.add)
                D_()
                TT(sta, cum, nbk, ALU.subtract)
                D_()
                STT(sta, sta, float(NE - 1), C("e"), ALU.add, ALU.subtract)
                rr = rk[:, 0:TILES, :]
                TS(KEY, rr, float(P), None, ALU.is_ge)
                D_()
                TT(EQ, KEY, sta.rearrange("p (o e) -> p o e", o=1).to_broadcast([P, TILES, NE]), ALU.mult)
                for b_ in range(2, MAXB):
                    STT(flat(KEY), bank[1][:, 0:TILES * NE], float(b_ * P), flat(KEY), ALU.is_ge, ALU.add)
                    D_()
                STT(flat(DST), bank[1][:, 0:TILES * NE], float(ITEMS), flat(EQ), ALU.mult, ALU.add)
                D_()
                STT(flat(DST), flat(KEY), float(1 - P * ITEMS), flat(DST), ALU.mult, ALU.add)
                D_()
                TT(DST, DST, C("e").rearrange("p (o e) -> p o e", o=1).to_broadcast([P, TILES, NE]), ALU.add)
                D_()
                for k, Sk in enumerate((S1, S2)):
                    TT(EQ, DST, Sk, ALU.mult)
                    D_()
                    dve.tensor_reduce(r1, EQ, AX.X, ALU.add)
                    D_()
                    dve.tensor_copy(dest_i[:, k, :], r1)
                    D_()
                W_ = ITEMS - NE + 2
                TT(big, C("item").rearrange("p (i o) -> p i o", o=1).to_broadcast([P, W_, NE]),
                   cum.rearrange("p (o e) -> p o e", o=1).to_broadcast([P, W_, NE]), ALU.is_ge)
                D_()
                dve.tensor_reduce(itf, big, AX.X, ALU.add)
                D_()
                TS(itf, itf, float(NE - 1), None, ALU.min)
                dve.tensor_copy(eid_i[:, 0:NE], C("e"))
                D_()
                dve.tensor_copy(eid_i[:, NE:], itf)
                PW = (ITEMS - NE) // 2
                b2 = big.rearrange("p i e -> p (i e)")[:, 0:PW]
                TT(b2, C("pair")[:, 0:PW], cum[:, NE - 1:NE].to_broadcast([P, PW]), ALU.is_lt)
                D_()
                dve.tensor_reduce(r1[:, 0:1], b2, AX.X, ALU.add)
                D_()
                TS(r1[:, 0:1], r1[:, 0:1], float(NE // 2 - 1), None, ALU.add)
                D_()
                dve.tensor_copy(np_i[:, l:l + 1], r1[:, 0:1])
                D_()
                dve.engine_nop().then_inc(S("tables"), 1)

            def experts(l):
                m = 2 * l + 1
                route(l)

                def low(i, u):
                    dve.wait_ge(S("hi_rdy"), i * len(UNITS) + (u + 1))
                    TT(WL[:, u % SPLIT, :, :], raw(u % RAW), WH[:, u % SPLIT, :, :].bitcast(F32), ALU.subtract)\
                        .then_inc(S("lo_rdy"), 1)

                first = pairs_before(dve, l)
                for u in range(SPLIT):
                    low(first, u)
                first, last = pairs(dve, l)

                def take_rows(j, i):
                    for g in range(2):
                        dve.wait_ge(S(f"hg_hi{j}"), 2 * i + (g + 1))
                        TT(HGL[:, j, 4 * g:4 * g + 4, :], bank[2 * j + g][:, :].rearrange("p (q r) -> p q r", r=P),
                           HGH[:, j, 4 * g:4 * g + 4, :].bitcast(F32), ALU.subtract).then_inc(S(f"hg_lo{j}"), 1)

                def pair(i, end):
                    def used(u):
                        dve.wait_ge(S("unit_used"), i * len(UNITS) + (UNIT0 + u + 1))

                    def act_times_up(j, u):
                        dve.wait_ge(S(f"sg{j}"), i + 1)
                        used(u)
                        TT(AE, SGE, bank[5 + 2 * j][:, :], ALU.mult).then_inc(S(f"a_rdy{j}"), 1)

                    def take_a(j):
                        dve.wait_ge(S(f"at_hi{j}"), i + 1)
                        TT(ATL[:, j, :, :], bank[2 * j][:, :].rearrange("p (q r) -> p q r", r=P),
                           ATH[:, j, :, :].bitcast(F32), ALU.subtract).then_inc(S(f"at_lo{j}"), 1)

                    def take_y(j, u):
                        used(u)
                        dve.wait_ge(S(f"y_st{j}"), (i + 1) * 16)
                        dve.tensor_copy(Y[j][:, 0:NB], bank[4 + 2 * j][:, :]).then_inc(S(f"y_ev_d{j}"), 1)

                    for u in range(SPLIT, SPLIT + len(UNITS)):
                        if u == 7:
                            act_times_up(0, 3)
                        if u == 11:
                            act_times_up(1, 7)
                        if not end or u < len(UNITS):
                            low(i, u)
                        if u == 5:
                            take_rows(1, i)
                        if u == 9:
                            take_a(0)
                        if u == 12:
                            take_a(1)
                        if u == 13:
                            if not end:
                                take_rows(0, i + 1)
                            take_y(0, 9)
                        if u == 15:
                            take_y(1, 11)

                take_rows(0, first)
                with dve.Fori(0, last) as k:
                    pair(first + k, False)
                pair(first + last, True)
                dve.wait_ge(S("ep_in"), 64 * m + 64)
                for t in range(TILES):
                    R = rows(t)
                    y1, y2 = (YG[t % 2][k][0:R, :] for k in range(2))
                    gt = BC[0:R, 0, :] if t < NT else SGATE
                    dve.wait_ge(S("y_gated"), l * TILES + t + 1)
                    STT(y1, y2, gates[0:R, 1, t:t + 1], y1, ALU.mult, ALU.add)
                    dve.drain()
                    TT(y1, y1, gt, ALU.mult)
                    dve.drain()
                    STT(X[0:R, t, :], X[0:R, t, :], ALPHA, y1, ALU.mult, ALU.add).then_inc(S(f"cmb{l}"), 1)
                    variance(m, t)
                    if t:
                        norm(m, t - 1)
                        if l == 0:
                            modulate(m + 1, t - 1)
                norm(m, NT)
                if l == 0:
                    modulate(m + 1, NT)

            experts(0)

            for i in range(6 * TILES):
                n, t = divmod(i, TILES)
                R = rows(t)
                dve.wait_ge(S("d_ev"), i + 1)
                nh, w, rot, src, cn, sn = ((4, HD, ROT, DRT[i % 2], "dcos", "dsin"), (4, HD, ROT, DRT[i % 2], "dcos", "dsin"),
                                           (KVH, HD, ROT, KV[:, t, :], "dcos", "dsin"),
                                           (8, ID, IROT, DRT[i % 2], "icos", "isin"), (8, ID, IROT, DRT[i % 2], "icos", "isin"),
                                           (1, ID, IROT, KIW[:, t, :], "icos", "isin"))[n]
                hf = rot // 2
                xv = src[0:R, 0:nh * w].rearrange("p (h d) -> p h d", d=w)
                x1, x2 = xv[:, :, 0:hf], xv[:, :, hf:rot]
                tb = lambda nm: C(nm)[0:R, t * hf:(t + 1) * hf].rearrange("p (o d) -> p o d", o=1).to_broadcast([R, nh, hf])
                rx = [RX[0:R, k, 0:nh * hf].rearrange("p (h d) -> p h d", d=hf) for k in range(4)]
                TT(rx[0], x1, tb(cn), ALU.mult)
                TT(rx[1], x2, tb(sn), ALU.mult)
                TT(rx[2], x1, tb(sn), ALU.mult)
                TT(rx[3], x2, tb(cn), ALU.mult)
                dve.drain()
                TT(x1, rx[0], rx[1], ALU.subtract)
                last = TT(x2, rx[2], rx[3], ALU.add)
                if n == 5:
                    dve.drain()
                    for c in range(2):
                        dve.tensor_copy(KID[0:R, t, c * ID:(c + 1) * ID], KIW[0:R, t, 0:ID])
                    last = TS(WI[0:R, t, :], KIW[0:R, t, ID:ID + IH], IH ** -0.5, None, ALU.mult)
                last.then_inc(S("d_rot"), 1)
                dve.drain()
            ix = 0
            assert TOPK_P % 32 == 0 and QH == 8
            for t in range(NT):
                L = (t + 1) * P
                if t == 0:
                    dve.tensor_copy(BIAS[0][:, 0:P], C("cbias"))
                    dve.drain()

                def index(part):
                    nonlocal ix
                    N = L + P
                    for h in range(part * IH // 4, (part + 1) * IH // 4):
                        dve.wait_ge(S("ix_rl"), ix + 1)
                        w_ = WI[:, t + 1, h:h + 1]
                        if h == 0:
                            TS(SCORE[:, 0:N], RL[ix % 4][:, 0:N], w_, None, ALU.mult).then_inc(S("ix_acc"), 1)
                        else:
                            STT(SCORE[:, 0:N], RL[ix % 4][:, 0:N], w_, SCORE[:, 0:N], ALU.mult, ALU.add)\
                                .then_inc(S("ix_acc"), 1)
                        dve.drain()
                        ix += 1
                    if part == 3:
                        TT(SCORE[:, L:N], SCORE[:, L:N], C("cbias"), ALU.add)
                        dve.drain()

                def choose(part):
                    N = L + P
                    for r in range(TOPK_P // 8 // 4):
                        dve.max(m8[:, :], SCORE[:, 0:N])
                        dve.drain()
                        dve.match_replace(out=SCORE[:, 0:N], in_to_replace=m8[:, :], in_values=SCORE[:, 0:N], imm_value=GONE)
                        dve.drain()
                    if part == 3:
                        TS(BIAS[(t + 1) % 2][:, 0:N], SCORE[:, 0:N], -2.0e38, NEG, ALU.is_gt, ALU.mult)
                        dve.drain()

                def sum_of(h):
                    a = t * QH + h
                    dve.wait_ge(S("e_rdy"), a + 1)
                    dve.reciprocal(ersum[:, a % 2:a % 2 + 1], esum[:, a % 2:a % 2 + 1]).then_inc(S("es_rdy"), 1)

                for s in range(QH + 1):
                    if s < QH:
                        a = t * QH + s
                        dve.wait_ge(S("lg_ps"), a + 1)
                        if a >= 4:
                            dve.wait_ge(S("pt_ps"), a - 3)
                        dve.tensor_tensor_reduce(out=E[a % 4][:, 0:L], in0=bank[2 + a % 2][:, 0:L], in1=BIAS[t % 2][:, 0:L],
                                                 scale=1.0, scalar=GONE, op0=ALU.add, op1=ALU.max,
                                                 accum_out=mx[:, a % 2:a % 2 + 1]).then_inc(S("lg_ev"), 1)
                        dve.drain()
                        TS(nbias[:, a % 2:a % 2 + 1], mx[:, a % 2:a % 2 + 1], -(HD ** -0.5), None, ALU.mult)\
                            .then_inc(S("nb_rdy"), 1)
                    if s:
                        sum_of(s - 1)
                    if s < 8 and t + 1 < NT:
                        (index if s < 4 else choose)(s % 4)
            dve.wait_ge(S("ot_ev"), NT * QH)
            dve.wait_ge(S("w_t"), 1)
            dve.wait_ge(S("mask_zero"), 2)
            for b in range(DEC):
                dve.tensor_copy(WM[:, :, b, b], bank[0][0:DEC, 0:2 * DEC].rearrange("p (c b) -> p c b", c=2)[:, :, b])
                for n in range(KVH):
                    dve.tensor_copy(QM[:, b, n, b * GRP:(b + 1) * GRP], DQT[:, n * GRP:(n + 1) * GRP, SEQ + b])
            dve.drain()
            dve.engine_nop().then_inc(S("wm_rdy"), 1)
            for b in range(DEC):
                if b >= 2:
                    dve.wait_ge(S("s_dot"), b - 1)
                dve.tensor_copy(KIBT[b % 2][:, PAST:LS], KIT[:, SEQ + b:SEQ + b + 1]).then_inc(S("ki_rdy"), 1)
                last = dve.tensor_copy(KBT[:, b, :, PAST], DKT[:, :, SEQ + b])
            last.then_inc(S("kn_rdy"), 1)
            dve.wait_ge(S("s_sc"), DEC)
            dve.tensor_copy(SCS, bank[6][0:DEC, 0:LS])
            dve.drain()
            for r in range(TOPK_S // 8):
                dve.max(m8[0:DEC, :], SCS)
                dve.drain()
                dve.match_replace(out=SCS, in_to_replace=m8[0:DEC, :], in_values=SCS, imm_value=GONE)
                dve.drain()
            TS(BIS, SCS, -2.0e38, NEG, ALU.is_gt, ALU.mult).then_inc(S("s_bias"), 1)
            r = DEC * GRP
            for n in range(KVH):
                dve.wait_ge(S("s_lg"), n + 1)
                dve.tensor_copy(PS[n][:, :], bank[n][0:r, 0:LS])
                dve.drain()
                dve.tensor_reduce(mx[0:r, n:n + 1], PS[n][:, :], AX.X, ALU.max)
                dve.drain()
                TS(nbias[0:r, n:n + 1], mx[0:r, n:n + 1], -(HD ** -0.5), None, ALU.mult).then_inc(S("s_nb"), 1)
            for n in range(KVH):
                dve.wait_ge(S("s_e"), n + 1)
                dve.reciprocal(ersum[0:r, n:n + 1], esum[0:r, n:n + 1])
                dve.drain()
                TS(PS[n][:, :], PS[n][:, :], ersum[0:r, n:n + 1], None, ALU.mult)
                dve.drain()
                TS(DG[:, n, :], ident[0:r, 0:r], PS[n][:, PAST:LS], None, ALU.mult).then_inc(S("s_p"), 1)
            mixer_close(2)
            experts(1)


_OUTS = [("y_prompt", (1, SEQ, D)), ("y_sample", (DEC, 1, D)), ("ret_prompt", (1, 1, RH, RDK, RDV)),
         ("ret_sample", (1, DEC, RH, RDK, RDV)), ("k_prompt", (1, 1, SEQ, KVH, HD)), ("v_prompt", (1, 1, SEQ, KVH, HD)),
         ("kidx_prompt", (1, 1, SEQ, ID)), ("k_sample", (1, DEC, 1, KVH, HD)), ("v_sample", (1, DEC, 1, KVH, HD)),
         ("kidx_sample", (1, DEC, 1, ID))]


def kernel(**inputs):
    import concourse.bacc as _bacc
    from concourse.bass_utils import run_bass_kernel_spmd as _run

    nc = _bacc.Bacc("TRN2", target_bir_lowering=False, num_devices=1)
    cst, rotc, tok = constants()
    arrays, args = {}, {}
    for name, a in list(inputs.items()) + [("cst", cst), ("rotc", rotc), ("tok", tok)]:
        a = np.ascontiguousarray(a)
        arrays["in_" + name] = a
        args[name] = nc.dram_tensor("in_" + name, a.shape, mybir.dt.from_np(a.dtype), kind="ExternalInput").ap()
    outs = {name: nc.dram_tensor("out_" + name, shape, F32, kind="ExternalOutput").ap() for name, shape in _OUTS}
    trunk(nc, args, outs)
    r = _run(nc, [arrays], core_ids=[0])
    return tuple(r.results[0]["out_" + name] for name, _ in _OUTS)
```
